# Optimizing a Trainium2 kernel written in Bass

```python
import math
import jax
import jax.numpy as jnp
from jax import lax
import numpy as np
import jax, jax.numpy as jnp

D_MODEL = 1024
BATCH = 1
SEQ = 256
DEPTH = 1

CHUNK = 64
CONV_K = 4
GDN_HEADS = D_MODEL // 128
GDN_DK = 128
GDN_DV = 128
GDN_QK = GDN_HEADS * GDN_DK
GDN_V = GDN_HEADS * GDN_DV
GDN_CONV_CH = 2 * GDN_QK + GDN_V
SSD_P = 64
SSD_HEADS = D_MODEL // SSD_P
SSD_G = 2
SSD_N = 128
SSD_INNER = SSD_HEADS * SSD_P
SSD_BC = SSD_G * SSD_N
SSD_CONV_CH = SSD_INNER + 2 * SSD_BC
MIX_WIDTH = GDN_V + SSD_INNER
IN_WIDTH = GDN_CONV_CH + GDN_V + 2 * GDN_HEADS + SSD_INNER + SSD_CONV_CH + SSD_HEADS
N_EXPERTS = 32
TOP_K = 4
D_FF = D_MODEL
SWIGLU_ALPHA = 1.702
SWIGLU_LIMIT = 7.0
EXPERT_BLOCK = 128
EPS = 1e-6


def rmsnorm(x, g):
    xf = x.astype(jnp.float32)
    y = xf * lax.rsqrt(jnp.mean(xf * xf, axis=-1, keepdims=True) + EPS)
    return (y * g.astype(jnp.float32)).astype(x.dtype)

def l2norm(x):
    return x * lax.rsqrt(jnp.sum(x * x, axis=-1, keepdims=True) + EPS)

def causal_dwconv(x, w):
    k, ch = w.shape
    return lax.conv_general_dilated(x, w[:, None, :], window_strides=(1,), padding=[(k - 1, 0)],
                                    dimension_numbers=("NWC", "WIO", "NWC"), feature_group_count=ch)

def gated_delta_rule_chunked(q, k, v, beta, g):
    bsz, s, h, dk = q.shape
    dv = v.shape[-1]
    nc = s // CHUNK

    def blocks(t):
        return jnp.moveaxis(t.reshape((bsz, nc, CHUNK, h) + t.shape[3:]), 3, 1)

    qc, kc, vc, bc, gc = blocks(q), blocks(k), blocks(v), blocks(beta), blocks(g)
    gam = jnp.cumsum(gc, axis=-1)
    incl = jnp.tril(jnp.ones((CHUNK, CHUNK), bool))
    strict = jnp.tril(jnp.ones((CHUNK, CHUNK), bool), -1)
    decay = jnp.exp(jnp.where(incl, gam[..., :, None] - gam[..., None, :], -jnp.inf))
    kk = jnp.einsum("bhnld,bhnsd->bhnls", kc, kc)
    a_mat = jnp.where(strict, bc[..., :, None] * kk * decay, 0.0) + jnp.eye(CHUNK, dtype=q.dtype)
    rhs = jnp.concatenate([vc * bc[..., None], kc * (bc * jnp.exp(gam))[..., None]], axis=-1)
    sol = lax.linalg.triangular_solve(a_mat, rhs, left_side=True, lower=True, unit_diagonal=True)
    u, w = sol[..., :dv], sol[..., dv:]
    qk = jnp.einsum("bhnld,bhnsd->bhnls", qc, kc) * decay
    q_dec = qc * jnp.exp(gam)[..., None]
    k_dec = kc * jnp.exp(gam[..., -1:] - gam)[..., None]
    chunk_dec = jnp.exp(gam[..., -1])

    def step(state, inp):
        u_i, w_i, qk_i, qd_i, kd_i, cd_i = inp
        v_new = u_i - jnp.einsum("bhld,bhdv->bhlv", w_i, state)
        o_i = jnp.einsum("bhld,bhdv->bhlv", qd_i, state) + jnp.einsum("bhls,bhsv->bhlv", qk_i, v_new)
        state = cd_i[..., None, None] * state + jnp.einsum("bhld,bhlv->bhdv", kd_i, v_new)
        return state, o_i

    xs = (jnp.moveaxis(u, 2, 0), jnp.moveaxis(w, 2, 0), jnp.moveaxis(qk, 2, 0),
          jnp.moveaxis(q_dec, 2, 0), jnp.moveaxis(k_dec, 2, 0), jnp.moveaxis(chunk_dec, 2, 0))
    s0 = jnp.zeros((bsz, h, dk, dv), q.dtype)
    _, o = lax.scan(step, s0, xs)
    return jnp.transpose(o, (1, 0, 3, 2, 4)).reshape(bsz, s, h, dv)

def ssd_chunked(x, dt, a_log, bm, cm):
    bsz, s, h, p = x.shape
    g, n = bm.shape[2], bm.shape[3]
    e = h // g
    nc = s // CHUNK
    a = -jnp.exp(a_log) * dt
    xc = (x * dt[..., None]).reshape(bsz, nc, CHUNK, g, e, p)
    ac = a.reshape(bsz, nc, CHUNK, g, e)
    bc = bm.reshape(bsz, nc, CHUNK, g, n)
    cc = cm.reshape(bsz, nc, CHUNK, g, n)
    a_cum = jnp.cumsum(ac, axis=2)
    incl = jnp.tril(jnp.ones((CHUNK, CHUNK), bool))
    seg = a_cum[:, :, :, None] - a_cum[:, :, None, :]
    decay = jnp.exp(jnp.where(incl[:, :, None, None], seg, -jnp.inf))
    cb = jnp.einsum("bclgn,bcsgn->bclsg", cc, bc)
    y_diag = jnp.einsum("bclsge,bcsgep->bclgep", cb[..., None] * decay, xc)
    states = jnp.einsum("bclgn,bclge,bclgep->bcgepn", bc, jnp.exp(a_cum[:, :, -1:] - a_cum), xc)
    chunk_dec = jnp.exp(a_cum[:, :, -1])

    def step(hs, inp):
        st, cd = inp
        return cd[..., None, None] * hs + st, hs

    h0 = jnp.zeros((bsz, g, e, p, n), x.dtype)
    _, h_prev = lax.scan(step, h0, (jnp.moveaxis(states, 1, 0), jnp.moveaxis(chunk_dec, 1, 0)))
    h_prev = jnp.moveaxis(h_prev, 0, 1)
    y_off = jnp.einsum("bclgn,bcgepn,bclge->bclgep", cc, h_prev, jnp.exp(a_cum))
    return (y_diag + y_off).reshape(bsz, s, h, p)

def hybrid_mixer(h, w_in, gdn_conv_w, gdn_a_log, gdn_dt_bias, gdn_norm_g,
                 ssd_conv_w, ssd_conv_b, ssd_a_log, ssd_dt_bias, ssd_d, ssd_norm_g, w_out):
    bsz, s, _ = h.shape
    f32 = jnp.float32
    proj = h @ w_in
    off = 0
    gdn_qkv = proj[..., off:off + GDN_CONV_CH]; off += GDN_CONV_CH
    gdn_z = proj[..., off:off + GDN_V]; off += GDN_V
    gdn_b = proj[..., off:off + GDN_HEADS]; off += GDN_HEADS
    gdn_a = proj[..., off:off + GDN_HEADS]; off += GDN_HEADS
    ssd_z = proj[..., off:off + SSD_INNER]; off += SSD_INNER
    ssd_xbc = proj[..., off:off + SSD_CONV_CH]; off += SSD_CONV_CH
    ssd_dt = proj[..., off:off + SSD_HEADS]

    qkv = jax.nn.silu(causal_dwconv(gdn_qkv, gdn_conv_w)).astype(f32)
    q = l2norm(qkv[..., :GDN_QK].reshape(bsz, s, GDN_HEADS, GDN_DK)) * (GDN_DK ** -0.5)
    k = l2norm(qkv[..., GDN_QK:2 * GDN_QK].reshape(bsz, s, GDN_HEADS, GDN_DK))
    v = qkv[..., 2 * GDN_QK:].reshape(bsz, s, GDN_HEADS, GDN_DV)
    beta = jax.nn.sigmoid(gdn_b.astype(f32))
    g = -jnp.exp(gdn_a_log.astype(f32)) * jax.nn.softplus(gdn_a.astype(f32) + gdn_dt_bias.astype(f32))
    o = gated_delta_rule_chunked(q, k, v, beta, g)
    o = rmsnorm(o, gdn_norm_g) * jax.nn.silu(gdn_z.astype(f32).reshape(bsz, s, GDN_HEADS, GDN_DV))
    gdn_out = o.reshape(bsz, s, GDN_V).astype(h.dtype)

    xbc = jax.nn.silu(causal_dwconv(ssd_xbc, ssd_conv_w) + ssd_conv_b).astype(f32)
    xs = xbc[..., :SSD_INNER].reshape(bsz, s, SSD_HEADS, SSD_P)
    bm = xbc[..., SSD_INNER:SSD_INNER + SSD_BC].reshape(bsz, s, SSD_G, SSD_N)
    cm = xbc[..., SSD_INNER + SSD_BC:].reshape(bsz, s, SSD_G, SSD_N)
    dt = jax.nn.softplus(ssd_dt.astype(f32) + ssd_dt_bias.astype(f32))
    y = ssd_chunked(xs, dt, ssd_a_log.astype(f32), bm, cm) + ssd_d.astype(f32)[:, None] * xs
    y = y.reshape(bsz, s, SSD_INNER) * jax.nn.silu(ssd_z.astype(f32))
    y = rmsnorm(y.reshape(bsz, s, SSD_G, SSD_INNER // SSD_G),
                ssd_norm_g.reshape(SSD_G, SSD_INNER // SSD_G)).reshape(bsz, s, SSD_INNER)
    ssd_out = y.astype(h.dtype)

    return jnp.concatenate([gdn_out, ssd_out], axis=-1) @ w_out

def clamped_swiglu(gu):
    gate, up = gu[..., :D_FF], gu[..., D_FF:]
    gate = jnp.minimum(gate, SWIGLU_LIMIT)
    up = jnp.clip(up, -SWIGLU_LIMIT, SWIGLU_LIMIT)
    return (up + 1.0) * (gate * jax.nn.sigmoid(gate * SWIGLU_ALPHA))

def moe_ffn(h, router_w, router_b, w_gu, b_gu, w_down, b_down):
    bsz, s, d = h.shape
    n_tok = bsz * s
    hf = h.reshape(n_tok, d)
    logits = (hf @ router_w + router_b).astype(jnp.float32)
    top_logit, top_idx = lax.top_k(logits, TOP_K)
    gates = jax.nn.softmax(top_logit, axis=-1)
    n_assign = n_tok * TOP_K
    eid = top_idx.reshape(n_assign)
    tok = jnp.arange(n_assign, dtype=jnp.int32) // TOP_K
    order = jnp.argsort(eid)
    eid_s = eid[order]
    counts = jnp.bincount(eid, length=N_EXPERTS)
    padded = (counts + EXPERT_BLOCK - 1) // EXPERT_BLOCK * EXPERT_BLOCK
    pad_end = jnp.cumsum(padded)
    pad_start = pad_end - padded
    start = jnp.cumsum(counts) - counts
    dest = pad_start[eid_s] + jnp.arange(n_assign, dtype=jnp.int32) - start[eid_s]
    n_rows = (-(-n_assign // EXPERT_BLOCK) + N_EXPERTS) * EXPERT_BLOCK
    n_blocks = n_rows // EXPERT_BLOCK
    row_tok = jnp.full((n_rows,), n_tok, jnp.int32).at[dest].set(tok[order])
    row_gate = jnp.zeros((n_rows,), jnp.float32).at[dest].set(gates.reshape(n_assign)[order])
    blk_start = jnp.arange(n_blocks, dtype=jnp.int32) * EXPERT_BLOCK
    blk_expert = jnp.minimum(jnp.searchsorted(pad_end, blk_start, side="right"), N_EXPERTS - 1)
    h_pad = jnp.concatenate([hf, jnp.zeros((1, d), hf.dtype)], axis=0)
    x_rows = h_pad[row_tok].reshape(n_blocks, EXPERT_BLOCK, d)

    def expert_block(args):
        xb, e = args
        y = clamped_swiglu(xb @ w_gu[e] + b_gu[e])
        return y @ w_down[e] + b_down[e]

    y_rows = lax.map(expert_block, (x_rows, blk_expert)).reshape(n_rows, d)
    y_rows = y_rows * row_gate[:, None].astype(y_rows.dtype)
    out = jax.ops.segment_sum(y_rows, row_tok, num_segments=n_tok + 1)[:n_tok]
    return out.reshape(bsz, s, d)

def first_inputs(seed: int = 0) -> dict:
    key = jax.random.key(seed)
    ks = jax.random.split(key, 26)
    f32 = jnp.float32
    L = DEPTH

    def nrm(k, shape, scale):
        return jax.random.normal(k, shape, f32) * scale

    def a_log_init(k, h):
        return jnp.log(jax.random.uniform(k, (L, h), f32, minval=1.0, maxval=16.0))

    def dt_bias_init(k, h):
        dt = jnp.exp(jax.random.uniform(k, (L, h), f32, minval=math.log(1e-3), maxval=math.log(1e-1)))
        return dt + jnp.log(-jnp.expm1(-dt))

    return {
        "x": nrm(ks[0], (BATCH, SEQ, D_MODEL), 1.0),
        "c": nrm(ks[1], (BATCH, D_MODEL), 1.0),
        "ada_w": nrm(ks[2], (L, D_MODEL, 6 * D_MODEL), 0.5 * D_MODEL ** -0.5),
        "ada_b": nrm(ks[3], (L, 6 * D_MODEL), 0.02),
        "norm1_g": 1.0 + nrm(ks[4], (L, D_MODEL), 0.02),
        "norm2_g": 1.0 + nrm(ks[5], (L, D_MODEL), 0.02),
        "w_in": nrm(ks[6], (L, D_MODEL, IN_WIDTH), D_MODEL ** -0.5),
        "gdn_conv_w": nrm(ks[7], (L, CONV_K, GDN_CONV_CH), CONV_K ** -0.5),
        "gdn_a_log": a_log_init(ks[8], GDN_HEADS),
        "gdn_dt_bias": dt_bias_init(ks[9], GDN_HEADS),
        "gdn_norm_g": 1.0 + nrm(ks[10], (L, GDN_DV), 0.02),
        "ssd_conv_w": nrm(ks[11], (L, CONV_K, SSD_CONV_CH), CONV_K ** -0.5),
        "ssd_conv_b": nrm(ks[12], (L, SSD_CONV_CH), 0.02),
        "ssd_a_log": a_log_init(ks[13], SSD_HEADS),
        "ssd_dt_bias": dt_bias_init(ks[14], SSD_HEADS),
        "ssd_d": 1.0 + nrm(ks[15], (L, SSD_HEADS), 0.02),
        "ssd_norm_g": 1.0 + nrm(ks[16], (L, SSD_INNER), 0.02),
        "w_out": nrm(ks[17], (L, MIX_WIDTH, D_MODEL), MIX_WIDTH ** -0.5),
        "router_w": nrm(ks[18], (L, D_MODEL, N_EXPERTS), D_MODEL ** -0.5),
        "router_b": nrm(ks[19], (L, N_EXPERTS), 0.01),
        "moe_w_gu": nrm(ks[20], (L, N_EXPERTS, D_MODEL, 2 * D_FF), D_MODEL ** -0.5),
        "moe_b_gu": nrm(ks[21], (L, N_EXPERTS, 2 * D_FF), 0.01),
        "moe_w_down": nrm(ks[22], (L, N_EXPERTS, D_FF, D_MODEL), D_FF ** -0.5),
        "moe_b_down": nrm(ks[23], (L, N_EXPERTS, D_MODEL), 0.01),
        "final_g": 1.0 + nrm(ks[24], (D_MODEL,), 0.02),
    }

def first_block(x, c, ada_w, ada_b, norm1_g, norm2_g, w_in, gdn_conv_w, gdn_a_log, gdn_dt_bias,
              gdn_norm_g, ssd_conv_w, ssd_conv_b, ssd_a_log, ssd_dt_bias, ssd_d, ssd_norm_g, w_out,
              router_w, router_b, moe_w_gu, moe_b_gu, moe_w_down, moe_b_down, final_g):
    c_act = jax.nn.silu(c)
    for l in range(DEPTH):
        mod = (c_act @ ada_w[l] + ada_b[l])[:, None, :]
        sh1, sc1, g1, sh2, sc2, g2 = jnp.split(mod, 6, axis=-1)
        h = rmsnorm(x, norm1_g[l]) * (1.0 + sc1) + sh1
        x = x + g1 * hybrid_mixer(h, w_in[l], gdn_conv_w[l], gdn_a_log[l], gdn_dt_bias[l], gdn_norm_g[l],
                                  ssd_conv_w[l], ssd_conv_b[l], ssd_a_log[l], ssd_dt_bias[l], ssd_d[l],
                                  ssd_norm_g[l], w_out[l])
        h = rmsnorm(x, norm2_g[l]) * (1.0 + sc2) + sh2
        x = x + g2 * moe_ffn(h, router_w[l], router_b[l], moe_w_gu[l], moe_b_gu[l],
                             moe_w_down[l], moe_b_down[l])
    return rmsnorm(x, final_g)


_first_inputs = first_inputs


def first_inputs(seed=0):
    import zlib

    import numpy as np

    out = dict(_first_inputs(seed))
    spreads = {}
    factors = {'norm1_g': 4.599,
     'norm2_g': 3.792,
     'gdn_norm_g': 8.0,
     'ssd_conv_b': 7.33,
     'ssd_d': 8.0,
     'ssd_norm_g': 8.0,
     'router_b': 5.266,
     'moe_b_gu': 8.0,
     'moe_b_down': 8.0,
     'final_g': 2.864}
    for name, (base, spread) in spreads.items():
        noise = np.random.default_rng([zlib.crc32(name.encode()), seed]).standard_normal(out[name].shape)
        drawn = base * np.exp(spread * noise) if base else spread * noise
        out[name] = jnp.asarray(drawn.astype(out[name].dtype))
    for name, factor in factors.items():
        out[name] = (out[name] * factor).astype(out[name].dtype)
    return out


_narrow_inputs = first_inputs


def first_inputs(seed=0):

    out = dict(_narrow_inputs(seed))
    wider = {'ssd_conv_b': 4.25,
     'ssd_d': 12.0,
     'ssd_norm_g': 7.8,
     'router_b': 3.57,
     'moe_b_gu': 6.16,
     'moe_b_down': 12.0,
     'final_g': 3.3}
    for name, times in wider.items():
        mean = out[name].mean()
        out[name] = (mean + times * (out[name] - mean)).astype(out[name].dtype)
    return out


NSA_HEADS = 8
NSA_KV_GROUPS = 2
NSA_HEADS_PER_GROUP = NSA_HEADS // NSA_KV_GROUPS
NSA_HEAD_DIM = 64
CMP_BLOCK = 32
CMP_STRIDE = 16
CMP_RATIO = CMP_BLOCK // CMP_STRIDE
CMP_HIDDEN = 256
SLC_BLOCK = 64
SLC_TOPK = 16
WINDOW = 512
Q_BLOCK = 128
GLA_HEADS = 4
GLA_KEY_DIM = 64
GLA_VAL_DIM = 128
GLA_RANK = 16
GLA_TAU = 16.0
GLA_CHUNK = 64
MOE_GROUPS = 4
MOE_EXPERTS_PER_GROUP = 8
MOE_N_EXPERTS = MOE_GROUPS * MOE_EXPERTS_PER_GROUP
MOE_TOPK = 2
MOE_D_FF = 512

ROPE_THETA = 10000.0
NEG_INF = -1e30
FORCED_SCORE = 1e4

NSA_Q_W = NSA_HEADS * NSA_HEAD_DIM
NSA_KV_W = NSA_KV_GROUPS * NSA_HEAD_DIM
GLA_QK_W = GLA_HEADS * GLA_KEY_DIM
GLA_V_W = GLA_HEADS * GLA_VAL_DIM
IN_SPLITS = (NSA_Q_W,) + (NSA_KV_W,) * 6 + (3 * NSA_HEADS, GLA_QK_W, GLA_QK_W, GLA_V_W, GLA_RANK, GLA_V_W, D_MODEL, D_MODEL)
IN_WIDTH_2 = sum(IN_SPLITS)


def rms_norm(x, g):
    xf = x.astype(jnp.float32)
    y = xf * lax.rsqrt(jnp.mean(xf * xf, axis=-1, keepdims=True) + EPS)
    return (y * g.astype(jnp.float32)).astype(x.dtype)

def rope(x, pos):
    half = x.shape[-1] // 2
    inv = 1.0 / (ROPE_THETA ** (jnp.arange(half, dtype=jnp.float32) / half))
    ang = pos.astype(jnp.float32)[..., None] * inv
    cos, sin = jnp.cos(ang), jnp.sin(ang)
    x1 = x[..., :half].astype(jnp.float32)
    x2 = x[..., half:].astype(jnp.float32)
    return jnp.concatenate([x1 * cos - x2 * sin, x2 * cos + x1 * sin], axis=-1).astype(x.dtype)

def _heads(t, n, dh):
    b, s, _ = t.shape
    return t.reshape(b, s, n, dh).transpose(0, 2, 1, 3)

def compress_blocks(t, pos_emb, w1, b1, w2, b2):
    bsz, g, seq, dh = t.shape
    chunks = t.reshape(bsz, g, seq // CMP_STRIDE, CMP_STRIDE, dh)
    n_cmp = seq // CMP_STRIDE - CMP_RATIO + 1
    blocks = jnp.concatenate([chunks[:, :, m:m + n_cmp] for m in range(CMP_RATIO)], axis=3)
    blocks = blocks + pos_emb
    flat = blocks.reshape(bsz, g, n_cmp, CMP_BLOCK * dh)
    return jax.nn.gelu(flat @ w1 + b1) @ w2 + b2

def cmp_to_slc_overlap(n_cmp, n_slc):
    c0 = CMP_STRIDE * jnp.arange(n_cmp)[:, None]
    s0 = SLC_BLOCK * jnp.arange(n_slc)[None, :]
    ov = jnp.clip(jnp.minimum(c0 + CMP_BLOCK, s0 + SLC_BLOCK) - jnp.maximum(c0, s0), 0, None)
    return ov.astype(jnp.float32) / CMP_BLOCK

def nsa_attention(q, k_c, v_c, k_s, v_s, k_w, v_w, gate_logits, positions,
                  cmp_pos_k, cmp_w1_k, cmp_b1_k, cmp_w2_k, cmp_b2_k,
                  cmp_pos_v, cmp_w1_v, cmp_b1_v, cmp_w2_v, cmp_b2_v):
    f32 = jnp.float32
    bsz, seq, _ = q.shape
    G, hpg, dh = NSA_KV_GROUPS, NSA_HEADS_PER_GROUP, NSA_HEAD_DIM
    pos_h = positions[:, None, :]
    q = (rope(_heads(q, NSA_HEADS, dh), pos_h) * dh ** -0.5).reshape(bsz, G, hpg, seq, dh)
    k_cmp = compress_blocks(_heads(k_c, G, dh), cmp_pos_k, cmp_w1_k, cmp_b1_k, cmp_w2_k, cmp_b2_k)
    v_cmp = compress_blocks(_heads(v_c, G, dh), cmp_pos_v, cmp_w1_v, cmp_b1_v, cmp_w2_v, cmp_b2_v)
    n_cmp = k_cmp.shape[2]
    cmp_end = CMP_STRIDE * jnp.arange(n_cmp) + CMP_BLOCK - 1
    k_cmp = rope(k_cmp, jnp.take(positions, cmp_end, axis=1)[:, None, :])
    n_slc = seq // SLC_BLOCK
    top_n = min(SLC_TOPK, n_slc)
    overlap = cmp_to_slc_overlap(n_cmp, n_slc)
    k_blocks = rope(_heads(k_s, G, dh), pos_h).reshape(bsz, G, n_slc, SLC_BLOCK, dh)
    v_blocks = _heads(v_s, G, dh).reshape(bsz, G, n_slc, SLC_BLOCK, dh)
    pad = ((0, 0), (0, 0), (WINDOW, 0), (0, 0))
    k_win = jnp.pad(rope(_heads(k_w, G, dh), pos_h), pad)
    v_win = jnp.pad(_heads(v_w, G, dh), pad)
    gates = jax.nn.sigmoid(gate_logits.astype(f32)).reshape(bsz, seq, NSA_HEADS, 3)
    gates = gates.transpose(0, 2, 1, 3).reshape(bsz, G, hpg, seq, 3)
    b_idx = jnp.arange(bsz)[:, None, None, None]
    g_idx = jnp.arange(G)[None, :, None, None]
    blk_ids = jnp.arange(n_slc)

    def query_block(c):
        q0 = c * Q_BLOCK
        t_idx = q0 + jnp.arange(Q_BLOCK)
        qc = lax.dynamic_slice_in_dim(q, q0, Q_BLOCK, axis=3)
        gc = lax.dynamic_slice_in_dim(gates, q0, Q_BLOCK, axis=3)
        s = jnp.einsum('bghqd,bgnd->bghqn', qc, k_cmp).astype(f32)
        cmp_ok = cmp_end[None, :] <= t_idx[:, None]
        p_cmp = jax.nn.softmax(jnp.where(cmp_ok, s, NEG_INF), axis=-1) * cmp_ok
        o_cmp = jnp.einsum('bghqn,bgnd->bghqd', p_cmp.astype(v_cmp.dtype), v_cmp)
        imp = jnp.einsum('bghqn,nj->bgqj', p_cmp, overlap)
        cur = t_idx // SLC_BLOCK
        forced = (blk_ids[None, :] == 0) | (blk_ids[None, :] == cur[:, None]) | (blk_ids[None, :] == cur[:, None] - 1)
        imp = jnp.where(forced, FORCED_SCORE, imp)
        imp = jnp.where(blk_ids[None, :] <= cur[:, None], imp, NEG_INF)
        _, sel = lax.top_k(imp, top_n)
        k_sel = k_blocks[b_idx, g_idx, sel].reshape(bsz, G, Q_BLOCK, top_n * SLC_BLOCK, dh)
        v_sel = v_blocks[b_idx, g_idx, sel].reshape(bsz, G, Q_BLOCK, top_n * SLC_BLOCK, dh)
        key_pos = (sel[..., None] * SLC_BLOCK + jnp.arange(SLC_BLOCK)).reshape(bsz, G, Q_BLOCK, top_n * SLC_BLOCK)
        sel_ok = (key_pos <= t_idx[:, None])[:, :, None]
        s = jnp.einsum('bghqd,bgqkd->bghqk', qc, k_sel).astype(f32)
        p = jax.nn.softmax(jnp.where(sel_ok, s, NEG_INF), axis=-1)
        o_slc = jnp.einsum('bghqk,bgqkd->bghqd', p.astype(v_sel.dtype), v_sel)
        kw = lax.dynamic_slice_in_dim(k_win, q0, Q_BLOCK + WINDOW, axis=2)
        vw = lax.dynamic_slice_in_dim(v_win, q0, Q_BLOCK + WINDOW, axis=2)
        kpos = q0 - WINDOW + jnp.arange(Q_BLOCK + WINDOW)
        win_ok = (kpos[None, :] >= 0) & (kpos[None, :] <= t_idx[:, None]) & (kpos[None, :] > t_idx[:, None] - WINDOW)
        s = jnp.einsum('bghqd,bgkd->bghqk', qc, kw).astype(f32)
        p = jax.nn.softmax(jnp.where(win_ok, s, NEG_INF), axis=-1)
        o_win = jnp.einsum('bghqk,bgkd->bghqd', p.astype(vw.dtype), vw)
        o = gc[..., 0:1] * o_cmp + gc[..., 1:2] * o_slc + gc[..., 2:3] * o_win
        return o.astype(q.dtype)

    out = lax.map(query_block, jnp.arange(seq // Q_BLOCK))
    return out.transpose(1, 0, 4, 2, 3, 5).reshape(bsz, seq, NSA_HEADS * dh)

def gla_attention(q, k, v, a_low, r, w_a2, b_a, norm_g):
    f32 = jnp.float32
    bsz, seq, _ = q.shape
    H, dk, dv, C = GLA_HEADS, GLA_KEY_DIM, GLA_VAL_DIM, GLA_CHUNK
    q = _heads(q, H, dk).astype(f32) * dk ** -0.5
    k = _heads(k, H, dk).astype(f32)
    v = _heads(v, H, dv).astype(f32)
    log_a = _heads(jax.nn.log_sigmoid((a_low @ w_a2 + b_a).astype(f32)) / GLA_TAU, H, dk)
    nc = seq // C

    def to_chunks(t):
        return t.reshape(bsz, H, nc, C, t.shape[-1]).transpose(2, 0, 1, 3, 4)

    causal = jnp.tril(jnp.ones((C, C), dtype=bool))[:, :, None]

    def step(state, xs):
        qc, kc, vc, lac = xs
        b = jnp.cumsum(lac, axis=2)
        o_inter = jnp.einsum('bhtd,bhde->bhte', qc * jnp.exp(b), state)
        diff = b[:, :, :, None, :] - b[:, :, None, :, :]
        decay = jnp.where(causal, jnp.exp(jnp.where(causal, diff, 0.0)), 0.0)
        attn = jnp.einsum('bhtd,bhsd,bhtsd->bhts', qc, kc, decay)
        o_intra = jnp.einsum('bhts,bhse->bhte', attn, vc)
        b_last = b[:, :, -1, :]
        k_dec = kc * jnp.exp(b_last[:, :, None, :] - b)
        state = jnp.exp(b_last)[..., None] * state + jnp.einsum('bhsd,bhse->bhde', k_dec, vc)
        return state, o_inter + o_intra

    state0 = jnp.zeros((bsz, H, dk, dv), f32)
    _, o = lax.scan(step, state0, (to_chunks(q), to_chunks(k), to_chunks(v), to_chunks(log_a)))
    o = o.transpose(1, 2, 0, 3, 4).reshape(bsz, H, seq, dv)
    o = o * lax.rsqrt(jnp.mean(o * o, axis=-1, keepdims=True) + EPS)
    o = o.transpose(0, 2, 1, 3).reshape(bsz, seq, H * dv) * norm_g.astype(f32)
    return (o * jax.nn.silu(r.astype(f32))).astype(r.dtype)

def hybrid_mixer_2(u, positions, w_in,
                 cmp_pos_k, cmp_w1_k, cmp_b1_k, cmp_w2_k, cmp_b2_k,
                 cmp_pos_v, cmp_w1_v, cmp_b1_v, cmp_w2_v, cmp_b2_v,
                 gla_w_a2, gla_b_a, gla_norm_g, w_proj_nsa, w_proj_gla, w_out):
    z = u @ w_in
    (nsa_q, k_c, v_c, k_s, v_s, k_w, v_w, nsa_g,
     g_q, g_k, g_v, g_a, g_r, m_a, m_b) = jnp.split(z, np.cumsum(IN_SPLITS)[:-1].tolist(), axis=-1)
    y_a = nsa_attention(nsa_q, k_c, v_c, k_s, v_s, k_w, v_w, nsa_g, positions,
                        cmp_pos_k, cmp_w1_k, cmp_b1_k, cmp_w2_k, cmp_b2_k,
                        cmp_pos_v, cmp_w1_v, cmp_b1_v, cmp_w2_v, cmp_b2_v) @ w_proj_nsa
    y_b = gla_attention(g_q, g_k, g_v, g_a, g_r, gla_w_a2, gla_b_a, gla_norm_g) @ w_proj_gla
    mixed = jax.nn.sigmoid(m_a) * y_a + jax.nn.sigmoid(m_b) * y_b
    return mixed @ w_out

def hier_moe(v, w_grp, b_grp, w_exp, b_exp, w_gate, w_up, w_down):
    f32 = jnp.float32
    bsz, seq, d = v.shape
    vt = v.reshape(-1, d)
    grp_prob = jax.nn.softmax((vt @ w_grp + b_grp).astype(f32), axis=-1)
    p_grp, g_sel = lax.top_k(grp_prob, 1)
    exp_logits = (vt @ w_exp + b_exp).astype(f32).reshape(-1, MOE_GROUPS, MOE_EXPERTS_PER_GROUP)
    in_grp = jnp.take_along_axis(exp_logits, g_sel[:, :, None], axis=1)[:, 0]
    p_in, e_sel = lax.top_k(jax.nn.softmax(in_grp, axis=-1), MOE_TOPK)
    w = p_grp * p_in / jnp.sum(p_in, axis=-1, keepdims=True)
    expert_id = g_sel * MOE_EXPERTS_PER_GROUP + e_sel
    combine = jnp.einsum('tk,tke->te', w, jax.nn.one_hot(expert_id, MOE_N_EXPERTS, dtype=f32))
    y = jnp.zeros(vt.shape, f32)
    for e in range(MOE_N_EXPERTS):
        hdn = jax.nn.silu(vt @ w_gate[e]) * (vt @ w_up[e])
        y = y + (combine[:, e:e + 1].astype(hdn.dtype) * hdn) @ w_down[e]
    return y.reshape(bsz, seq, d).astype(v.dtype)

def second_inputs(seed: int = 0) -> dict:
    key = jax.random.key(seed)
    ks = jax.random.split(key, 32)
    f32 = jnp.float32
    L, D, dh = DEPTH, D_MODEL, NSA_HEAD_DIM

    def nrm(k, shape, scale):
        return jax.random.normal(k, shape, f32) * scale

    start = jax.random.randint(ks[1], (BATCH,), 0, 1024)
    positions = (start[:, None] + jnp.arange(SEQ)[None, :]).astype(jnp.int32)
    return {
        "x": nrm(ks[0], (BATCH, SEQ, D), 1.0),
        "positions": positions,
        "g_mix": 1.0 + nrm(ks[2], (L, D), 0.02),
        "w_in": nrm(ks[3], (L, D, IN_WIDTH_2), D ** -0.5),
        "cmp_pos_k": nrm(ks[4], (L, CMP_BLOCK, dh), 0.02),
        "cmp_w1_k": nrm(ks[5], (L, CMP_BLOCK * dh, CMP_HIDDEN), (CMP_BLOCK * dh) ** -0.5),
        "cmp_b1_k": nrm(ks[6], (L, CMP_HIDDEN), 0.01),
        "cmp_w2_k": nrm(ks[7], (L, CMP_HIDDEN, dh), CMP_HIDDEN ** -0.5),
        "cmp_b2_k": nrm(ks[8], (L, dh), 0.01),
        "cmp_pos_v": nrm(ks[9], (L, CMP_BLOCK, dh), 0.02),
        "cmp_w1_v": nrm(ks[10], (L, CMP_BLOCK * dh, CMP_HIDDEN), (CMP_BLOCK * dh) ** -0.5),
        "cmp_b1_v": nrm(ks[11], (L, CMP_HIDDEN), 0.01),
        "cmp_w2_v": nrm(ks[12], (L, CMP_HIDDEN, dh), CMP_HIDDEN ** -0.5),
        "cmp_b2_v": nrm(ks[13], (L, dh), 0.01),
        "gla_w_a2": nrm(ks[14], (L, GLA_RANK, GLA_QK_W), GLA_RANK ** -0.5),
        "gla_b_a": nrm(ks[15], (L, GLA_QK_W), 0.1),
        "gla_norm_g": 1.0 + nrm(ks[16], (L, GLA_V_W), 0.02),
        "w_proj_nsa": nrm(ks[17], (L, NSA_Q_W, D), NSA_Q_W ** -0.5),
        "w_proj_gla": nrm(ks[18], (L, GLA_V_W, D), GLA_V_W ** -0.5),
        "w_out": nrm(ks[19], (L, D, D), D ** -0.5),
        "g_ffn": 1.0 + nrm(ks[20], (L, D), 0.02),
        "w_grp": nrm(ks[21], (L, D, MOE_GROUPS), D ** -0.5),
        "b_grp": nrm(ks[22], (L, MOE_GROUPS), 0.01),
        "w_exp": nrm(ks[23], (L, D, MOE_N_EXPERTS), D ** -0.5),
        "b_exp": nrm(ks[24], (L, MOE_N_EXPERTS), 0.01),
        "w_gate": nrm(ks[25], (L, MOE_N_EXPERTS, D, MOE_D_FF), D ** -0.5),
        "w_up": nrm(ks[26], (L, MOE_N_EXPERTS, D, MOE_D_FF), D ** -0.5),
        "w_down": nrm(ks[27], (L, MOE_N_EXPERTS, MOE_D_FF, D), MOE_D_FF ** -0.5),
        "g_final": 1.0 + nrm(ks[28], (D,), 0.02),
    }

def second_block(x, positions, g_mix, w_in,
              cmp_pos_k, cmp_w1_k, cmp_b1_k, cmp_w2_k, cmp_b2_k,
              cmp_pos_v, cmp_w1_v, cmp_b1_v, cmp_w2_v, cmp_b2_v,
              gla_w_a2, gla_b_a, gla_norm_g, w_proj_nsa, w_proj_gla, w_out,
              g_ffn, w_grp, b_grp, w_exp, b_exp, w_gate, w_up, w_down, g_final):
    h = x
    for layer in range(DEPTH):
        u = rms_norm(h, g_mix[layer])
        h = h + hybrid_mixer_2(u, positions, w_in[layer],
                             cmp_pos_k[layer], cmp_w1_k[layer], cmp_b1_k[layer], cmp_w2_k[layer], cmp_b2_k[layer],
                             cmp_pos_v[layer], cmp_w1_v[layer], cmp_b1_v[layer], cmp_w2_v[layer], cmp_b2_v[layer],
                             gla_w_a2[layer], gla_b_a[layer], gla_norm_g[layer],
                             w_proj_nsa[layer], w_proj_gla[layer], w_out[layer])
        h = h + hier_moe(rms_norm(h, g_ffn[layer]), w_grp[layer], b_grp[layer], w_exp[layer], b_exp[layer],
                         w_gate[layer], w_up[layer], w_down[layer])
    return rms_norm(h, g_final)


def setup_inputs(seed=0):
    out = dict(first_inputs(seed))
    for name, value in second_inputs(seed + 1).items():
        if name != "x":
            out[name + "_2"] = value
    return out


def reference(
    x, c, ada_w, ada_b, norm1_g, norm2_g, w_in, gdn_conv_w, gdn_a_log, gdn_dt_bias, gdn_norm_g,
    ssd_conv_w, ssd_conv_b, ssd_a_log, ssd_dt_bias, ssd_d, ssd_norm_g, w_out, router_w,
    router_b, moe_w_gu, moe_b_gu, moe_w_down, moe_b_down, final_g, positions_2, g_mix_2, w_in_2,
    cmp_pos_k_2, cmp_w1_k_2, cmp_b1_k_2, cmp_w2_k_2, cmp_b2_k_2, cmp_pos_v_2, cmp_w1_v_2,
    cmp_b1_v_2, cmp_w2_v_2, cmp_b2_v_2, gla_w_a2_2, gla_b_a_2, gla_norm_g_2, w_proj_nsa_2,
    w_proj_gla_2, w_out_2, g_ffn_2, w_grp_2, b_grp_2, w_exp_2, b_exp_2, w_gate_2, w_up_2,
    w_down_2, g_final_2,
):
    x = first_block(
        x, c, ada_w, ada_b, norm1_g, norm2_g, w_in, gdn_conv_w, gdn_a_log, gdn_dt_bias,
        gdn_norm_g, ssd_conv_w, ssd_conv_b, ssd_a_log, ssd_dt_bias, ssd_d, ssd_norm_g, w_out,
        router_w, router_b, moe_w_gu, moe_b_gu, moe_w_down, moe_b_down, final_g,
    )
    return second_block(
        x, positions_2, g_mix_2, w_in_2, cmp_pos_k_2, cmp_w1_k_2, cmp_b1_k_2, cmp_w2_k_2,
        cmp_b2_k_2, cmp_pos_v_2, cmp_w1_v_2, cmp_b1_v_2, cmp_w2_v_2, cmp_b2_v_2, gla_w_a2_2,
        gla_b_a_2, gla_norm_g_2, w_proj_nsa_2, w_proj_gla_2, w_out_2, g_ffn_2, w_grp_2, b_grp_2,
        w_exp_2, b_exp_2, w_gate_2, w_up_2, w_down_2, g_final_2,
    )


_drawn_inputs = setup_inputs


def setup_inputs(seed=0):
    import zlib

    import numpy as np

    out = dict(_drawn_inputs(seed))
    spreads = {}
    factors = {'ssd_d': 8.0,
     'g_mix_2': 8.0,
     'cmp_pos_k_2': 38.218,
     'cmp_w1_k_2': 4.803,
     'cmp_b1_k_2': 64.0,
     'cmp_w2_k_2': 4.559,
     'cmp_b2_k_2': 64.0,
     'cmp_pos_v_2': 33.275,
     'cmp_b1_v_2': 33.64,
     'cmp_b2_v_2': 33.611,
     'gla_b_a_2': 8.0,
     'gla_norm_g_2': 8.0,
     'g_ffn_2': 5.455,
     'b_grp_2': 64.0,
     'b_exp_2': 24.296,
     'g_final_2': 8.287}
    for name, (base, spread) in spreads.items():
        noise = np.random.default_rng([zlib.crc32(name.encode()), seed]).standard_normal(out[name].shape)
        drawn = base * np.exp(spread * noise) if base else spread * noise
        out[name] = jnp.asarray(drawn.astype(out[name].dtype))
    for name, factor in factors.items():
        out[name] = (out[name] * factor).astype(out[name].dtype)
    return out
```

```python
import concourse.bass as bass
from concourse import mybir
from contextlib import ExitStack
import math

F32 = mybir.dt.float32
I32 = mybir.dt.int32
ALU = mybir.AluOpType
ACT = mybir.ActivationFunctionType
X_AXIS = mybir.AxisListType.X

P = 128
D = 1024
T = 2
KD = D // P
EPS = 1e-6
BIG = 1e30
SLOTS = 6
SLOT = 4096
NE = 32
CAP = 128


class Chain:

    def __init__(self, eng, sem):
        self.eng, self.sem, self.n = eng, sem, 0

    def __call__(self, ins):
        ins.then_inc(self.sem, 1)
        self.n += 1
        self.eng.wait_ge(self.sem, self.n)
        return ins


class Count:

    def __init__(self):
        self.n = 0

    def up(self, by=1):
        self.n += by
        return self.n


GH, SH, SP_ = 8, 16, 64
C_GZ, C_BA, C_SZ, C_XBC, C_DT = 3072, 4096, 4112, 5136, 6672


def program(nc, a, out, dbg=None):
    V, A, G, M = nc.vector, nc.scalar, nc.gpsimd, nc.tensor
    ctx = ExitStack()

    def sb(name, shape, dt=F32):
        return ctx.enter_context(nc.sbuf_tensor(name, shape, dt))

    made, cleared = [], []

    def sem(name):
        if cleared:
            return cleared.pop(0)
        made.append(ctx.enter_context(nc.semaphore(name)))
        return made[-1]

    def recycle(sems):
        with nc.Block() as block:
            @block.sync
            def _(sp):
                for s in sems:
                    sp.sem_clear(s)
        cleared.extend(sems)

    ring = sb("ring", [P, SLOTS, SLOT])
    ident = sb("ident", [P, P])
    tri_le = sb("tri_le", [P, P])
    tri_lt = sb("tri_lt", [P, P])
    ones = sb("ones", [P, P])
    small = sb("small", [P, 512])
    arena = sb("arena", [P, 25600])
    ps = ctx.enter_context(nc.psum_tensor("ps", [P, 8, 512], F32))

    def ar(at, *dims):
        n = math.prod(dims)
        assert at + n <= 25600, (at, dims)
        v = arena[:, at:at + n]
        if len(dims) == 1:
            return v
        names = "abcd"[:len(dims)]
        pat = f"p ({' '.join(names)}) -> p {' '.join(names)}"
        return v.rearrange(pat, **dict(zip(names, dims)))

    def banks(b, n, *dims):
        v = ps[:, b:b + n, :].rearrange("p a b -> p (a b)")
        names = "abcd"[:len(dims)]
        return v.rearrange(f"p ({' '.join(names)}) -> p {' '.join(names)}", **dict(zip(names, dims)))

    x_res = ar(0, T, D)
    mix = ar(2048, T, 2 * D)

    c_v, c_a, c_g = Chain(V, sem("vector_order")), Chain(A, sem("scalar_order")), Chain(G, sem("gpsimd_order"))

    def vv(ins):
        return c_v(ins)

    def aa(ins):
        return c_a(ins)

    def gg(ins):
        return c_g(ins)

    def bcast(ap, n):
        return ap.unsqueeze(len(ap.shape)).to_broadcast(list(ap.shape) + [n])

    def rep(ap, n):
        return ap.unsqueeze(1).to_broadcast([ap.shape[0], n] + list(ap.shape[1:]))

    def row_everywhere(ap):
        return ap.partition_broadcast(P)

    eps_t, eps128_t = small[:, 510:511], small[:, 511:512]

    def cols(w, c0, n=512):
        return w[:, c0:c0 + n].rearrange("(k p) n -> p k n", p=P)

    def slot(s, k=KD, n=512):
        v = ring[:, s, 0:k * n]
        return v.rearrange("p (k n) -> p k n", k=k)

    class Ring:

        def __init__(self, name):
            self.full = [sem(f"{name}_slot{s}_full") for s in range(SLOTS)]
            self.chunks, self.sent, self.used = [], 0, 0

        def add(self, src, shape, released):
            self.chunks.append((src, shape, released))

        def load(self, sp, upto):
            while self.sent < min(upto, len(self.chunks)):
                n = self.sent
                src, (k, w), _ = self.chunks[n]
                if n >= SLOTS:
                    sp.wait_ge(*self.chunks[n - SLOTS][2])
                sp.dma_start(slot(n % SLOTS, k, w), src).then_inc(self.full[n % SLOTS], 16)
                self.sent += 1

        def take(self, pe):
            n = self.used
            pe.wait_ge(self.full[n % SLOTS], 16 * (n // SLOTS + 1))
            self.used += 1
            _, (k, w), _ = self.chunks[n]
            return slot(n % SLOTS, k, w)

    w_in, ada_w = a["w_in"][0], a["ada_w"][0]
    ra = Ring("pre1")
    s_ada = sem("ada_chunk_multiplied")
    s_unit = sem("ssd_projection_ready")
    s_gunit = sem("gdn_projection_ready")
    for j in range(4):
        ra.add(cols(ada_w, 512 * j), (KD, 512), (s_ada, j + 1))
    for j in range(3):
        ra.add(cols(w_in, C_XBC + 512 * j), (KD, 512), (s_unit, 4 * j + 4))
    for j in range(2):
        ra.add(cols(w_in, C_SZ + 512 * j), (KD, 512), (s_unit, 12 + 2 * j + 2))
    for j in range(6):
        ra.add(cols(w_in, 512 * j), (KD, 512), (s_gunit, 4 * j + 4))
    for j in range(2):
        ra.add(cols(w_in, C_GZ + 512 * j), (KD, 512), (s_gunit, 24 + 2 * j + 2))
    for j in range(4, 12):
        ra.add(cols(ada_w, 512 * j), (KD, 512), (s_ada, j + 1))
    s_wout = sem("w_out_chunk_multiplied")
    for n in range(2):
        for k in range(2):
            ra.add(a["w_out"][0][1024 * k:1024 * k + 1024, 512 * n:512 * n + 512]
                   .rearrange("(k p) n -> p k n", p=P), (KD, 512), (s_wout, 2 * n + k + 1))

    hT = ar(12288, KD, T * P)
    xbcT = ar(14336, 12, T * P)
    convw = sb("convw", [P, 36 * 4 + 12 + 8])
    heads = small[:, 0:64]
    wsm = ar(6144, KD, 32)
    rowsA, rowsB = ar(17408, P), ar(17536, P)
    cb = ar(18432, KD, P)
    abias = ar(19456, 2 * D)
    n1g = ar(21504, D)
    modA, modB = ar(22528, D), ar(23552, D)
    hn = ar(2048, T, D)
    ss = small[:, 64:66]
    rstd = small[:, 66:68]

    s_const = sem("constants_ready")
    s_rows = sem("parameter_rows_loaded")
    s_small = sem("small_parameters_loaded")
    s_x = sem("x_loaded")
    s_rowsT = sem("parameter_rows_transposed")
    s_convw = sem("parameter_columns_ready")
    s_cb = sem("condition_ready")
    s_mod = sem("modulation_taken")
    s_ss = sem("squares_summed")
    s_h = sem("normed_ready")
    s_hT = sem("normed_transposed")
    s_hTt = sem("normed_transposed_taken")

    with nc.Block() as block:
        @block.sync
        def _(sp):
            sp.dma_start(rowsA[0:96, :], a["gdn_conv_w"][0].rearrange("k (c p) -> (k c) p", p=P)).then_inc(s_rows, 16)
            sp.dma_start(rowsB[0:48, :], a["ssd_conv_w"][0].rearrange("k (c p) -> (k c) p", p=P)).then_inc(s_rows, 16)
            sp.dma_start(rowsB[48:60, :], a["ssd_conv_b"][0].rearrange("(c p) -> c p", p=P)).then_inc(s_rows, 16)
            sp.dma_start(rowsB[60:68, :], a["c"][0].rearrange("(c p) -> c p", p=P)).then_inc(s_rows, 16)
            sp.dma_start(x_res, a["x"][0].rearrange("(t p) d -> p t d", p=P)).then_inc(s_x, 16)
            ra.load(sp, 2)
            at = 0
            for name, n in (("gdn_dt_bias", 8), ("ssd_dt_bias", 16), ("gdn_a_log", 8), ("ssd_a_log", 16), ("ssd_d", 16)):
                sp.dma_start(heads[:, at:at + n], row_everywhere(a[name][0])).then_inc(s_small, 16)
                at += n
            sp.dma_start(abias, row_everywhere(a["ada_b"][0][0:2 * D])).then_inc(s_small, 16)
            sp.dma_start(n1g, row_everywhere(a["norm1_g"][0])).then_inc(s_small, 16)
            sp.dma_start(wsm[:, :, 0:16], cols(w_in, C_BA, 16)).then_inc(s_small, 16)
            sp.dma_start(wsm[:, :, 16:32], cols(w_in, C_DT, 16)).then_inc(s_small, 16)
            ra.load(sp, 4 + SLOTS)

        @block.gpsimd
        def _(pool):
            gg(G.memset(ident[:, :], 0.0))
            gg(G.memset(tri_le[:, :], 1.0))
            gg(G.memset(tri_lt[:, :], 1.0))
            gg(G.memset(ones[:, :], 1.0))
            gg(G.memset(eps_t, EPS))
            gg(G.memset(eps128_t, EPS * P))
            gg(G.affine_select(out=ident[:, :], in_=ident[:, :], compare_op=ALU.not_equal, fill=1.0,
                               base=0, pattern=[[-1, P]], channel_multiplier=1))
            gg(G.affine_select(out=tri_le[:, :], in_=tri_le[:, :], compare_op=ALU.is_ge, fill=0.0,
                               base=0, pattern=[[1, P]], channel_multiplier=-1))
            G.affine_select(out=tri_lt[:, :], in_=tri_lt[:, :], compare_op=ALU.is_gt, fill=0.0,
                            base=0, pattern=[[1, P]], channel_multiplier=-1).then_inc(s_const, 1)

        @block.tensor
        def _(pe):
            pe.wait_ge(s_const, 1)
            pe.wait_ge(s_rows, 64)
            M.transpose(ps[:, 7, 0:96], rowsA[0:96, :], ident[0:96, 0:96])
            M.transpose(ps[:, 7, 96:164], rowsB[0:68, :], ident[0:68, 0:68]).then_inc(s_rowsT, 1)
            pe.wait_ge(s_cb, 1)
            for j in range(4):
                w = ra.take(pe)
                for k in range(KD):
                    last = M.matmul(ps[:, j, :], cb[:, k, :], w[:, k, :], start=(k == 0), stop=(k == KD - 1))
                last.then_inc(s_ada, 1)
            for t in range(T):
                pe.wait_ge(s_h, t + 1)
                for k in range(KD):
                    last = M.transpose(ps[:, 4 + 2 * t + k // 4, (k % 4) * P:(k % 4 + 1) * P],
                                       hn[:, t, k * P:(k + 1) * P], ident[:, :])
                last.then_inc(s_hT, 1)

        @block.scalar
        def _(act):
            act.wait_ge(s_rowsT, 1)
            aa(A.activation(convw[:, :], ps[:, 7, 0:164], ACT.Copy))
            aa(A.activation(convw[:, 156:164], convw[:, 156:164], ACT.Silu))
            A.activation(cb, bcast(convw[:, 156:164], P), ACT.Copy).then_inc(s_cb, 1)
            act.wait_ge(s_x, 16)
            for t in range(T):
                A.activation(hn[:, t, :], x_res[:, t, :], ACT.Square, accum_out=ss[:, t:t + 1]).then_inc(s_ss, 1)
            act.wait_ge(s_ss, 2)
            A.activation(rstd, ss, ACT.Sqrt, bias=eps_t, scale=1.0 / D).then_inc(s_ss, 1)
            for t in range(T):
                act.wait_ge(s_hT, t + 1)
                for k2 in range(2):
                    A.activation(hT[:, 4 * k2:4 * k2 + 4, t * P:(t + 1) * P],
                                 ps[:, 4 + 2 * t + k2, :].rearrange("p (k m) -> p k m", k=4), ACT.Copy).then_inc(s_hTt, 1)

        @block.vector
        def _(dve):
            dve.wait_ge(s_ss, 3)
            vv(V.reciprocal(rstd, rstd))
            dve.wait_ge(s_x, 16)
            for t in range(T):
                vv(V.tensor_scalar(hn[:, t, :], x_res[:, t, :], rstd[:, t:t + 1], None, ALU.mult))
            dve.wait_ge(s_small, 16 * 9)
            dve.wait_ge(s_ada, 4)
            vv(V.tensor_tensor(modB, banks(0, 2, 1024), abias[:, 0:D], ALU.add))
            vv(V.tensor_tensor(modA, banks(2, 2, 1024), abias[:, D:2 * D], ALU.add))
            vv(V.scalar_tensor_tensor(modA, modA, 1.0, n1g, ALU.add, ALU.mult))
            for t in range(T):
                vv(V.tensor_tensor(hn[:, t, :], hn[:, t, :], modA, ALU.mult))
                V.tensor_tensor(hn[:, t, :], hn[:, t, :], modB, ALU.add).then_inc(s_h, 1)

    sm = small[:, 96:160].rearrange("p (t c) -> p t c", t=T)
    soft = small[:, 160:208].rearrange("p (t c) -> p t c", t=T)
    dec = small[:, 208:256].rearrange("p (t c) -> p t c", t=T)
    beta = small[:, 256:272].rearrange("p (t c) -> p t c", t=T)
    negA = small[:, 272:296]
    tmp24 = small[:, 296:344].rearrange("p (t c) -> p t c", t=T)
    s_conv = sem("ssd_unit_taken")
    s_act = sem("ssd_convolved")
    s_zt = sem("ssd_gate_taken")
    s_sm = sem("narrow_taken")
    s_sp = sem("softplus_steps")

    def conv(dve, order_ready, first, n, dst, tap0, bias0, ready, taken, taps):
        for u in range(n):
            dve.wait_ge(ready, u + 1)
            src = ps[:, u % 8, 0:T * P]
            w = [convw[:, tap0 + k * taps + u:tap0 + k * taps + u + 1] for k in range(4)]
            if bias0 is None:
                vv(V.tensor_scalar(dst(u), src, w[3], None, ALU.mult))
            else:
                vv(V.tensor_scalar(dst(u), src, w[3], convw[:, bias0 + u:bias0 + u + 1], ALU.mult, ALU.add))
            for s in (1, 2, 3):
                ins = V.scalar_tensor_tensor(dst(u)[:, s:T * P], src[:, 0:T * P - s], w[3 - s], dst(u)[:, s:T * P],
                                             ALU.mult, ALU.add)
                if s < 3:
                    vv(ins)
                else:
                    ins.then_inc(taken, 1)

    with nc.Block() as block:
        @block.sync
        def _(sp):
            ra.load(sp, 9 + SLOTS)

        @block.tensor
        def _(pe):
            for j in range(3):
                w = ra.take(pe)
                for c in range(4):
                    u = 4 * j + c
                    if u >= 8:
                        pe.wait_ge(s_conv, u - 7)
                    for k in range(KD):
                        last = M.matmul(ps[:, u % 8, 0:T * P], w[:, k, c * P:(c + 1) * P], hT[:, k, :],
                                        start=(k == 0), stop=(k == KD - 1))
                    last.then_inc(s_unit, 1)
            for n in range(2):
                w = ra.take(pe)
                for t in range(T):
                    u = 12 + 2 * n + t
                    pe.wait_ge(s_conv, u - 7)
                    for k in range(KD):
                        last = M.matmul(ps[:, u % 8, :], hT[:, k, t * P:(t + 1) * P], w[:, k, :],
                                        start=(k == 0), stop=(k == KD - 1))
                    last.then_inc(s_unit, 1)
            for t in range(T):
                u = 16 + t
                pe.wait_ge(s_conv, u - 7)
                for k in range(KD):
                    last = M.matmul(ps[:, u % 8, 0:32], hT[:, k, t * P:(t + 1) * P], wsm[:, k, :],
                                    start=(k == 0), stop=(k == KD - 1))
                last.then_inc(s_unit, 1)

        @block.scalar
        def _(act):
            for u in range(12):
                act.wait_ge(s_conv, u + 1)
                A.activation(xbcT[:, u, :], xbcT[:, u, :], ACT.Silu).then_inc(s_act, 1)
            for u in range(12, 16):
                act.wait_ge(s_unit, u + 1)
                n, t = divmod(u - 12, 2)
                A.activation(mix[:, t, D + 512 * n:D + 512 * n + 512], ps[:, u % 8, :], ACT.Silu).then_inc(s_zt, 1)
            act.wait_ge(s_sm, 3)
            aa(A.activation(beta, sm[:, :, 0:8], ACT.Sigmoid))
            aa(A.activation(tmp24, tmp24, ACT.Exp))
            aa(A.activation(negA, heads[:, 24:48], ACT.Exp))
            A.activation(tmp24, tmp24, ACT.Ln, bias=1.0).then_inc(s_sp, 1)

        @block.vector
        def _(dve):
            conv(dve, None, 0, 12, lambda u: xbcT[:, u, :], 96, 144, s_unit, s_conv, 12)
            dve.wait_ge(s_unit, 18)
            for t in range(T):
                V.tensor_copy(sm[:, t, :], ps[:, t, 0:32]).then_inc(s_sm, 1)
            dve.wait_ge(s_sm, 2)
            vv(V.tensor_tensor(soft, sm[:, :, 8:32], rep(heads[:, 0:24], T), ALU.add))
            V.scalar_tensor_tensor(tmp24, soft, -1.0, soft, ALU.mult, ALU.min).then_inc(s_sm, 1)
            vv(V.tensor_scalar(soft, soft, 0.0, None, ALU.max))
            dve.wait_ge(s_sp, 1)
            vv(V.tensor_tensor(soft, soft, tmp24, ALU.add))
            vv(V.scalar_tensor_tensor(dec, soft, -1.0, rep(negA, T), ALU.mult, ALU.mult))

    x_tok = ar(6400, D)
    b_tok = ar(7424, 2, P)
    xdt = ar(7680, D)
    xde = ar(8704, D)
    state = ar(9728, 2, 512)
    yb = ar(10752, D)
    abc = ar(17408, SH, P)
    dmat = ar(19456, SH, P)
    neg_t = ar(21504, P)
    cbT = ar(21632, 2, P)
    ysq = ar(21888, D)
    sng = ar(22912, D)
    acum = small[:, 344:360]
    eac = small[:, 360:376]
    edec = small[:, 376:392]
    atot = small[:, 392:408]
    gss = small[:, 408:410]

    s_p3 = sem("ssd_parameters_loaded")
    s_neg = sem("causal_mask_ready")
    s_abc = sem("ssd_decays_repeated")
    s_row = sem("ssd_decay_rows")
    s_tr = sem("ssd_transposes")
    s_rowt = sem("ssd_rows_taken")
    s_trt = sem("ssd_transposes_taken")
    s_cb3 = sem("ssd_cb_ready")
    s_dx = sem("ssd_exponents_ready")
    s_de = sem("ssd_decays_ready")
    s_m3 = sem("ssd_operands_ready")
    s_y3 = sem("ssd_products_ready")
    s_st = sem("ssd_state_taken")
    s_y3t = sem("ssd_products_taken")
    s_var3, s_root3 = sem("ssd_squares_summed"), sem("ssd_roots_ready")

    with nc.Block() as block:
        @block.sync
        def _(sp):
            sp.dma_start(sng, row_everywhere(a["ssd_norm_g"][0])).then_inc(s_p3, 16)

        @block.gpsimd
        def _(pool):
            gg(G.memset(neg_t, 0.0))
            G.affine_select(out=neg_t, in_=neg_t, compare_op=ALU.is_ge, fill=-BIG, base=0,
                            pattern=[[1, P]], channel_multiplier=-1).then_inc(s_neg, 1)
            for t in range(T):
                if t:
                    pool.wait_ge(s_y3, 2)
                G.tensor_copy(abc, bcast(dec[:, t, 8:24], P)).then_inc(s_abc, 1)

        @block.tensor
        def _(pe):
            for t in range(T):
                tok = slice(t * P, (t + 1) * P)
                pe.wait_ge(s_abc, t + 1)
                if t:
                    pe.wait_ge(s_y3t, 1)
                    pe.wait_ge(s_st, 1)
                for h in range(SH):
                    last = M.matmul(ps[:, h // 4, (h % 4) * P:(h % 4 + 1) * P], abc[:, h, :], tri_le[:, :])
                M.matmul(ps[:, 4, 0:SH], tri_le[:, :], dec[:, t, 8:24])
                last = M.matmul(ps[:, 4, 16:16 + SH], ones[:, :], dec[:, t, 8:24])
                last.then_inc(s_row, 1)
                for g in range(2):
                    M.matmul(ps[:, 5, g * P:(g + 1) * P], xbcT[:, 8 + g, tok], xbcT[:, 10 + g, tok])
                for g in range(2):
                    last = M.transpose(ps[:, 5, (2 + g) * P:(3 + g) * P], xbcT[:, 8 + g, tok], ident[:, :])
                for k in range(KD):
                    last = M.transpose(ps[:, 6 + k // 4, (k % 4) * P:(k % 4 + 1) * P], xbcT[:, k, tok], ident[:, :])
                last.then_inc(s_tr, 1)
                pe.wait_ge(s_m3, 2 * t + 2)
                for h in range(SH):
                    last = M.matmul(ps[:, h // 8, (h % 8) * SP_:(h % 8 + 1) * SP_], abc[:, h, :],
                                    xdt[:, h * SP_:(h + 1) * SP_])
                for g in range(2):
                    if t == 0:
                        last = M.matmul(ps[:, 2 + g, :], b_tok[:, g, :], xde[:, g * 512:(g + 1) * 512])
                    else:
                        last = M.matmul(ps[:, 2 + g, :], xbcT[:, 10 + g, tok], state[:, g, :])
                last.then_inc(s_y3, 2)

        @block.scalar
        def _(act):
            for t in range(T):
                act.wait_ge(s_dx, 3 * t + 1)
                A.activation(eac, acum, ACT.Exp).then_inc(s_de, 1)
                A.activation(edec, edec, ACT.Exp).then_inc(s_de, 1)
                for q in range(2):
                    act.wait_ge(s_dx, 3 * t + 2 + q)
                    A.activation(dmat[:, 8 * q:8 * q + 8, :], dmat[:, 8 * q:8 * q + 8, :], ACT.Exp).then_inc(s_de, 1)
                if t == 0:
                    act.wait_ge(s_y3, 2)
                    A.activation(state, banks(2, 2, 2, 512), ACT.Copy).then_inc(s_st, 1)
                act.wait_ge(s_var3, t + 1)
                A.activation(gss, gss, ACT.Sqrt, bias=eps_t, scale=1.0 / 512).then_inc(s_root3, 1)

        @block.vector
        def _(dve):
            dve.wait_ge(s_neg, 1)
            for t in range(T):
                dve.wait_ge(s_row, t + 1)
                vv(V.tensor_copy(acum, ps[:, 4, 0:SH]))
                V.tensor_tensor(edec, ps[:, 4, 16:16 + SH], acum, ALU.subtract).then_inc(s_dx, 1)
                for h in range(SH):
                    ins = V.scalar_tensor_tensor(dmat[:, h, :], ps[:, h // 4, (h % 4) * P:(h % 4 + 1) * P],
                                                 acum[:, h:h + 1], neg_t, ALU.subtract, ALU.add)
                    if h % 8 == 7:
                        ins.then_inc(s_dx, 1)
                dve.wait_ge(s_tr, t + 1)
                vv(V.tensor_copy(b_tok, ps[:, 5, 256:512].rearrange("p (g n) -> p g n", g=2)))
                vv(V.tensor_copy(cbT, ps[:, 5, 0:256].rearrange("p (g n) -> p g n", g=2)))
                vv(V.tensor_copy(x_tok, banks(6, 2, 1024)))
                xh = x_tok.rearrange("p (h q) -> p h q", h=SH)
                xd = xdt.rearrange("p (h q) -> p h q", h=SH)
                vv(V.tensor_tensor(xd, xh, bcast(soft[:, t, 8:24], SP_), ALU.mult))
                dve.wait_ge(s_de, 4 * t + 2)
                V.tensor_tensor(xde.rearrange("p (h q) -> p h q", h=SH), xd, bcast(edec, SP_), ALU.mult).then_inc(s_m3, 1)
                dve.wait_ge(s_de, 4 * t + 4)
                for g in range(2):
                    ins = V.tensor_tensor(abc[:, 8 * g:8 * g + 8, :], dmat[:, 8 * g:8 * g + 8, :],
                                          rep(cbT[:, g, :], 8), ALU.mult)
                    if g == 0:
                        vv(ins)
                ins.then_inc(s_m3, 1)
                dve.wait_ge(s_y3, 2 * t + 2)
                yh = yb.rearrange("p (h q) -> p h q", h=SH)
                vv(V.tensor_tensor(ysq.rearrange("p (h q) -> p h q", h=SH), xh, bcast(heads[:, 48:64], SP_), ALU.mult))
                ins = V.tensor_tensor(yb, ysq, banks(0, 2, 1024), ALU.add)
                if t == 0:
                    ins.then_inc(s_y3t, 1)
                    dve.wait_ge(s_y3t, 1)
                else:
                    vv(ins)
                    vv(V.tensor_tensor(ysq.rearrange("p (h q) -> p h q", h=SH), banks(2, 2, SH, SP_), bcast(eac, SP_), ALU.mult))
                    vv(V.tensor_tensor(yb, yb, ysq, ALU.add))
                vv(V.tensor_tensor(yb, yb, mix[:, t, D:2 * D], ALU.mult))
                vv(V.tensor_tensor(ysq, yb, yb, ALU.mult))
                V.tensor_reduce(gss, ysq.rearrange("p (g n) -> p g n", g=2), X_AXIS, ALU.add).then_inc(s_var3, 1)
                dve.wait_ge(s_root3, t + 1)
                vv(V.reciprocal(gss, gss))
                if t == 0:
                    dve.wait_ge(s_p3, 16)
                vv(V.tensor_tensor(yb, yb, sng, ALU.mult))
                vv(V.tensor_tensor(mix[:, t, D:2 * D].rearrange("p (g n) -> p g n", g=2),
                                   yb.rearrange("p (g n) -> p g n", g=2), bcast(gss, 512), ALU.mult))

    qkvT = ar(6144, 24, T * P)
    sqT = ar(14336, 16, T * P)
    rsT = ar(18432, 16, T * P)
    ones128 = ar(22528, P)
    s_gconv = sem("gdn_unit_taken")
    s_gact = sem("gdn_convolved")
    s_gz = sem("gdn_gate_taken")
    s_sq = sem("gdn_squares_ready")
    s_sqs = sem("gdn_lengths_ready")
    s_on = sem("scaled_ones_ready")
    s_len = sem("gdn_length_roots_ready")

    with nc.Block() as block:
        @block.sync
        def _(sp):
            ra.load(sp, 17 + SLOTS)

        @block.gpsimd
        def _(pool):
            G.memset(ones128, float(P)).then_inc(s_on, 1)
            for u in range(16):
                pool.wait_ge(s_gact, u + 1)
                G.tensor_tensor(sqT[:, u, :], qkvT[:, u, :], qkvT[:, u, :], ALU.mult).then_inc(s_sq, 1)

        @block.tensor
        def _(pe):
            for j in range(6):
                w = ra.take(pe)
                for c in range(4):
                    u = 4 * j + c
                    if u >= 8:
                        pe.wait_ge(s_gconv, u - 7)
                    for k in range(KD):
                        last = M.matmul(ps[:, u % 8, 0:T * P], w[:, k, c * P:(c + 1) * P], hT[:, k, :],
                                        start=(k == 0), stop=(k == KD - 1))
                    last.then_inc(s_gunit, 1)
            for n in range(2):
                w = ra.take(pe)
                for t in range(T):
                    u = 24 + 2 * n + t
                    pe.wait_ge(s_gconv, u - 7)
                    for k in range(KD):
                        last = M.matmul(ps[:, u % 8, :], hT[:, k, t * P:(t + 1) * P], w[:, k, :],
                                        start=(k == 0), stop=(k == KD - 1))
                    last.then_inc(s_gunit, 1)
            pe.wait_ge(s_on, 1)
            pe.wait_ge(s_sq, 16)
            pe.wait_ge(s_gconv, 24)
            pe.wait_ge(s_gz, 4)
            for b in range(8):
                last = M.matmul(ps[:, b, :], ones128 if b < 4 else ones[:, :],
                                sqT[:, 2 * b:2 * b + 2, :].rearrange("p a b -> p (a b)"))
                last.then_inc(s_sqs, 1)

        @block.scalar
        def _(act):
            for u in range(24):
                act.wait_ge(s_gconv, u + 1)
                A.activation(qkvT[:, u, :], qkvT[:, u, :], ACT.Silu).then_inc(s_gact, 1)
            for u in range(24, 28):
                act.wait_ge(s_gunit, u + 1)
                n, t = divmod(u - 24, 2)
                A.activation(mix[:, t, 512 * n:512 * n + 512], ps[:, u % 8, :], ACT.Silu).then_inc(s_gz, 1)
            for b in range(8):
                act.wait_ge(s_sqs, b + 1)
                A.activation(rsT[:, 2 * b:2 * b + 2, :], ps[:, b, :].rearrange("p (a b) -> p a b", a=2), ACT.Sqrt,
                             bias=eps128_t if b < 4 else eps_t).then_inc(s_len, 1)

        @block.vector
        def _(dve):
            conv(dve, None, 0, 24, lambda u: qkvT[:, u, :], 0, None, s_gunit, s_gconv, 24)
            for b in range(8):
                dve.wait_ge(s_len, b + 1)
                r = rsT[:, 2 * b:2 * b + 2, :]
                vv(V.reciprocal(r, r))
                dve.wait_ge(s_gact, 2 * b + 2)
                vv(V.tensor_tensor(qkvT[:, 2 * b:2 * b + 2, :], qkvT[:, 2 * b:2 * b + 2, :], r, ALU.mult))

    if dbg == "b4":
        s_o = sem("dbg")
        with nc.Block() as block:
            @block.sync
            def _(sp):
                sp.dma_start(out[0].rearrange("(t p) d -> p t d", p=P), mix[:, :, D:2 * D]).then_inc(s_o, 16)
                sp.wait_ge(s_o, 16)
        return

    W = 12288
    Lm, Xi, Yi = ar(W, GH, P), ar(W + 1024, GH, P), ar(W + 2048, GH, P)
    LM, Q1 = ar(W + 3072, GH, P), ar(W + 4096, GH, P)
    qkd, kbe, kdc = ar(W + 5120, GH, P), ar(W + 6144, GH, P), ar(W + 7168, GH, P)
    Ug, wTg, qdT, stg = ar(W + 8192, GH, P), ar(W + 9216, GH, P), ar(W + 10240, GH, P), ar(W + 11264, GH, P)
    ob, osq, gbc = LM, Q1, Xi
    NL = 7
    masks = sb("masks", [P, NL + 3, P])
    neg_u, pos_l, gng = masks[:, NL, :], masks[:, NL + 1, :], masks[:, NL + 2, :]
    gam, gdk = small[:, 344:352], small[:, 352:360]
    gtot, eg, beg = small[:, 360:368], small[:, 368:376], small[:, 376:384]
    oss = small[:, 384:392]

    s_gm = sem("gdn_masks_ready")
    s_gn = sem("gdn_norm_weight_loaded")
    s_gbc = sem("gdn_decays_repeated")
    s_grow = sem("gdn_decay_rows")
    s_gx = sem("gdn_exponents_ready")
    s_ge = sem("gdn_decays_ready")
    s_gkk = sem("gdn_products_of_keys")
    s_gtr = sem("gdn_transposes")
    s_L = sem("gdn_L_ready")
    s_gops = sem("gdn_operands_ready")
    s_lm = sem("gdn_masked_L_ready")
    s_xi = sem("gdn_inverse_started")
    s_xt = sem("gdn_inverse_transposed")
    s_yt = sem("gdn_inverse_transpose_taken")
    s_q1 = sem("gdn_level_product")
    s_q1t = sem("gdn_level_product_taken")
    s_dd = sem("gdn_level_correction")
    s_upd = sem("gdn_inverse_updated")
    s_uw = sem("gdn_solutions")
    s_wt = sem("gdn_w_taken")
    s_ws = sem("gdn_state_read")
    s_u = sem("gdn_new_values")
    s_o = sem("gdn_outputs")
    s_gst = sem("gdn_state_taken")
    s_oss = sem("gdn_output_squares")
    s_or = sem("gdn_output_roots")
    s_cb2 = sem("condition_repeated_again")

    with nc.Block() as block:
        @block.sync
        def _(sp):
            sp.dma_start(gng, row_everywhere(a["gdn_norm_g"][0])).then_inc(s_gn, 16)

        @block.gpsimd
        def _(pool):
            gg(G.memset(masks[:, 0:NL + 1, :], 0.0))
            gg(G.memset(pos_l, 0.0))
            for lv in range(NL):
                b = 1 << lv
                m = masks[:, lv, :].rearrange("p (n j) -> p n j", j=2 * b)
                gg(G.memset(m[:, :, 0:b], 1.0))
                gg(G.affine_select(out=m, in_=m, compare_op=ALU.is_ge, fill=0.0, base=-b,
                                   pattern=[[-2 * b, P // (2 * b)], [0, 2 * b]], channel_multiplier=1))
                gg(G.affine_select(out=m, in_=m, compare_op=ALU.is_ge, fill=0.0, base=2 * b - 1,
                                   pattern=[[2 * b, P // (2 * b)], [0, 2 * b]], channel_multiplier=-1))
            gg(G.affine_select(out=neg_u, in_=neg_u, compare_op=ALU.is_ge, fill=-BIG, base=0,
                               pattern=[[1, P]], channel_multiplier=-1))
            G.affine_select(out=pos_l, in_=pos_l, compare_op=ALU.is_gt, fill=BIG, base=0,
                            pattern=[[-1, P]], channel_multiplier=1).then_inc(s_gm, 1)
            for t in range(T):
                if t:
                    pool.wait_ge(s_o, 1)
                G.tensor_copy(gbc, bcast(dec[:, t, 0:8], P)).then_inc(s_gbc, 1)
                pool.wait_ge(s_L, t + 1)
                G.tensor_tensor(LM, Lm, rep(masks[:, 0, :], GH), ALU.mult).then_inc(s_lm, 1)
                for lv in range(1, NL):
                    for g in range(2):
                        if lv == 1:
                            pool.wait_ge(s_xi, t + 1)
                        else:
                            pool.wait_ge(s_q1, 12 * t + 2 * (lv - 2) + g + 1)
                        G.tensor_tensor(LM[:, 4 * g:4 * g + 4, :], Lm[:, 4 * g:4 * g + 4, :],
                                        rep(masks[:, lv, :], 4), ALU.mult).then_inc(s_lm, 1)

        @block.tensor
        def _(pe):
            def per_head(b0, fn, start=True, stop=True):
                for h in range(GH):
                    lhsT, rhs = fn(h)
                    ins = M.matmul(ps[:, b0 + h // 4, (h % 4) * P:(h % 4 + 1) * P], lhsT, rhs, start=start, stop=stop)
                return ins

            for t in range(T):
                tok = slice(t * P, (t + 1) * P)
                pe.wait_ge(s_gbc, t + 1)
                per_head(0, lambda h: (gbc[:, h, :], tri_le[:, :]))
                M.matmul(ps[:, 7, 0:8], tri_le[:, :], dec[:, t, 0:8])
                M.matmul(ps[:, 7, 8:16], ones[:, :], dec[:, t, 0:8]).then_inc(s_grow, 1)
                per_head(2, lambda h: (qkvT[:, 8 + h, tok], qkvT[:, 8 + h, tok]))
                per_head(4, lambda h: (qkvT[:, 8 + h, tok], qkvT[:, h, tok])).then_inc(s_gkk, 1)
                pe.wait_ge(s_ge, (3 + t) * 1 if t == 0 else 3 + 4)
                for b0, c0 in ((6, 8), (0, 16)):
                    for h in range(GH):
                        last = M.transpose(ps[:, b0 + h // 4, (h % 4) * P:(h % 4 + 1) * P], qkvT[:, c0 + h, tok], ident[:, :])
                    last.then_inc(s_gtr, 1)
                pe.wait_ge(s_xi, t + 1)
                pe.wait_ge(s_gops, t + 1)
                for h in range(GH):
                    last = M.transpose(ps[:, 2 + h // 4, (h % 4) * P:(h % 4 + 1) * P], Xi[:, h, :], ident[:, :])
                last.then_inc(s_xt, 1)
                pe.wait_ge(s_yt, t + 1)
                for lv in range(1, NL):
                    for g in range(2):
                        pe.wait_ge(s_lm, 13 * t + 2 + 2 * (lv - 1) + g)
                        if lv > 1:
                            pe.wait_ge(s_upd, 12 * t + 2 * (lv - 2) + g + 1)
                        for h in range(4 * g, 4 * g + 4):
                            last = M.matmul(ps[:, g, (h % 4) * P:(h % 4 + 1) * P], LM[:, h, :], Yi[:, h, :])
                        last.then_inc(s_q1, 1)
                    for g in range(2):
                        pe.wait_ge(s_q1t, 12 * t + 2 * (lv - 1) + g + 1)
                        for h in range(4 * g, 4 * g + 4):
                            last = M.matmul(ps[:, 2 + g, (h % 4) * P:(h % 4 + 1) * P], Xi[:, h, :], Q1[:, h, :])
                        if lv < NL - 1:
                            for h in range(4 * g, 4 * g + 4):
                                last = M.matmul(ps[:, 4 + g, (h % 4) * P:(h % 4 + 1) * P], Q1[:, h, :], Xi[:, h, :])
                        last.then_inc(s_dd, 1)
                pe.wait_ge(s_upd, 12 * t + 12)
                last = per_head(0, lambda h: (Yi[:, h, :], Ug[:, h, :]))
                if t:
                    last = per_head(2, lambda h: (kbe[:, h, :], Yi[:, h, :]))
                last.then_inc(s_uw, 1)
                if t == 0:
                    pe.wait_ge(s_u, 1)
                    per_head(4, lambda h: (qkd[:, h, :], Ug[:, h, :]))
                    per_head(6, lambda h: (kdc[:, h, :], Ug[:, h, :])).then_inc(s_o, 1)
                    pe.wait_ge(s_gst, 1)
                    pe.wait_ge(s_oss, 1)
                else:
                    pe.wait_ge(s_wt, 1)
                    per_head(6, lambda h: (wTg[:, h, :], stg[:, h, :])).then_inc(s_ws, 1)
                    pe.wait_ge(s_u, 2)
                    for h in range(GH):
                        dst = ps[:, 4 + h // 4, (h % 4) * P:(h % 4 + 1) * P]
                        M.matmul(dst, qdT[:, h, :], stg[:, h, :], start=True, stop=False)
                        last = M.matmul(dst, qkd[:, h, :], Ug[:, h, :], start=False, stop=True)
                    last.then_inc(s_o, 1)

        @block.scalar
        def _(act):
            for t in range(T):
                act.wait_ge(s_gx, 3 * t + 1)
                aa(A.activation(eg, gam, ACT.Exp))
                A.activation(gdk, gdk, ACT.Exp).then_inc(s_ge, 1)
                act.wait_ge(s_gx, 3 * t + 3)
                A.activation(LM, LM, ACT.Exp, scale=-1.0).then_inc(s_ge, 1)
                A.activation(Q1, Q1, ACT.Exp).then_inc(s_ge, 1)
                if t:
                    A.activation(qdT, banks(0, 2, GH, P), ACT.Exp).then_inc(s_ge, 1)
                act.wait_ge(s_xt, t + 1)
                A.activation(Yi, banks(2, 2, GH, P), ACT.Copy).then_inc(s_yt, 1)
                for lv in range(1, NL):
                    for g in range(2):
                        act.wait_ge(s_q1, 12 * t + 2 * (lv - 1) + g + 1)
                        A.activation(Q1[:, 4 * g:4 * g + 4, :], ps[:, g, :].rearrange("p (h m) -> p h m", h=4),
                                     ACT.Copy).then_inc(s_q1t, 1)
                act.wait_ge(s_uw, t + 1)
                if t:
                    A.activation(wTg, banks(2, 2, GH, P), ACT.Copy).then_inc(s_wt, 1)
                else:
                    act.wait_ge(s_o, 1)
                    A.activation(stg, banks(6, 2, GH, P), ACT.Copy).then_inc(s_gst, 1)
                act.wait_ge(s_oss, 2 * t + 2)
                A.activation(oss, oss, ACT.Sqrt, bias=eps_t, scale=1.0 / P).then_inc(s_or, 1)
            A.activation(ar(W, KD, P), bcast(convw[:, 156:164], P), ACT.Copy).then_inc(s_cb2, 1)

        @block.vector
        def _(dve):
            dve.wait_ge(s_gm, 1)
            dve.wait_ge(s_gn, 16)
            for t in range(T):
                bt = beta[:, t, :]
                dve.wait_ge(s_grow, t + 1)
                vv(V.tensor_copy(gam, ps[:, 7, 0:8]))
                V.tensor_tensor(gdk, ps[:, 7, 8:16], gam, ALU.subtract).then_inc(s_gx, 1)
                for dst, mask in ((LM, pos_l), (Q1, neg_u)):
                    for h in range(GH):
                        last = V.scalar_tensor_tensor(dst[:, h, :], ps[:, h // 4, (h % 4) * P:(h % 4 + 1) * P],
                                                      gam[:, h:h + 1], mask, ALU.subtract, ALU.add)
                    last.then_inc(s_gx, 1)
                dve.wait_ge(s_gkk, t + 1)
                dve.wait_ge(s_ge, 3 if t == 0 else 7)
                for h in range(GH):
                    last = V.scalar_tensor_tensor(Lm[:, h, :], ps[:, 2 + h // 4, (h % 4) * P:(h % 4 + 1) * P],
                                                  bt[:, h:h + 1], LM[:, h, :], ALU.mult, ALU.mult)
                last.then_inc(s_L, 1)
                vv(V.tensor_tensor(qkd, banks(4, 2, GH, P), Q1, ALU.mult))
                vv(V.tensor_tensor(beg, bt, eg, ALU.mult))
                dve.wait_ge(s_gtr, 2 * t + 2)
                vv(V.tensor_tensor(kbe, banks(6, 2, GH, P), bcast(beg, P), ALU.mult))
                vv(V.tensor_tensor(kdc, banks(6, 2, GH, P), bcast(gdk, P), ALU.mult))
                if t:
                    vv(V.tensor_tensor(qdT, qdT, qkvT[:, 0:8, P:2 * P], ALU.mult))
                V.tensor_tensor(Ug, banks(0, 2, GH, P), bcast(bt, P), ALU.mult).then_inc(s_gops, 1)
                dve.wait_ge(s_lm, 13 * t + 1)
                V.tensor_tensor(Xi, rep(ident[:, :], GH), LM, ALU.subtract).then_inc(s_xi, 1)
                dve.wait_ge(s_xi, t + 1)
                for lv in range(1, NL):
                    for g in range(2):
                        dve.wait_ge(s_dd, 12 * t + 2 * (lv - 1) + g + 1)
                        y, x = Yi[:, 4 * g:4 * g + 4, :], Xi[:, 4 * g:4 * g + 4, :]
                        if lv < NL - 1:
                            vv(V.tensor_tensor(x, x, ps[:, 4 + g, :].rearrange("p (h m) -> p h m", h=4), ALU.subtract))
                        V.tensor_tensor(y, y, ps[:, 2 + g, :].rearrange("p (h m) -> p h m", h=4), ALU.subtract).then_inc(s_upd, 1)
                dve.wait_ge(s_uw, t + 1)
                if t == 0:
                    V.tensor_copy(Ug, banks(0, 2, GH, P)).then_inc(s_u, 1)
                else:
                    vv(V.tensor_copy(Ug, banks(0, 2, GH, P)))
                    dve.wait_ge(s_ws, 1)
                    V.tensor_tensor(Ug, Ug, banks(6, 2, GH, P), ALU.subtract).then_inc(s_u, 1)
                dve.wait_ge(s_o, t + 1)
                V.tensor_copy(ob, banks(4, 2, GH, P)).then_inc(s_oss, 1)
                dve.wait_ge(s_oss, 2 * t + 1)
                vv(V.tensor_tensor(osq, ob, ob, ALU.mult))
                V.tensor_reduce(oss, osq, X_AXIS, ALU.add).then_inc(s_oss, 1)
                dve.wait_ge(s_or, t + 1)
                vv(V.reciprocal(oss, oss))
                z = mix[:, t, 0:D].rearrange("p (h m) -> p h m", h=GH)
                vv(V.tensor_tensor(ob, ob, bcast(oss, P), ALU.mult))
                vv(V.tensor_tensor(ob, ob, rep(gng, GH), ALU.mult))
                vv(V.tensor_tensor(z, z, ob, ALU.mult))

    if dbg == "b5":
        s_o5 = sem("dbg")
        with nc.Block() as block:
            @block.sync
            def _(sp):
                sp.dma_start(out[0].rearrange("(t p) d -> p t d", p=P), mix[:, :, 0:D]).then_inc(s_o5, 16)
                sp.wait_ge(s_o5, 16)
        return

    mixT = ar(6144, 16, T * P)
    h2T = ar(10240, KD, T * P)
    cb2 = ar(12288, KD, P)
    n2g = ar(13312, D)
    rw = ar(14336, KD, NE)
    rb = ar(14592, NE)
    wo_t = ar(15616, 2 * 512)
    abias2 = ar(17408, 4, D)
    mods = ar(21504, 4, D)
    h2 = ar(2048, T, D)
    NI = 2 * NE + 1
    slot_of = sb("slot_of", [P, T, NI])
    gate_of = sb("gate_of", [P, T, NI])
    iota_row = sb("iota_row", [P, CAP])
    passes = sb("passes", [1, 1], I32)

    def select_top(dve, l, k, m8, sel, tmp, s1):
        n = l.shape[1]
        vv(V.max(m8, l))
        vv(V.tensor_scalar(sel, l, m8[:, k - 1:k], None, ALU.is_gt))
        vv(V.tensor_scalar(tmp, l, m8[:, k - 1:k], None, ALU.is_equal))
        vv(V.tensor_reduce(s1, sel, X_AXIS, ALU.add))
        vv(V.tensor_scalar(s1, s1, -1.0, float(k), ALU.mult, ALU.add))
        cum = scratch_cum[:, 0:n]
        vv(V.tensor_tensor_scan(cum, ones[:, 0:n], tmp, 0.0, ALU.mult, ALU.add))
        vv(V.scalar_tensor_tensor(tmp, cum, s1, tmp, ALU.is_le, ALU.mult))
        vv(V.tensor_tensor(sel, sel, tmp, ALU.add))

    scratch_cum = small[:, 470:502]
    lg = small[:, 0:64].rearrange("p (t e) -> p t e", t=T)
    sel = small[:, 64:128].rearrange("p (t e) -> p t e", t=T)
    selsum = small[:, 128:160]
    m8 = small[:, 160:176].rearrange("p (t e) -> p t e", t=T)
    nm = small[:, 176:178]
    s1 = small[:, 178:179]
    gs = small[:, 180:182]
    cmax = small[:, 184:185]
    tmpe = small[:, 192:224]
    ss2 = small[:, 224:226]

    s_p6 = sem("block6_parameters_loaded")
    s_modt = sem("late_modulation_taken")
    s_mT = sem("mixed_transposed")
    s_mTt = sem("mixed_transposed_taken")
    s_res = sem("residual_added")
    s_ss2 = sem("second_norm_squares")
    s_h2 = sem("second_normed_ready")
    s_h2T = sem("second_normed_transposed")
    s_h2Tt = sem("second_normed_transposed_taken")
    s_lg = sem("router_logits_ready")
    s_nm = sem("router_max_ready")
    s_el = sem("router_exponentials")
    s_sel = sem("selection_ready")
    s_rk = sem("ranks_ready")

    def dispatch_tables(dve, rank_bank):
        for t in range(T):
            vv(V.scalar_tensor_tensor(tmpe, ps[:, rank_bank, 32 * t:32 * t + 32], 1.0, sel[:, t, :], ALU.add, ALU.mult))
            vv(V.tensor_scalar(slot_of[:, t, 0:NE], tmpe, -1.0, None, ALU.add))
            vv(V.tensor_scalar(slot_of[:, t, NE:2 * NE], tmpe, -1.0 - CAP, None, ALU.add))
            vv(V.memset(slot_of[:, t, 2 * NE:NI], -1.0))
            vv(V.tensor_copy(gate_of[:, t, NE:2 * NE], gate_of[:, t, 0:NE]))
            vv(V.memset(gate_of[:, t, 2 * NE:NI], 0.0))
        vv(V.tensor_reduce(cmax, ps[:, rank_bank, 64:96], X_AXIS, ALU.max))
        vv(V.tensor_scalar(cmax, cmax, float(CAP), 1.0, ALU.is_gt, ALU.add))
        return V.tensor_copy(passes[0:1, 0:1], cmax[0:1, :])

    def rank_matmuls(rank_bank):
        M.matmul(ps[:, rank_bank, 0:32], tri_lt[:, :], sel[:, 0, :])
        M.matmul(ps[:, rank_bank, 32:64], tri_lt[:, :], sel[:, 1, :], start=True, stop=False)
        M.matmul(ps[:, rank_bank, 32:64], ones[:, :], sel[:, 0, :], start=False, stop=True)
        return M.matmul(ps[:, rank_bank, 64:96], ones[:, :], selsum)

    MOE1_LOADS = []

    with nc.Block() as block:
        @block.sync
        def _(sp):
            sp.dma_start(abias2.rearrange("p a b -> p (a b)"), row_everywhere(a["ada_b"][0][2 * D:6 * D])).then_inc(s_p6, 16)
            sp.dma_start(n2g, row_everywhere(a["norm2_g"][0])).then_inc(s_p6, 16)
            sp.dma_start(rw, a["router_w"][0].rearrange("(k p) e -> p k e", p=P)).then_inc(s_p6, 16)
            sp.dma_start(rb, row_everywhere(a["router_b"][0])).then_inc(s_p6, 16)
            ra.load(sp, 99)

        @block.gpsimd
        def _(pool):
            gg(G.iota(iota_row[:, :], pattern=[[1, CAP]], base=0, channel_multiplier=0,
                      allow_small_or_imprecise_dtypes=True))

        @block.tensor
        def _(pe):
            pe.wait_ge(s_cb2, 1)
            for j in range(8):
                w = ra.take(pe)
                if j >= 4:
                    pe.wait_ge(s_modt, j - 3)
                for k in range(KD):
                    last = M.matmul(ps[:, j % 4, :], cb2[:, k, :], w[:, k, :], start=(k == 0), stop=(k == KD - 1))
                last.then_inc(s_ada, 1)
                if j % 2 == 1 and j // 2 < 4:
                    i = j // 2
                    t, half = divmod(i, 2)
                    if i >= 2:
                        pe.wait_ge(s_mTt, i - 1)
                    for k in range(8):
                        last = M.transpose(ps[:, 4 + 2 * (i % 2) + k // 4, (k % 4) * P:(k % 4 + 1) * P],
                                           mix[:, t, (8 * half + k) * P:(8 * half + k + 1) * P], ident[:, :])
                    last.then_inc(s_mT, 1)
            pe.wait_ge(s_modt, 8)
            pe.wait_ge(s_mTt, 4)
            for n in range(2):
                for kh in range(2):
                    w = ra.take(pe)
                    for t in range(T):
                        for k in range(KD):
                            last = M.matmul(ps[:, 2 * t + n, :], mixT[:, 8 * kh + k, t * P:(t + 1) * P], w[:, k, :],
                                            start=(kh == 0 and k == 0), stop=(kh == 1 and k == KD - 1))
                    last.then_inc(s_wout, 1)
            for t in range(T):
                pe.wait_ge(s_h2, t + 1)
                for k in range(KD):
                    last = M.transpose(ps[:, 4 + 2 * t + k // 4, (k % 4) * P:(k % 4 + 1) * P],
                                       h2[:, t, k * P:(k + 1) * P], ident[:, :])
                last.then_inc(s_h2T, 1)
            pe.wait_ge(s_h2Tt, 4)
            for t in range(T):
                for k in range(KD):
                    last = M.matmul(ps[:, 0, 32 * t:32 * t + 32], h2T[:, k, t * P:(t + 1) * P], rw[:, k, :],
                                    start=(k == 0), stop=(k == KD - 1))
            last.then_inc(s_lg, 1)
            pe.wait_ge(s_sel, 1)
            rank_matmuls(1).then_inc(s_rk, 1)

        @block.scalar
        def _(act):
            for i in range(4):
                act.wait_ge(s_mT, i + 1)
                t, half = divmod(i, 2)
                A.activation(mixT[:, 8 * half:8 * half + 8, t * P:(t + 1) * P],
                             banks(4 + 2 * (i % 2), 2, 8, P), ACT.Copy).then_inc(s_mTt, 1)
            for t in range(T):
                act.wait_ge(s_res, t + 1)
                A.activation(h2[:, t, :], x_res[:, t, :], ACT.Square, accum_out=ss2[:, t:t + 1]).then_inc(s_ss2, 1)
            act.wait_ge(s_ss2, 2)
            A.activation(ss2, ss2, ACT.Sqrt, bias=eps_t, scale=1.0 / D).then_inc(s_ss2, 1)
            for t in range(T):
                act.wait_ge(s_h2T, t + 1)
                for k2 in range(2):
                    A.activation(h2T[:, 4 * k2:4 * k2 + 4, t * P:(t + 1) * P],
                                 ps[:, 4 + 2 * t + k2, :].rearrange("p (k m) -> p k m", k=4), ACT.Copy).then_inc(s_h2Tt, 1)
            act.wait_ge(s_nm, 1)
            for t in range(T):
                A.activation(gate_of[:, t, 0:NE], lg[:, t, :], ACT.Exp, bias=nm[:, t:t + 1]).then_inc(s_el, 1)

        @block.vector
        def _(dve):
            dve.wait_ge(s_p6, 64)
            for j in range(8):
                dve.wait_ge(s_ada, 5 + j)
                i, half = divmod(j, 2)
                V.tensor_tensor(mods[:, i, 512 * half:512 * half + 512], ps[:, j % 4, :],
                                abias2[:, i, 512 * half:512 * half + 512], ALU.add).then_inc(s_modt, 1)
            dve.wait_ge(s_modt, 8)
            vv(V.scalar_tensor_tensor(mods[:, 2, :], mods[:, 2, :], 1.0, n2g, ALU.add, ALU.mult))
            dve.wait_ge(s_wout, 4)
            for t in range(T):
                vv(V.tensor_tensor(wo_t, banks(2 * t, 2, 1024), mods[:, 0, :], ALU.mult))
                V.tensor_tensor(x_res[:, t, :], x_res[:, t, :], wo_t, ALU.add).then_inc(s_res, 1)
                dve.wait_ge(s_res, t + 1)
            dve.wait_ge(s_ss2, 3)
            vv(V.reciprocal(ss2, ss2))
            for t in range(T):
                vv(V.scalar_tensor_tensor(h2[:, t, :], x_res[:, t, :], ss2[:, t:t + 1], mods[:, 2, :], ALU.mult, ALU.mult))
                V.tensor_tensor(h2[:, t, :], h2[:, t, :], mods[:, 1, :], ALU.add).then_inc(s_h2, 1)
            dve.wait_ge(s_lg, 1)
            vv(V.tensor_tensor(lg, ps[:, 0, 0:64].rearrange("p (t e) -> p t e", t=T), rep(rb, T), ALU.add))
            for t in range(T):
                select_top(dve, lg[:, t, :], 4, m8[:, t, :], sel[:, t, :], tmpe, s1)
            vv(V.tensor_tensor(selsum, sel[:, 0, :], sel[:, 1, :], ALU.add))
            V.tensor_scalar(nm, m8[:, :, 0], -1.0, None, ALU.mult).then_inc(s_nm, 1)
            dve.wait_ge(s_nm, 1)
            V.tensor_copy(gs, nm).then_inc(s_sel, 1)
            dve.wait_ge(s_el, 2)
            vv(V.tensor_tensor(gate_of[:, :, 0:NE], gate_of[:, :, 0:NE], sel, ALU.mult))
            vv(V.tensor_reduce(gs, gate_of[:, :, 0:NE], X_AXIS, ALU.add))
            vv(V.reciprocal(gs, gs))
            vv(V.tensor_tensor(gate_of[:, :, 0:NE], gate_of[:, :, 0:NE], bcast(gs, NE), ALU.mult))
            dve.wait_ge(s_rk, 1)
            vv(dispatch_tables(dve, 1))

    def experts(name, x_tok, gu, down, halves, unroll, bias, acc_start):
        NC = 2 * halves + (2 if halves == 2 else 1)
        xgT, tg, tu, sg = ar(7168, KD, P), ar(8192, 512), ar(8704, 512), ar(9216, 512)
        y, yT, y2 = ar(9728, 4 * halves, P), ar(10752, 4 * halves, P), ar(11776, 2, 512)
        onehot, gated, GT = ar(12800, T, P), ar(13056, T, P), ar(13312, T, P)
        bias_t = ar(5120, 2, 1024)
        full = [sem(f"{name}_slot{s}_full") for s in range(SLOTS)]
        s_done = sem(f"{name}_chunk_multiplied")
        s_bias = sem(f"{name}_bias_loaded") if bias else None
        s_one = sem(f"{name}_onehot_ready")
        s_gat = sem(f"{name}_gated_ready")
        s_xg = sem(f"{name}_gathered")
        s_xgt = sem(f"{name}_gathered_taken")
        s_gfree = sem(f"{name}_gate_taken") if bias else None
        s_ufree = sem(f"{name}_up_taken") if bias else None
        s_g = sem(f"{name}_gate_clamped") if bias else None
        s_sig = sem(f"{name}_sigmoid_ready")
        s_y = sem(f"{name}_hidden_ready")
        s_yT = sem(f"{name}_hidden_transposed")
        s_yTt = sem(f"{name}_hidden_transposed_taken")
        s_GT = sem(f"{name}_gated_transposed")
        s_GTt = sem(f"{name}_gated_transposed_taken")
        s_y2 = sem(f"{name}_result_taken")
        s_v = sem(f"{name}_vector_order") if bias else None
        H = halves
        s_half = sem(f"{name}_first_result_half") if H == 1 else None

        def chunk_list(e):
            out_ = []
            for h in range(H):
                out_ += [gu(e, h, 0), gu(e, h, 1)]
            return out_ + down(e)

        def at_slot(u, c):
            return (u * NC + c) % SLOTS

        with nc.Block() as block:
            @block.sync
            def _(sp):
                for u in range(unroll):
                    for c, (src, k, w) in enumerate(chunk_list(u)):
                        sp.dma_start(slot(at_slot(u, c), k, w), src).then_inc(full[at_slot(u, c)], 16)
                if bias:
                    sp.dma_start(bias_t.rearrange("p a b -> p (a b)"), row_everywhere(bias(0))).then_inc(s_bias, 16)
                n = sp.value_load(passes[0:1, 0:1], min_val=1, max_val=2)

                def items(base, lo, hi):
                    with sp.Fori(lo // unroll, hi // unroll) as q:
                        e = q * unroll
                        for u in range(unroll):
                            for c, (src, k, w) in enumerate(chunk_list(e + u + unroll)):
                                s = at_slot(u, c)
                                sp.wait_ge(s_done, (e + u + base) * NC + c + 1)
                                sp.dma_start(slot(s, k, w), src).then_inc(full[s], 16)
                                if bias and c == 2 * H - 1:
                                    sp.wait_ge(s_ufree, (e + base) * H + H)
                                    sp.dma_start(bias_t.rearrange("p a b -> p (a b)"),
                                                 row_everywhere(bias(e + 1))).then_inc(s_bias, 16)
                items(0, 0, NE - unroll)
                with sp.If(n > 1):
                    for u in range(unroll):
                        for c, (src, k, w) in enumerate(chunk_list(u)):
                            sp.wait_ge(s_done, (NE - unroll + u) * NC + c + 1)
                            sp.dma_start(slot(at_slot(u, c), k, w), src).then_inc(full[at_slot(u, c)], 16)
                            if bias and c == 2 * H - 1:
                                sp.wait_ge(s_ufree, NE * H)
                                sp.dma_start(bias_t.rearrange("p a b -> p (a b)"), row_everywhere(bias(0))).then_inc(s_bias, 16)
                    items(NE, 0, NE - unroll)

            @block.tensor
            def _(pe):
                def gather(i):
                    pe.wait_ge(s_one, i + 1)
                    for b in range(2):
                        for k in range(4 * b, 4 * b + 4):
                            dst = ps[:, 6 + b, (k % 4) * P:(k % 4 + 1) * P]
                            for t in range(T):
                                last = M.matmul(dst, x_tok[:, t, k * P:(k + 1) * P], onehot[:, t, :],
                                                start=(t == 0), stop=(t == T - 1))
                        last.then_inc(s_xg, 1)

                acc_start(pe)
                gather(0)
                n = pe.value_load(passes[0:1, 0:1], min_val=1, max_val=2)
                with pe.Fori(0, n) as p:
                    with pe.Fori(0, NE // unroll) as q:
                        e0 = q * unroll
                        for u in range(unroll):
                            i = p * NE + e0 + u

                            def arrived(c):
                                s = at_slot(u, c)
                                if unroll == 1:
                                    pe.wait_ge(full[s], i * 16 + 16)
                                else:
                                    pe.wait_ge(full[s], p * (NE * 8) + e0 * 8 + 16)
                                return s
                            pe.wait_ge(s_xgt, i * 2 + 2)
                            for h in range(H):
                                for which in range(2):
                                    c = 2 * h + which
                                    w = slot(arrived(c))
                                    if h:
                                        pe.wait_ge(s_ufree if which else s_gfree, i * H + h)
                                    for k in range(KD):
                                        last = M.matmul(ps[:, 4 + which, :], xgT[:, k, :], w[:, k, :],
                                                        start=(k == 0), stop=(k == KD - 1))
                                    last.then_inc(s_done, 1)
                            gather(i + 1)
                            for h in range(H):
                                pe.wait_ge(s_y, i * H + h + 1)
                                pe.wait_ge(s_xgt, i * 2 + 3 + h)
                                for k in range(4):
                                    last = M.transpose(ps[:, 6 + h, k * P:(k + 1) * P], y[:, 4 * h + k, :], ident[:, :])
                                last.then_inc(s_yT, 1)
                            if bias:
                                pe.wait_ge(s_gfree, i * H + H)
                                pe.wait_ge(s_ufree, i * H + H)
                            pe.wait_ge(s_yTt, i * H + H)
                            KH = 4 * H
                            for d in range(2):
                                if H == 2:
                                    w = slot(arrived(2 * H + d))
                                    for k in range(KH):
                                        last = M.matmul(ps[:, 4 + d, :], yT[:, k, :], w[:, k, :],
                                                        start=(k == 0), stop=(k == KH - 1))
                                    last.then_inc(s_done, 1)
                                else:
                                    if d == 0:
                                        w = slot(arrived(2), 4, 1024)
                                    for k in range(KH):
                                        last = M.matmul(ps[:, 4 + d, :], yT[:, k, :], w[:, k, 512 * d:512 * d + 512],
                                                        start=(k == 0), stop=(k == KH - 1))
                                    last.then_inc(s_half if d == 0 else s_done, 1)
                                if d == 0:
                                    pe.wait_ge(s_gat, i + 1)
                                    for t in range(T):
                                        last = M.transpose(ps[:, 6, t * P:(t + 1) * P], gated[:, t, :], ident[:, :])
                                    last.then_inc(s_GT, 1)
                            pe.wait_ge(s_GTt, i + 1)
                            for d in range(2):
                                pe.wait_ge(s_y2, i * 2 + d + 1)
                                for t in range(T):
                                    M.matmul(ps[:, 2 * t + d, :], GT[:, t, :], y2[:, d, :], start=False, stop=False,
                                             skip_group_check=True)
                M.matmul(ps[:, 7, 0:P], ident[:, :], ident[:, :]).then_inc(s_GT, 1)

            @block.scalar
            def _(act):
                def take_gathered(i):
                    for b in range(2):
                        act.wait_ge(s_xg, i * 2 + b + 1)
                        A.activation(xgT[:, 4 * b:4 * b + 4, :], ps[:, 6 + b, :].rearrange("p (k m) -> p k m", k=4),
                                     ACT.Copy).then_inc(s_xgt, 1)
                take_gathered(0)
                n = act.value_load(passes[0:1, 0:1], min_val=1, max_val=2)
                with act.Fori(0, n) as p:
                    with act.Fori(0, NE // unroll) as q:
                        e0 = q * unroll
                        for u in range(unroll):
                            i = p * NE + e0 + u
                            for h in range(H):
                                if bias:
                                    act.wait_ge(s_g, i * H + h + 1)
                                    A.activation(sg, tg, ACT.Sigmoid, scale=1.702).then_inc(s_sig, 1)
                                else:
                                    act.wait_ge(s_done, i * NC + 1)
                                    A.activation(sg, ps[:, 4, :], ACT.Silu).then_inc(s_sig, 1)
                            take_gathered(i + 1)
                            for h in range(H):
                                act.wait_ge(s_yT, i * H + h + 1)
                                A.activation(yT[:, 4 * h:4 * h + 4, :], ps[:, 6 + h, :].rearrange("p (k m) -> p k m", k=4),
                                             ACT.Copy).then_inc(s_yTt, 1)
                            if H == 2:
                                act.wait_ge(s_done, i * NC + NC - 1)
                            else:
                                act.wait_ge(s_half, i + 1)
                            A.activation(y2[:, 0, :], ps[:, 4, :], ACT.Copy).then_inc(s_y2, 1)
                            act.wait_ge(s_GT, i + 1)
                            A.activation(GT, ps[:, 6, 0:2 * P].rearrange("p (t m) -> p t m", t=T), ACT.Copy).then_inc(s_GTt, 1)
                            act.wait_ge(s_done, i * NC + NC)
                            A.activation(y2[:, 1, :], ps[:, 5, :], ACT.Copy).then_inc(s_y2, 1)

            @block.vector
            def _(dve):
                def make_onehot(i):
                    for t in range(T):
                        ins = V.tensor_scalar(onehot[:, t, :], iota_row[:, :], slot_of[:, t, bass.ds(i, 1)], None, ALU.is_equal)
                    ins.then_inc(s_one, 1)
                make_onehot(0)
                n = dve.value_load(passes[0:1, 0:1], min_val=1, max_val=2)
                with dve.Fori(0, n) as p:
                    with dve.Fori(0, NE // unroll) as q:
                        e0 = q * unroll
                        for u in range(unroll):
                            i = p * NE + e0 + u
                            dve.wait_ge(s_done, i * NC + 1)
                            make_onehot(i + 1)
                            for t in range(T):
                                ins = V.tensor_scalar(gated[:, t, :], iota_row[:, :], slot_of[:, t, bass.ds(i, 1)],
                                                      gate_of[:, t, bass.ds(i, 1)], ALU.is_equal, ALU.mult)
                            ins.then_inc(s_gat, 1)
                            if bias:
                                dve.wait_ge(s_bias, i * 16 + 16)
                            for h in range(H):
                                yh = y[:, 4 * h:4 * h + 4, :].rearrange("p a b -> p (a b)")
                                if bias:
                                    if h:
                                        dve.wait_ge(s_y, i * H + h)
                                    V.tensor_tensor(tg, ps[:, 4, :], bias_t[:, 0, 512 * h:512 * h + 512], ALU.add).then_inc(s_gfree, 1)
                                    dve.wait_ge(s_gfree, i * H + h + 1)
                                    V.tensor_scalar(tg, tg, 7.0, None, ALU.min).then_inc(s_g, 1)
                                    dve.wait_ge(s_done, i * NC + 2 * h + 2)
                                    V.tensor_tensor(tu, ps[:, 5, :], bias_t[:, 1, 512 * h:512 * h + 512], ALU.add).then_inc(s_ufree, 1)
                                    dve.wait_ge(s_ufree, i * H + h + 1)
                                    V.tensor_scalar(tu, tu, 7.0, -7.0, ALU.min, ALU.max).then_inc(s_v, 1)
                                    dve.wait_ge(s_sig, i * H + h + 1)
                                    V.tensor_tensor(tg, tg, sg, ALU.mult).then_inc(s_v, 1)
                                    dve.wait_ge(s_v, i * 2 * H + 2 * h + 2)
                                    V.scalar_tensor_tensor(yh, tu, 1.0, tg, ALU.add, ALU.mult).then_inc(s_y, 1)
                                    if h + 1 < H:
                                        dve.wait_ge(s_done, i * NC + 2 * h + 3)
                                else:
                                    dve.wait_ge(s_sig, i + 1)
                                    dve.wait_ge(s_done, i * NC + 2)
                                    V.tensor_tensor(yh, ps[:, 5, :], sg, ALU.mult).then_inc(s_y, 1)

    bdn = ar(14336, D)
    gT = ar(15360, T * P)
    s_bdn = sem("down_bias_loaded")
    s_gT, s_gTt = sem("gates_transposed"), sem("gates_transposed_taken")
    with nc.Block() as block:
        @block.sync
        def _(sp):
            sp.dma_start(bdn[0:NE, :], a["moe_b_down"][0]).then_inc(s_bdn, 16)

        @block.tensor
        def _(pe):
            for t in range(T):
                last = M.transpose(ps[0:NE, 7, t * P:(t + 1) * P], gate_of[:, t, 0:NE], ident[:, :])
            last.then_inc(s_gT, 1)

        @block.scalar
        def _(act):
            act.wait_ge(s_gT, 1)
            A.activation(gT[0:NE, :], ps[0:NE, 7, 0:T * P], ACT.Copy).then_inc(s_gTt, 1)

    def start_acc(pe):
        pe.wait_ge(s_bdn, 16)
        pe.wait_ge(s_gTt, 1)
        for t in range(T):
            for d in range(2):
                M.matmul(ps[:, 2 * t + d, :], gT[0:NE, t * P:(t + 1) * P], bdn[0:NE, 512 * d:512 * d + 512],
                         start=True, stop=False, skip_group_check=True)

    def one(w, e):
        return w[e] if isinstance(e, int) else w[bass.ds(e, 1)].rearrange("o r c -> (o r) c")

    w_gu, w_dn, b_gu = a["moe_w_gu"][0], a["moe_w_down"][0], a["moe_b_gu"][0]
    experts("experts1", h2,
            lambda e, h, which: (cols(one(w_gu, e), 1024 * which + 512 * h), KD, 512),
            lambda e: [(cols(one(w_dn, e), 512 * d), KD, 512) for d in range(2)],
            2, 1, lambda e: b_gu[e] if isinstance(e, int) else b_gu[bass.ds(e, 1)].rearrange("o n -> (o n)"), start_acc)
    if dbg == "b7":
        s_o7 = sem("dbg")
        s_o7a = sem("dbga")
        with nc.Block() as block:
            @block.vector
            def _(dve):
                V.tensor_copy(ar(6144, T, D), banks(0, 4, T, D)).then_inc(s_o7a, 1)
            @block.sync
            def _(sp):
                sp.wait_ge(s_o7a, 1)
                sp.dma_start(out[0].rearrange("(t p) d -> p t d", p=P), ar(6144, T, D)).then_inc(s_o7, 16)
                sp.wait_ge(s_o7, 16)
        return

    recycle([s for s in made if s not in (c_v.sem, c_a.sem, c_g.sem)])

    class C2:
        Q, KC, VC, KS, VS, KW, VW, GATE, GQ, GK, GV, GA, GR, MA, MB, END = (
            0, 512, 640, 768, 896, 1024, 1152, 1280, 1304, 1560, 1816, 2328, 2344, 2856, 3880, 4904)

    ZW = C2.END
    z = ar(2048, T, ZW)
    uT = ar(11856, KD, T * P)
    un = ar(13904, T, D)
    fg, mg = ar(15952, D), ar(16976, D)
    acc_sb = ar(18000, T, D)
    rope_in = ar(20100, 3, 32)
    rope_k = ar(20200, 3, 32)
    trig = ar(25088, 2, 3, 32)
    inv = ar(20300, 32)
    posi = ar(20400, 4).bitcast(I32)
    posf = ar(20408, 4)
    ss3 = small[:, 230:232]

    rb2 = Ring("pre2")
    s_z = sem("projection_unit_ready")
    s_cmp = sem("compressed_hidden_ready")
    s_pa = sem("branch_projection_ready")
    s_po = sem("output_projection_ready")
    w2 = a["w_in_2"][0]
    NZ = -(-ZW // 512)
    for j in range(NZ):
        n = min(512, ZW - 512 * j)
        rb2.add(cols(w2, 512 * j, n), (KD, n), (s_z, 2 * j + 2))
    for i, kv in enumerate("kv"):
        rb2.add(a[f"cmp_w1_{kv}_2"][0].rearrange("(j p) n -> p j n", p=P), (16, 256), (s_cmp, i + 1))
    for i, nm_ in enumerate(("w_proj_nsa_2", "w_proj_gla_2")):
        rb2.add(a[nm_][0].rearrange("(k p) n -> p k n", p=P), (4, 1024), (s_pa, i + 1))
    for i in range(2):
        rb2.add(cols(a["w_out_2"][0], 512 * i), (KD, 512), (s_po, i + 1))

    s_p8 = sem("block8_parameters_loaded")
    s_pos = sem("positions_loaded")
    s_pz = sem("positions_cleared")
    s_inv = sem("frequencies_ready")
    s_fs = sem("norm_squares_ready")
    s_fr = sem("norm_roots_ready")
    s_un = sem("normed_again_ready")
    s_uT = sem("normed_again_transposed")
    s_uTt = sem("normed_again_transposed_taken")
    s_zt2 = sem("projection_unit_taken")
    s_ang = sem("angles_reduced")

    TWO_PI = 2.0 * math.pi
    PI_C1 = 6.28125
    PI_C2 = math.floor((TWO_PI - PI_C1) * 2.0 ** 22) / 2.0 ** 22
    PI_C3 = TWO_PI - PI_C1 - PI_C2
    ROUND = 1.5 * 2.0 ** 23
    PI_F = 3.1415925

    s_xr = sem("residual2_added")
    with nc.Block() as block:
        @block.sync
        def _(sp):
            rb2.load(sp, 1)
            sp.dma_start(fg, row_everywhere(a["final_g"])).then_inc(s_p8, 16)
            sp.dma_start(mg, row_everywhere(a["g_mix_2"][0])).then_inc(s_p8, 16)
            pos = a["positions_2"][0]
            sp.wait_ge(s_pz, 1)
            sp.dma_start(posi[:, 0:2], pos.rearrange("(t p) -> p t", p=P), allow_slow_non_contiguous=True).then_inc(s_pos, 16)
            for q in range(4):
                sp.dma_start(posi[32 * q:32 * q + 15, 2:3], pos[31:256:16].rearrange("(p o) -> p o", o=1), allow_slow_non_contiguous=True).then_inc(s_pos, 16)
            rb2.load(sp, NZ + SLOTS)

        @block.gpsimd
        def _(pool):
            G.memset(posi[:, :], 0).then_inc(s_pz, 1)
            for i in range(32):
                last = G.memset(inv[:, i:i + 1], 10000.0 ** (-i / 32.0))
            last.then_inc(s_inv, 1)

        @block.tensor
        def _(pe):
            for t in range(T):
                pe.wait_ge(s_un, t + 1)
                for k in range(KD):
                    last = M.transpose(ps[:, 4 + 2 * t + k // 4, (k % 4) * P:(k % 4 + 1) * P],
                                       un[:, t, k * P:(k + 1) * P], ident[:, :])
                last.then_inc(s_uT, 1)
            pe.wait_ge(s_uTt, 4)
            for j in range(NZ):
                w = rb2.take(pe)
                n = min(512, ZW - 512 * j)
                for t in range(T):
                    u = 2 * j + t
                    if u >= 8:
                        pe.wait_ge(s_zt2, u - 7)
                    for k in range(KD):
                        last = M.matmul(ps[:, u % 8, 0:n], uT[:, k, t * P:(t + 1) * P], w[:, k, :],
                                        start=(k == 0), stop=(k == KD - 1))
                    last.then_inc(s_z, 1)

        @block.scalar
        def _(act):
            for rnd in range(2):
                for t in range(T):
                    act.wait_ge(s_xr, 2 * rnd + t + 1)
                    A.activation(un[:, t, :], x_res[:, t, :], ACT.Square, accum_out=ss3[:, t:t + 1]).then_inc(s_fs, 1)
                act.wait_ge(s_fs, 2 * rnd + 2)
                A.activation(ss3, ss3, ACT.Sqrt, bias=eps_t, scale=1.0 / D).then_inc(s_fr, 1)
            for t in range(T):
                act.wait_ge(s_uT, t + 1)
                for k2 in range(2):
                    A.activation(uT[:, 4 * k2:4 * k2 + 4, t * P:(t + 1) * P],
                                 ps[:, 4 + 2 * t + k2, :].rearrange("p (k m) -> p k m", k=4), ACT.Copy).then_inc(s_uTt, 1)
            for j in range(NZ):
                n = min(512, ZW - 512 * j)
                for t in range(T):
                    act.wait_ge(s_z, 2 * j + t + 1)
                    A.activation(z[:, t, 512 * j:512 * j + n], ps[:, (2 * j + t) % 8, 0:n], ACT.Copy).then_inc(s_zt2, 1)
            act.wait_ge(s_ang, 1)
            A.activation(trig.rearrange("p a b c -> p (a b c)"), trig.rearrange("p a b c -> p (a b c)"), ACT.Sin)

        @block.vector
        def _(dve):
            dve.wait_ge(s_p8, 32)
            g2m = mods[:, 3, :]
            for t in range(T):
                vv(V.tensor_tensor(acc_sb[:, t, :], banks(2 * t, 2, 1024), g2m, ALU.mult))
                V.tensor_tensor(x_res[:, t, :], x_res[:, t, :], acc_sb[:, t, :], ALU.add).then_inc(s_xr, 1)
            for rnd in range(2):
                dve.wait_ge(s_fr, rnd + 1)
                vv(V.reciprocal(ss3, ss3))
                for t in range(T):
                    if rnd == 0:
                        V.scalar_tensor_tensor(x_res[:, t, :], x_res[:, t, :], ss3[:, t:t + 1], fg, ALU.mult, ALU.mult).then_inc(s_xr, 1)
                    else:
                        V.scalar_tensor_tensor(un[:, t, :], x_res[:, t, :], ss3[:, t:t + 1], mg, ALU.mult, ALU.mult).then_inc(s_un, 1)
            dve.wait_ge(s_pos, 80)
            dve.wait_ge(s_inv, 1)
            vv(V.tensor_copy(posf[:, 0:3], posi[:, 0:3]))
            for c in range(3):
                vv(V.tensor_scalar(rope_in[:, c, :], inv, posf[:, c:c + 1], None, ALU.mult))
            flat = lambda v: v.rearrange("p a b -> p (a b)")
            ri, rk, cosv, sinv = flat(rope_in), flat(rope_k), flat(trig[:, 0, :, :]), flat(trig[:, 1, :, :])
            vv(V.tensor_scalar(rk, ri, 1.0 / TWO_PI, ROUND, ALU.mult, ALU.add))
            vv(V.tensor_scalar(rk, rk, ROUND, None, ALU.subtract))
            for part in (PI_C1, PI_C2, PI_C3):
                vv(V.scalar_tensor_tensor(ri, rk, -part, ri, ALU.mult, ALU.add))
            vv(V.tensor_scalar(sinv, ri, PI_F, -PI_F, ALU.min, ALU.max))
            vv(V.tensor_scalar(cosv, ri, math.pi / 2, None, ALU.add))
            vv(V.tensor_scalar(rk, cosv, PI_F, -TWO_PI, ALU.is_gt, ALU.mult))
            vv(V.tensor_tensor(cosv, cosv, rk, ALU.add))
            V.tensor_scalar(cosv, cosv, PI_F, -PI_F, ALU.min, ALU.max).then_inc(s_ang, 1)

    NH, NG, DH, NCB = 8, 2, 64, 15
    B = 11856
    qT2, kT2, cT2 = ar(B, 4, T * P), ar(B + 1024, 4, T * P), ar(B + 2048, 4, T * P)
    Fc = ar(B + 3072, 2, 16, P)
    S = ar(B + 3072, 2048)
    PT = ar(B + 5120, 2048)
    o_nsa = ar(B + 7168, T, 512)
    o_gla = ar(B + 8192, T, 512)
    rt = ar(B + 9216, 4, 256)
    hid = ar(B + 9216, 2, 256)
    hidT = ar(B + 9728, 4, P)
    b1 = ar(B + 10240, 2, 256)
    w2c = ar(B + 10752, 2, 2, DH)
    b2c = ar(B + 11008, 2, DH)
    kv_c = ar(B + 11136, 2, DH)
    kcT = ar(B + 11264, P)
    posT = ar(B + 11392, 32)
    pos_rows = ar(B + 11424, P)
    cmp_ok = ar(B + 11552, 2, T, DH)
    cmp_neg = ar(B + 11808, 2, T, DH)
    caus = ar(B + 12064, P)
    kdup = ar(B + 12192, P)
    kd = ar(B + 7168, T, 8, P)
    sg_nsa = ar(B + 12320, T, 24)
    rmax, rsum = ar(B + 12368, NH), ar(B + 12376, NH)
    assert B + 12384 <= 25088

    s_p9 = sem("nsa_parameters_loaded")
    s_m9 = sem("nsa_masks_ready")
    s_rp = sem("roped")
    s_dup = sem("doubled")
    s_t9 = sem("nsa_transposed")
    s_t9t = sem("nsa_transposed_taken")
    s_pT = sem("block_positions_transposed")
    s_F = sem("block_inputs_ready")
    s_hb = sem("compressed_hidden_biased")
    s_hg = sem("compressed_hidden_activated")
    s_hT = sem("compressed_hidden_transposed")
    s_hTt2 = sem("compressed_hidden_transposed_taken")
    s_kc = sem("compressed_ready")
    s_kct = sem("compressed_taken")
    s_kcT = sem("compressed_keys_transposed")
    s_kcTt = sem("compressed_keys_transposed_taken")
    s_sc = sem("scores_ready")
    s_sm9 = sem("scores_shifted")
    s_ex = sem("scores_exponentiated")
    s_pr = sem("probabilities_ready")
    s_ptr = sem("probabilities_transposed")
    s_ptt = sem("probabilities_transposed_taken")
    s_ov = sem("attention_part_ready")
    s_ovt = sem("attention_part_taken")
    s_sg9 = sem("branch_gates_ready")

    UNITS = [(t, br) for t in range(T) for br in range(3)]

    def head_of(s):
        return 2 * (s % 4) + s // 4

    def score_at(s, Lk):
        return s * Lk if Lk >= P else (s // 4) * 512 + (s % 4) * Lk

    def parts_of(t, br):
        return 2 if (br and t) else 1

    with nc.Block() as block:
        @block.sync
        def _(sp):
            for i, kv in enumerate("kv"):
                sp.dma_start(pos_rows[16 * i:16 * i + 16, :], a[f"cmp_pos_{kv}_2"][0].rearrange("(j i) d -> j (i d)", i=2)).then_inc(s_p9, 16)
                sp.dma_start(b1[:, i, :], row_everywhere(a[f"cmp_b1_{kv}_2"][0])).then_inc(s_p9, 16)
                sp.dma_start(w2c[:, i, :, :], a[f"cmp_w2_{kv}_2"][0].rearrange("(k p) n -> p k n", p=P)).then_inc(s_p9, 16)
                sp.dma_start(b2c[:, i, :], row_everywhere(a[f"cmp_b2_{kv}_2"][0])).then_inc(s_p9, 16)
            rb2.load(sp, 99)

        @block.gpsimd
        def _(pool):
            gg(G.memset(Fc.rearrange("p a b c -> p (a b c)"), 0.0))
            gg(G.memset(caus, 0.0))
            gg(G.affine_select(out=caus, in_=caus, compare_op=ALU.is_ge, fill=-BIG, base=0,
                               pattern=[[-1, P]], channel_multiplier=1))
            gg(G.memset(cmp_ok.rearrange("p a b c -> p (a b c)"), 0.0))
            for g in range(NG):
                for t in range(T):
                    own = cmp_ok[:, g, t, 32 * g:32 * g + NCB]
                    gg(G.memset(own, 1.0))
                    gg(G.affine_select(out=own, in_=own, compare_op=ALU.is_ge, fill=0.0, base=P * t - 31,
                                       pattern=[[-16, NCB]], channel_multiplier=1))
            f = lambda v: v.rearrange("p a b c -> p (a b c)")
            G.tensor_scalar(f(cmp_neg), f(cmp_ok), BIG, -BIG, ALU.mult, ALU.add).then_inc(s_m9, 1)

        @block.tensor
        def _(pe):
            pe.wait_ge(s_p9, 128)
            M.transpose(ps[:, 6, 0:32], pos_rows[0:32, :], ident[0:32, 0:32]).then_inc(s_pT, 1)
            pe.wait_ge(s_dup, 2)
            for g in range(NG):
                for kv in range(2):
                    for t in range(T):
                        last = M.transpose(ps[:, 4 + kv, (2 * g + t) * P:(2 * g + t + 1) * P],
                                           kd[:, t, 2 * kv + g, :], ident[:, :])
            last.then_inc(s_t9, 1)
            pe.wait_ge(s_dup, 6)
            for hp in range(4):
                for t in range(T):
                    M.transpose(ps[:, hp // 2, (hp % 2) * 256 + t * P:(hp % 2) * 256 + (t + 1) * P],
                                z[:, t, P * hp:P * hp + P], ident[:, :])
            for br in range(2):
                for g in range(NG):
                    for t in range(T):
                        last = M.transpose(ps[:, 2 + br, 256 * g + t * P:256 * g + (t + 1) * P],
                                           kd[:, t, 4 + 2 * br + g, :], ident[:, :])
            last.then_inc(s_t9, 1)
            pe.wait_ge(s_F, 1)
            for kv in range(2):
                w = rb2.take(pe)
                for j in range(16):
                    last = M.matmul(ps[:, 6 + kv, 0:256], Fc[:, kv, j, :], w[:, j, :], start=(j == 0), stop=(j == 15))
                last.then_inc(s_cmp, 1)
            pe.wait_ge(s_hg, 1)
            pe.wait_ge(s_t9t, 2)
            for kv in range(2):
                for k in range(2):
                    last = M.transpose(ps[:, 5, (2 * kv + k) * P:(2 * kv + k + 1) * P], hid[:, kv, k * P:(k + 1) * P], ident[:, :])
            last.then_inc(s_hT, 1)
            pe.wait_ge(s_hTt2, 1)
            for kv in range(2):
                for k in range(2):
                    last = M.matmul(ps[:, 6, DH * kv:DH * kv + DH], hidT[:, 2 * kv + k, :], w2c[:, kv, k, :],
                                    start=(k == 0), stop=(k == 1))
            last.then_inc(s_kc, 1)
            pe.wait_ge(s_kct, 1)
            M.transpose(ps[:, 5, 0:P], kdup, ident[:, :]).then_inc(s_kcT, 1)
            pe.wait_ge(s_kcTt, 1)
            pe.wait_ge(s_t9t, 4)
            np_ = 0
            for n, (t, br) in enumerate(UNITS):
                if n:
                    pe.wait_ge(s_sm9, 2 * n - 1)
                Lk = DH if br == 0 else P * (t + 1)
                for s in range(NH):
                    h = head_of(s)
                    b, g = DH * (h % 2), h // 4
                    q = qT2[b:b + DH, h // 2, t * P:(t + 1) * P]
                    keys = kcT[b:b + DH, 0:DH] if br == 0 else kT2[b:b + DH, 2 * (br - 1) + g, 0:Lk]
                    at = score_at(s, Lk)
                    last = M.matmul(ps[:, at // 512, at % 512:at % 512 + Lk], q, keys)
                last.then_inc(s_sc, 1)
                pe.wait_ge(s_pr, n + 1)
                for part in range(parts_of(t, br)):
                    if np_:
                        pe.wait_ge(s_ptt, np_)
                    places = range(NH) if parts_of(t, br) == 1 else range(4 * part, 4 * part + 4)
                    Sv = S[:, 0:NH * Lk]
                    if br == 0:
                        for hp in range(4):
                            last = M.transpose(ps[:, 4, hp * P:(hp + 1) * P], Sv[:, hp * P:(hp + 1) * P], ident[:, :])
                    else:
                        for i, s in enumerate(places):
                            for kt in range(t + 1):
                                at = (i * (t + 1) + kt) * P
                                last = M.transpose(ps[:, 4 + at // 512, at % 512:at % 512 + P],
                                                   Sv[:, s * Lk + kt * P:s * Lk + (kt + 1) * P], ident[:, :])
                    last.then_inc(s_ptr, 1)
                    np_ += 1
                    pe.wait_ge(s_ptt, np_)
                    if part == 0 and n:
                        pe.wait_ge(s_ovt, n)
                    for i, s in enumerate(places):
                        b, g = DH * (s % 2), head_of(s) // 4
                        dst = ps[:, 6 + s % 2, DH * (s // 2):DH * (s // 2) + DH]
                        if br == 0:
                            last = M.matmul(dst, PT[b:b + DH, (s // 2) * P:(s // 2 + 1) * P], kv_c[b:b + DH, 1, :])
                        else:
                            c0 = C2.VS + 256 * (br - 1) + DH * g
                            for kt in range(t + 1):
                                at = (i * (t + 1) + kt) * P
                                last = M.matmul(dst, PT[:, at:at + P], z[:, kt, c0:c0 + DH],
                                                start=(kt == 0), stop=(kt == t))
                last.then_inc(s_ov, 1)

        @block.scalar
        def _(act):
            aa(A.activation(posT, ones[:, 0:32], ACT.Copy))
            act.wait_ge(s_pT, 1)
            A.activation(posT, ps[:, 6, 0:32], ACT.Copy).then_inc(s_t9t, 1)
            act.wait_ge(s_t9, 1)
            A.activation(cT2, banks(4, 2, 4, 256), ACT.Copy).then_inc(s_t9t, 1)
            A.activation(sg_nsa, z[:, :, C2.GATE:C2.GATE + 24], ACT.Sigmoid).then_inc(s_sg9, 1)
            act.wait_ge(s_t9, 2)
            A.activation(qT2, banks(0, 2, 4, 256), ACT.Copy).then_inc(s_t9t, 1)
            A.activation(kT2, banks(2, 2, 4, 256), ACT.Copy).then_inc(s_t9t, 1)
            act.wait_ge(s_hb, 1)
            A.activation(hid, hid, ACT.Gelu_apprx_tanh).then_inc(s_hg, 1)
            act.wait_ge(s_hT, 1)
            A.activation(hidT, ps[:, 5, :].rearrange("p (k m) -> p k m", k=4), ACT.Copy).then_inc(s_hTt2, 1)
            act.wait_ge(s_kcT, 1)
            A.activation(kcT, ps[:, 5, 0:P], ACT.Copy).then_inc(s_kcTt, 1)
            np_ = 0
            for n, (t, br) in enumerate(UNITS):
                Lk = DH if br == 0 else P * (t + 1)
                act.wait_ge(s_sm9, 2 * n + 2)
                A.activation(S[:, 0:NH * Lk], S[:, 0:NH * Lk], ACT.Exp, scale=DH ** -0.5).then_inc(s_ex, 1)
                for part in range(parts_of(t, br)):
                    act.wait_ge(s_ptr, np_ + 1)
                    if np_ and part == 0:
                        act.wait_ge(s_ov, n)
                    w = 512 if br == 0 else 1024
                    A.activation(PT[:, 0 + 0:w], ps[:, 4:6, :].rearrange("p a b -> p (a b)")[:, 0:w], ACT.Copy).then_inc(s_ptt, 1)
                    np_ += 1

        @block.vector
        def _(dve):
            def rope_heads(v, c, s):
                nh = v.shape[1]
                x1, x2 = v[:, :, 0:32], v[:, :, 32:64]
                cc, sn = rep(c, nh), rep(s, nh)
                t_ = [rt[:, i, 0:nh * 32].rearrange("p (h d) -> p h d", d=32) for i in range(4)]
                vv(V.tensor_tensor(t_[0], x1, cc, ALU.mult))
                vv(V.tensor_tensor(t_[1], x2, sn, ALU.mult))
                vv(V.tensor_tensor(t_[2], x2, cc, ALU.mult))
                vv(V.tensor_tensor(t_[3], x1, sn, ALU.mult))
                vv(V.tensor_tensor(x1, t_[0], t_[1], ALU.subtract))
                return V.tensor_tensor(x2, t_[2], t_[3], ALU.add)

            def doubled(dst, src):
                return V.tensor_copy(dst.rearrange("p n (a d) -> p n a d", a=2),
                                     src.unsqueeze(2).to_broadcast([P, src.shape[1], 2, DH]))

            for t in range(T):
                doubled(kd[:, t, 0:4, :], z[:, t, C2.KC:C2.KC + 256].rearrange("p (n d) -> p n d", d=DH)).then_inc(s_dup, 1)
            dve.wait_ge(s_m9, 1)
            dve.wait_ge(s_t9t, 2)
            for kv in range(2):
                for g in range(NG):
                    for i in range(2):
                        rows = slice(DH * i, DH * i + DH)
                        tokens = cT2[rows, 2 * kv + g, :].rearrange("p (m j i) -> p m j i", j=8, i=2)
                        for jh in range(2):
                            dst = Fc[rows, kv, 8 * jh:8 * jh + 8, 32 * g:32 * g + NCB].rearrange("p j n -> p n j")
                            pos_ = rep(posT[rows, 16 * kv + 8 * jh:16 * kv + 8 * jh + 8], NCB)
                            vv(V.tensor_tensor(dst, tokens[:, jh:jh + NCB, :, i], pos_, ALU.add))
            V.tensor_copy(Fc[:, :, :, DH:P], Fc[:, :, :, 0:DH]).then_inc(s_F, 1)
            for t in range(T):
                for c0, nh in ((C2.Q, NH), (C2.KS, NG), (C2.KW, NG)):
                    rope_heads(z[:, t, c0:c0 + nh * DH].rearrange("p (h d) -> p h d", d=DH),
                               trig[:, 0, t, :], trig[:, 1, t, :]).then_inc(s_rp, 1)
                    dve.wait_ge(s_rp, 3 * t + {C2.Q: 1, C2.KS: 2, C2.KW: 3}[c0])
                for br in range(2):
                    c0 = C2.KS + 256 * br
                    doubled(kd[:, t, 4 + 2 * br:6 + 2 * br, :],
                            z[:, t, c0:c0 + P].rearrange("p (n d) -> p n d", d=DH)).then_inc(s_dup, 1)
            dve.wait_ge(s_cmp, 2)
            dve.wait_ge(s_p9, 128)
            V.tensor_tensor(hid, ps[:, 6:8, 0:256], b1, ALU.add).then_inc(s_hb, 1)
            dve.wait_ge(s_kc, 1)
            vv(V.tensor_tensor(kv_c, ps[:, 6, 0:P].rearrange("p (a b) -> p a b", a=2), b2c, ALU.add))
            vv(rope_heads(kv_c[:, 0:1, :], trig[:, 0, 2, :], trig[:, 1, 2, :]))
            doubled(kdup.unsqueeze(1), kv_c[:, 0:1, :]).then_inc(s_kct, 1)
            dve.wait_ge(s_sg9, 1)
            for n, (t, br) in enumerate(UNITS):
                Lk = DH if br == 0 else P * (t + 1)
                sv = S[:, 0:NH * Lk].rearrange("p (h k) -> p h k", h=NH)
                if br == 0:
                    sc = ps[:, 0:2, 0:4 * DH].rearrange("p a (g o k) -> p a g o k", g=NG, k=DH)
                    sg4 = S[:, 0:NH * DH].rearrange("p (a g o k) -> p a g o k", a=2, g=NG, k=DH)
                else:
                    sc = ps[:, 0:4, :].rearrange("p a b -> p (a b)")[:, 0:NH * Lk].rearrange("p (h k) -> p h k", h=NH)
                dve.wait_ge(s_sc, n + 1)
                if n:
                    dve.wait_ge(s_ov, n)
                if br == 0:
                    for g in range(NG):
                        for par in range(2):
                            ins = V.tensor_tensor(sg4[:, par, g, :, :], sc[:, par, g, :, :], rep(cmp_neg[:, g, t, :], 2), ALU.add)
                            if (g, par) != (1, 1):
                                vv(ins)
                else:
                    if t:
                        vv(V.tensor_copy(sv[:, :, 0:P], sc[:, :, 0:P]))
                    ins = V.tensor_tensor(sv[:, :, Lk - P:Lk], sc[:, :, Lk - P:Lk], rep(caus, NH), ALU.add)
                ins.then_inc(s_sm9, 1)
                dve.wait_ge(s_sm9, 2 * n + 1)
                vv(V.tensor_reduce(rmax, sv, X_AXIS, ALU.max))
                V.tensor_tensor(sv, sv, bcast(rmax, Lk), ALU.subtract).then_inc(s_sm9, 1)
                dve.wait_ge(s_ex, n + 1)
                vv(V.tensor_reduce(rsum, sv, X_AXIS, ALU.add))
                vv(V.reciprocal(rsum, rsum))
                gate = sg_nsa[:, t, :].rearrange("p (i a b) -> p a i b", a=2, b=3)[:, :, :, br]
                vv(V.tensor_tensor(rsum.rearrange("p (a i) -> p a i", a=2), rsum.rearrange("p (a i) -> p a i", a=2), gate, ALU.mult))
                if br == 0:
                    for g in range(NG):
                        for par in range(2):
                            v_ = sg4[:, par, g, :, :]
                            vv(V.tensor_tensor(v_, v_, rep(cmp_ok[:, g, t, :], 2), ALU.mult))
                V.tensor_tensor(sv, sv, bcast(rsum, Lk), ALU.mult).then_inc(s_pr, 1)
                dve.wait_ge(s_ov, n + 1)
                for par in range(2):
                    dst = o_nsa[:, t, :].rearrange("p (g r o d) -> p r o g d", g=2, r=2, o=2)[:, par]
                    src = ps[:, 6 + par, 0:4 * DH].rearrange("p (o g d) -> p o g d", o=2, g=2)
                    ins = V.tensor_copy(dst, src) if br == 0 else V.tensor_tensor(dst, dst, src, ALU.add)
                    if par == 0:
                        vv(ins)
                ins.then_inc(s_ovt, 1)
                dve.wait_ge(s_ovt, n + 1)

    if dbg == "b9":
        s_o9 = sem("dbg")
        with nc.Block() as block:
            @block.sync
            def _(sp):
                sp.dma_start(out[0].rearrange("(t p) d -> p t d", p=P)[:, :, 0:512], o_nsa).then_inc(s_o9, 16)
                sp.wait_ge(s_o9, 16)
        return

    LH, LK, LV, LR, SUB = 4, 64, 128, 16, 16
    NSUB = T * P // SUB
    lq, lk, la = ar(B, 2, T * P), ar(B + 512, 2, T * P), ar(B + 1024, T * P)
    bT = ar(B + 1280, 2, T * P)
    bex = ar(B + 1792, 2, T * P)
    absx = ar(B + 2304, 2, T * P)
    refs = ar(B + 2816, 2, NSUB)
    NBUF = 4
    kt_buf = [ar(B + 2848 + 512 * i, 2, T * P) for i in range(NBUF)]
    negcap = ar(B + 4896, 512)
    wa2 = ar(B + 5408, 256)
    ba = ar(B + 5664, 2)
    lrows = ar(B + 5666, P)
    ST = ar(B + 9216, LH, 384)
    one_row = ar(B + 11776, T * P)
    lng = ar(B + 10752, LH * LV)
    osq2 = ar(B + 11264, 512)
    lss = small[:, 236:240]
    silu_r = ar(B + 5794, 1024).rearrange("p (t n) -> p t n", t=T)

    s_p10 = sem("gla_parameters_loaded")
    s_cap = sem("exponent_caps_ready")
    s_lt = sem("gla_transposed")
    s_ltt = sem("gla_transposed_taken")
    s_la = sem("log_decay_logits")
    s_lab = sem("log_decay_steps")
    s_lae = sem("log_decay_exponentials")
    s_lb = sem("query_exponents_ready")
    s_lbe = sem("query_decays_ready")
    s_lqd = sem("decayed_queries_ready")
    s_ke = sem("key_exponents_ready")
    s_kee = sem("key_decays_ready")
    s_kd = sem("decayed_keys_ready")
    s_ls = sem("gla_scores_ready")
    s_lm2 = sem("gla_scores_masked")
    s_lo = sem("gla_outputs_ready")
    s_lr = sem("gla_gate_ready")
    s_lsq = sem("gla_squares_summed")
    s_lrt = sem("gla_roots_ready")

    def span(i):
        return P * (i // (P // SUB) + 1)

    with nc.Block() as block:
        @block.sync
        def _(sp):
            sp.dma_start(wa2[0:LR, :], a["gla_w_a2_2"][0]).then_inc(s_p10, 16)
            sp.dma_start(lrows[0:2, :], a["gla_b_a_2"][0].rearrange("(h p) -> h p", p=P)).then_inc(s_p10, 16)
            sp.dma_start(lng, row_everywhere(a["gla_norm_g_2"][0])).then_inc(s_p10, 16)

        @block.gpsimd
        def _(pool):
            G.memset(negcap[:, 0:256], -80.0).then_inc(s_cap, 1)
            G.memset(negcap[:, 256:512], 1e4).then_inc(s_cap, 1)
            for i in range(NSUB):
                L = span(i)
                pool.wait_ge(s_kee, i + 1)
                kt = kt_buf[i % NBUF]
                G.tensor_tensor(kt[:, :, 0:L], kt[:, :, 0:L], lk[:, :, 0:L], ALU.mult).then_inc(s_kd, 1)

        @block.tensor
        def _(pe):
            pe.wait_ge(s_p10, 48)
            M.transpose(ps[:, 3, 0:2], lrows[0:2, :], ident[0:2, 0:2])
            for t in range(T):
                M.transpose(ps[0:LR, 2, t * P:(t + 1) * P], z[:, t, C2.GA:C2.GA + LR], ident[:, :])
                for hp in range(2):
                    M.transpose(ps[:, 0, 256 * hp + t * P:256 * hp + (t + 1) * P], z[:, t, C2.GQ + P * hp:C2.GQ + P * hp + P], ident[:, :])
                    last = M.transpose(ps[:, 1, 256 * hp + t * P:256 * hp + (t + 1) * P], z[:, t, C2.GK + P * hp:C2.GK + P * hp + P], ident[:, :])
            last.then_inc(s_lt, 1)
            pe.wait_ge(s_ltt, 2)
            for hp in range(2):
                last = M.matmul(ps[:, 7, 256 * hp:256 * hp + 256], wa2[0:LR, P * hp:P * hp + P], la[0:LR, :])
            last.then_inc(s_la, 1)
            pe.wait_ge(s_ltt, 4)
            pe.wait_ge(s_lqd, 1)
            for i in range(NSUB):
                pe.wait_ge(s_kd, i + 1)
                kt = kt_buf[i % NBUF]
                for h in range(LH):
                    b, hp = LK * (h % 2), h // 2
                    for st in range(span(i) // P):
                        if st == 0:
                            dst = ps[:, 4 + h % 2, 256 * hp + SUB * i:256 * hp + SUB * i + SUB]
                        else:
                            dst = ps[:, 2 + h % 2, P * hp + SUB * i - P:P * hp + SUB * i - P + SUB]
                        last = M.matmul(dst, kt[b:b + LK, hp, st * P:(st + 1) * P], bex[b:b + LK, hp, SUB * i:SUB * i + SUB])
                last.then_inc(s_ls, 1)
            pe.wait_ge(s_lm2, 1)
            for t in range(T):
                for h in range(LH):
                    for st in range(t + 1):
                        lhsT = ST[:, h, t * P:(t + 1) * P] if st == 0 else ST[:, h, 256:384]
                        last = M.matmul(ps[:, t, LV * h:LV * h + LV], lhsT, z[:, st, C2.GV + LV * h:C2.GV + LV * h + LV],
                                        start=(st == 0), stop=(st == t))
                last.then_inc(s_lo, 1)

        @block.scalar
        def _(act):
            act.wait_ge(s_lt, 1)
            A.activation(la[0:LR, :], ps[0:LR, 2, 0:T * P], ACT.Copy).then_inc(s_ltt, 1)
            A.activation(ba, ps[:, 3, 0:2], ACT.Copy).then_inc(s_ltt, 1)
            A.activation(lq, ps[:, 0, :].rearrange("p (h n) -> p h n", h=2), ACT.Copy).then_inc(s_ltt, 1)
            A.activation(lk, ps[:, 1, :].rearrange("p (h n) -> p h n", h=2), ACT.Copy).then_inc(s_ltt, 1)
            act.wait_ge(s_lab, 1)
            aa(A.activation(absx, absx, ACT.Exp))
            A.activation(absx, absx, ACT.Ln, bias=1.0).then_inc(s_lae, 1)
            act.wait_ge(s_lb, 1)
            A.activation(bex, bex, ACT.Exp).then_inc(s_lbe, 1)
            for i in range(NSUB):
                L = span(i)
                act.wait_ge(s_ke, i + 1)
                kt = kt_buf[i % NBUF]
                A.activation(kt[:, :, 0:L], kt[:, :, 0:L], ACT.Exp, scale=-1.0).then_inc(s_kee, 1)
            A.activation(silu_r, z[:, :, C2.GR:C2.GR + 512], ACT.Silu).then_inc(s_lr, 1)
            A.activation(z[:, :, C2.MA:C2.END], z[:, :, C2.MA:C2.END], ACT.Sigmoid).then_inc(s_lr, 1)
            for t in range(T):
                act.wait_ge(s_lsq, t + 1)
                A.activation(lss, lss, ACT.Sqrt, bias=eps_t, scale=1.0 / LV).then_inc(s_lrt, 1)

        @block.vector
        def _(dve):
            dve.wait_ge(s_la, 1)
            dve.wait_ge(s_ltt, 2)
            for hp in range(2):
                vv(V.tensor_scalar(bT[:, hp, :], ps[:, 7, 256 * hp:256 * hp + 256], ba[:, hp:hp + 1], None, ALU.add))
            V.scalar_tensor_tensor(absx, bT, -1.0, bT, ALU.mult, ALU.min).then_inc(s_lab, 1)
            vv(V.tensor_scalar(bT, bT, 0.0, None, ALU.min))
            dve.wait_ge(s_lae, 1)
            vv(V.tensor_tensor(bT, bT, absx, ALU.subtract))
            vv(V.tensor_scalar(bT, bT, 1.0 / 16.0, None, ALU.mult))
            vv(V.memset(one_row, 1.0))
            for hp in range(2):
                vv(V.tensor_tensor_scan(absx[:, hp, :], one_row, bT[:, hp, :], 0.0, ALU.mult, ALU.add))
            b_ = absx
            vv(V.memset(refs[:, :, 0:1], 0.0))
            vv(V.tensor_copy(refs[:, :, 1:NSUB], b_[:, :, SUB - 1:T * P - 1:SUB]))
            for hp in range(2):
                ins = V.tensor_tensor(bex[:, hp, :].rearrange("p (n s) -> p n s", s=SUB),
                                      b_[:, hp, :].rearrange("p (n s) -> p n s", s=SUB), bcast(refs[:, hp, :], SUB), ALU.subtract)
                if hp == 0:
                    vv(ins)
            ins.then_inc(s_lb, 1)
            dve.wait_ge(s_lbe, 1)
            dve.wait_ge(s_ltt, 3)
            V.scalar_tensor_tensor(bex, bex, LK ** -0.5, lq, ALU.mult, ALU.mult).then_inc(s_lqd, 1)
            dve.wait_ge(s_cap, 2)
            for i in range(NSUB):
                L = span(i)
                if i >= NBUF:
                    dve.wait_ge(s_ls, i - NBUF + 1)
                kt = kt_buf[i % NBUF]
                for hp in range(2):
                    at = 256 - SUB * (i + 1)
                    ins = V.scalar_tensor_tensor(kt[:, hp, 0:L], b_[:, hp, 0:L], refs[:, hp, i:i + 1], negcap[:, at:at + L],
                                                 ALU.subtract, ALU.max)
                ins.then_inc(s_ke, 1)
            dve.wait_ge(s_ls, NSUB)
            for h in range(LH):
                b0 = 256 * (h // 2)
                vv(V.tensor_tensor(ST[:, h, 0:P], ps[:, 4 + h % 2, b0:b0 + P], tri_le[:, :], ALU.mult))
                vv(V.tensor_copy(ST[:, h, P:2 * P], ps[:, 4 + h % 2, b0 + P:b0 + 2 * P]))
                ins = V.tensor_tensor(ST[:, h, 2 * P:3 * P], ps[:, 2 + h % 2, P * (h // 2):P * (h // 2) + P], tri_le[:, :], ALU.mult)
                if h < LH - 1:
                    vv(ins)
            ins.then_inc(s_lm2, 1)
            dve.wait_ge(s_lr, 2)
            dve.wait_ge(s_p10, 48)
            for t in range(T):
                o = o_gla[:, t, :]
                dve.wait_ge(s_lo, t + 1)
                vv(V.tensor_copy(o, ps[:, t, :]))
                vv(V.tensor_tensor(osq2, o, o, ALU.mult))
                V.tensor_reduce(lss, osq2.rearrange("p (h v) -> p h v", h=LH), X_AXIS, ALU.add).then_inc(s_lsq, 1)
                dve.wait_ge(s_lrt, t + 1)
                vv(V.reciprocal(lss, lss))
                oh = o.rearrange("p (h v) -> p h v", h=LH)
                vv(V.tensor_tensor(oh, oh, bcast(lss, LV), ALU.mult))
                vv(V.tensor_tensor(o, o, lng, ALU.mult))
                vv(V.tensor_tensor(o, o, silu_r[:, t, :], ALU.mult))

    if dbg == "b10":
        s_o10 = sem("dbg")
        with nc.Block() as block:
            @block.sync
            def _(sp):
                sp.dma_start(out[0].rearrange("(t p) d -> p t d", p=P)[:, :, 0:512], o_gla).then_inc(s_o10, 16)
                sp.wait_ge(s_o10, 16)
        return

    oT = ar(B, 8, T * P)
    mx = ar(B + 2048, T, D)
    mT = ar(B + 4096, KD, T * P)
    h2b = ar(2048, T, D)
    h2bT = ar(B, KD, T * P)
    rw2 = ar(B + 6144, KD, 36)
    rb2_ = ar(B + 6432, 36)
    fgn = ar(B + 9216, D)
    lg2 = small[:, 388:460].rearrange("p (t e) -> p t e", t=T)
    lg8 = small[:, 256:272].rearrange("p (t e) -> p t e", t=T)
    gsel = small[:, 272:288].rearrange("p (t e) -> p t e", t=T)
    gexp = small[:, 288:296].rearrange("p (t e) -> p t e", t=T)
    gm8 = small[:, 296:312].rearrange("p (t e) -> p t e", t=T)
    gsum = small[:, 312:314]
    gneg = small[:, 314:316]
    lgm = small[:, 316:380].rearrange("p (t e) -> p t e", t=T)
    gexpm = small[:, 380:388].rearrange("p (t e) -> p t e", t=T)

    s_p11 = sem("router2_parameters_loaded")
    s_oT = sem("branches_transposed")
    s_oTt = sem("branches_transposed_taken")
    s_mxr = sem("mixed2_ready")
    s_mxT = sem("mixed2_transposed")
    s_mxTt = sem("mixed2_transposed_taken")
    s_r11 = sem("residual3_added")
    s_q11 = sem("norm3_squares")
    s_n11 = sem("norm3_ready")
    s_nT = sem("norm3_transposed")
    s_nTt = sem("norm3_transposed_taken")
    s_l11 = sem("router2_logits_ready")
    s_g11 = sem("group_max_ready")
    s_e11 = sem("group_exponentials")
    s_m11 = sem("expert_max_ready")
    s_e12 = sem("expert_exponentials")
    s_s11 = sem("selection2_ready")
    s_k11 = sem("ranks2_ready")

    with nc.Block() as block:
        @block.sync
        def _(sp):
            sp.dma_start(rw2[:, :, 0:4], a["w_grp_2"][0].rearrange("(k p) e -> p k e", p=P)).then_inc(s_p11, 16)
            sp.dma_start(rw2[:, :, 4:36], a["w_exp_2"][0].rearrange("(k p) e -> p k e", p=P)).then_inc(s_p11, 16)
            sp.dma_start(rb2_[:, 0:4], row_everywhere(a["b_grp_2"][0])).then_inc(s_p11, 16)
            sp.dma_start(rb2_[:, 4:36], row_everywhere(a["b_exp_2"][0])).then_inc(s_p11, 16)
            sp.dma_start(fgn, row_everywhere(a["g_ffn_2"][0])).then_inc(s_p11, 16)

        @block.tensor
        def _(pe):
            for i, o in enumerate((o_nsa, o_gla)):
                for t in range(T):
                    for k in range(4):
                        last = M.transpose(ps[:, 2 * i + k // 2, (k % 2) * 256 + t * P:(k % 2) * 256 + (t + 1) * P],
                                           o[:, t, k * P:(k + 1) * P], ident[:, :])
                last.then_inc(s_oT, 1)
            pe.wait_ge(s_oTt, 2)
            for i in range(2):
                w = rb2.take(pe)
                for t in range(T):
                    for n in range(2):
                        for k in range(4):
                            last = M.matmul(ps[:, 4 * i + 2 * t + n, :], oT[:, 4 * i + k, t * P:(t + 1) * P],
                                            w[:, k, 512 * n:512 * n + 512], start=(k == 0), stop=(k == 3))
                last.then_inc(s_pa, 1)
            for t in range(T):
                pe.wait_ge(s_mxr, t + 1)
                for k in range(KD):
                    last = M.transpose(ps[:, 2 * t + k // 4, (k % 4) * P:(k % 4 + 1) * P], mx[:, t, k * P:(k + 1) * P], ident[:, :])
                last.then_inc(s_mxT, 1)
            pe.wait_ge(s_mxTt, 2)
            for n in range(2):
                w = rb2.take(pe)
                for t in range(T):
                    for k in range(KD):
                        last = M.matmul(ps[:, 4 + 2 * t + n, :], mT[:, k, t * P:(t + 1) * P], w[:, k, :],
                                        start=(k == 0), stop=(k == KD - 1))
                last.then_inc(s_po, 1)
            for t in range(T):
                pe.wait_ge(s_n11, t + 1)
                for k in range(KD):
                    last = M.transpose(ps[:, 2 * t + k // 4, (k % 4) * P:(k % 4 + 1) * P], h2b[:, t, k * P:(k + 1) * P], ident[:, :])
                last.then_inc(s_nT, 1)
            pe.wait_ge(s_nTt, 2)
            pe.wait_ge(s_p11, 80)
            for t in range(T):
                for k in range(KD):
                    last = M.matmul(ps[:, 4, 36 * t:36 * t + 36], h2bT[:, k, t * P:(t + 1) * P], rw2[:, k, :],
                                    start=(k == 0), stop=(k == KD - 1))
            last.then_inc(s_l11, 1)
            pe.wait_ge(s_s11, 1)
            rank_matmuls(5).then_inc(s_k11, 1)

        @block.scalar
        def _(act):
            for i in range(2):
                act.wait_ge(s_oT, i + 1)
                A.activation(oT[:, 4 * i:4 * i + 4, :], banks(2 * i, 2, 4, 256), ACT.Copy).then_inc(s_oTt, 1)
            for t in range(T):
                act.wait_ge(s_mxT, t + 1)
                A.activation(mT[:, :, t * P:(t + 1) * P], banks(2 * t, 2, KD, P), ACT.Copy).then_inc(s_mxTt, 1)
            for t in range(T):
                act.wait_ge(s_r11, t + 1)
                A.activation(mx[:, t, :], x_res[:, t, :], ACT.Square, accum_out=ss3[:, t:t + 1]).then_inc(s_q11, 1)
            act.wait_ge(s_q11, 2)
            A.activation(ss3, ss3, ACT.Sqrt, bias=eps_t, scale=1.0 / D).then_inc(s_q11, 1)
            for t in range(T):
                act.wait_ge(s_nT, t + 1)
                A.activation(h2bT[:, :, t * P:(t + 1) * P], banks(2 * t, 2, KD, P), ACT.Copy).then_inc(s_nTt, 1)
            act.wait_ge(s_g11, 1)
            for t in range(T):
                A.activation(gexp[:, t, :], lg2[:, t, 0:4], ACT.Exp, bias=gneg[:, t:t + 1]).then_inc(s_e11, 1)
            act.wait_ge(s_m11, 1)
            for t in range(T):
                A.activation(gate_of[:, t, 0:NE], lgm[:, t, :], ACT.Exp, bias=nm[:, t:t + 1]).then_inc(s_e12, 1)

        @block.vector
        def _(dve):
            dve.wait_ge(s_pa, 2)
            for t in range(T):
                vv(V.tensor_tensor(mx[:, t, :], banks(2 * t, 2, D), z[:, t, C2.MA:C2.MB], ALU.mult))
                zb = z[:, t, C2.MB:C2.END]
                vv(V.tensor_tensor(zb, banks(4 + 2 * t, 2, D), zb, ALU.mult))
                V.tensor_tensor(mx[:, t, :], mx[:, t, :], zb, ALU.add).then_inc(s_mxr, 1)
            dve.wait_ge(s_po, 2)
            for t in range(T):
                V.tensor_tensor(x_res[:, t, :], x_res[:, t, :], banks(4 + 2 * t, 2, D), ALU.add).then_inc(s_r11, 1)
            dve.wait_ge(s_q11, 3)
            vv(V.reciprocal(ss3, ss3))
            dve.wait_ge(s_p11, 80)
            for t in range(T):
                V.scalar_tensor_tensor(h2b[:, t, :], x_res[:, t, :], ss3[:, t:t + 1], fgn, ALU.mult, ALU.mult).then_inc(s_n11, 1)
            dve.wait_ge(s_l11, 1)
            vv(V.tensor_tensor(lg2, ps[:, 4, 0:72].rearrange("p (t e) -> p t e", t=T), rep(rb2_, T), ALU.add))
            vv(V.memset(lg8, -BIG))
            vv(V.tensor_copy(lg8[:, :, 0:4], lg2[:, :, 0:4]))
            for t in range(T):
                select_top(dve, lg8[:, t, :], 1, gm8[:, t, :], gsel[:, t, :], tmpe[:, 0:8], s1)
            V.tensor_scalar(gneg, gm8[:, :, 0], -1.0, None, ALU.mult).then_inc(s_g11, 1)
            for t in range(T):
                vv(V.tensor_scalar(gexpm[:, t, :], gsel[:, t, 0:4], BIG, -BIG, ALU.mult, ALU.add))
                vv(V.tensor_tensor(lgm[:, t, :].rearrange("p (g e) -> p g e", g=4),
                                   lg2[:, t, 4:36].rearrange("p (g e) -> p g e", g=4), bcast(gexpm[:, t, :], 8), ALU.add))
                select_top(dve, lgm[:, t, :], 2, m8[:, t, :], sel[:, t, :], tmpe, s1)
            vv(V.tensor_tensor(selsum, sel[:, 0, :], sel[:, 1, :], ALU.add))
            V.tensor_scalar(nm, m8[:, :, 0], -1.0, None, ALU.mult).then_inc(s_m11, 1)
            dve.wait_ge(s_m11, 1)
            V.tensor_copy(gs, nm).then_inc(s_s11, 1)
            dve.wait_ge(s_e11, 2)
            vv(V.tensor_reduce(gsum, gexp, X_AXIS, ALU.add))
            dve.wait_ge(s_e12, 2)
            vv(V.tensor_tensor(gate_of[:, :, 0:NE], gate_of[:, :, 0:NE], sel, ALU.mult))
            vv(V.tensor_reduce(gs, gate_of[:, :, 0:NE], X_AXIS, ALU.add))
            vv(V.tensor_tensor(gs, gs, gsum, ALU.mult))
            vv(V.reciprocal(gs, gs))
            vv(V.tensor_tensor(gate_of[:, :, 0:NE], gate_of[:, :, 0:NE], bcast(gs, NE), ALU.mult))
            dve.wait_ge(s_k11, 1)
            vv(dispatch_tables(dve, 5))

    zero = ar(14336, P)
    s_zero = sem("zero_ready")

    def start_zero(pe):
        pe.wait_ge(s_zero, 1)
        for b in range(4):
            M.matmul(ps[:, b, :], zero, h2b[:, 0, 0:512], start=True, stop=False, skip_group_check=True)

    with nc.Block() as block:
        @block.gpsimd
        def _(pool):
            G.memset(zero, 0.0).then_inc(s_zero, 1)

    w_gt, w_up, w_d2 = a["w_gate_2"][0], a["w_up_2"][0], a["w_down_2"][0]
    experts("experts2", h2b,
            lambda e, h, which: (one(w_up if which else w_gt, e).rearrange("(k p) n -> p k n", p=P), KD, 512),
            lambda e: [(one(w_d2, e).rearrange("(k p) n -> p k n", p=P), 4, 1024)],
            1, 2, None, start_zero)

    gfin = ar(5120, D)
    fin = ar(6144, T, D)
    s_p13 = sem("final_weight_loaded")
    s_r13 = sem("last_residual_added")
    s_q13 = sem("last_squares")
    s_f13 = sem("result_ready")
    s_out = sem("result_stored")
    with nc.Block() as block:
        @block.sync
        def _(sp):
            sp.dma_start(gfin, row_everywhere(a["g_final_2"])).then_inc(s_p13, 16)
            sp.wait_ge(s_f13, 2)
            sp.dma_start(out[0].rearrange("(t p) d -> p t d", p=P), fin).then_inc(s_out, 16)
            sp.wait_ge(s_out, 16)

        @block.scalar
        def _(act):
            for t in range(T):
                act.wait_ge(s_r13, t + 1)
                A.activation(fin[:, t, :], x_res[:, t, :], ACT.Square, accum_out=ss3[:, t:t + 1]).then_inc(s_q13, 1)
            act.wait_ge(s_q13, 2)
            A.activation(ss3, ss3, ACT.Sqrt, bias=eps_t, scale=1.0 / D).then_inc(s_q13, 1)

        @block.vector
        def _(dve):
            for t in range(T):
                V.tensor_tensor(x_res[:, t, :], x_res[:, t, :], banks(2 * t, 2, D), ALU.add).then_inc(s_r13, 1)
            dve.wait_ge(s_q13, 3)
            vv(V.reciprocal(ss3, ss3))
            dve.wait_ge(s_p13, 16)
            for t in range(T):
                V.scalar_tensor_tensor(fin[:, t, :], x_res[:, t, :], ss3[:, t:t + 1], gfin, ALU.mult, ALU.mult).then_inc(s_f13, 1)


def kernel(**inputs):
    import numpy as np
    import concourse.bacc as bacc
    from concourse.bass_utils import run_bass_kernel_spmd

    nc = bacc.Bacc("TRN2", target_bir_lowering=False, num_devices=1)
    arrays, args = {}, {}
    for name in inputs:
        value = np.ascontiguousarray(inputs[name])
        arrays[f"in_{name}"] = value
        args[name] = nc.dram_tensor(f"in_{name}", value.shape, mybir.dt.from_np(value.dtype), kind="ExternalInput").ap()
    out = nc.dram_tensor("out", (1, T * P, D), F32, kind="ExternalOutput").ap()
    program(nc, args, out)
    got = run_bass_kernel_spmd(nc, [arrays], core_ids=[0])
    return got.results[0]["out"]
```

```python
import concourse.bass as bass
from concourse import mybir
from contextlib import ExitStack
import math

F32 = mybir.dt.float32
I32 = mybir.dt.int32
ALU = mybir.AluOpType
ACT = mybir.ActivationFunctionType
X_AXIS = mybir.AxisListType.X

P = 128
D = 1024
T = 2
KD = D // P
EPS = 1e-6
BIG = 1e30
SLOTS = 6
SLOT = 4096
NE = 32
CAP = 64


class Chain:

    def __init__(self, eng, sem):
        self.eng, self.sem, self.n = eng, sem, 0

    def __call__(self, ins):
        ins.then_inc(self.sem, 1)
        self.n += 1
        self.eng.wait_ge(self.sem, self.n)
        return ins


GH, SH, SP_ = 8, 16, 64
C_GZ, C_BA, C_SZ, C_XBC, C_DT = 3072, 4096, 4112, 5136, 6672


def program(nc, a, out):
    V, A, G, M = nc.vector, nc.scalar, nc.gpsimd, nc.tensor
    ctx = ExitStack()

    def sb(name, shape, dt=F32):
        return ctx.enter_context(nc.sbuf_tensor(name, shape, dt))

    made, cleared = [], []

    def sem(name):
        if cleared:
            return cleared.pop(0)
        made.append(ctx.enter_context(nc.semaphore(name)))
        return made[-1]

    def recycle(sems):
        with nc.Block() as block:
            @block.sync
            def _(sp):
                for s in sems[0::3]:
                    sp.sem_clear(s)

            @block.gpsimd
            def _(pool):
                for s in sems[1::3]:
                    pool.sem_clear(s)

            @block.scalar
            def _(act):
                for s in sems[2::3]:
                    act.sem_clear(s)
        cleared.extend(sems)

    ring = sb("ring", [P, SLOTS, SLOT])
    ident = sb("ident", [P, P])
    tri_le = sb("tri_le", [P, P])
    tri_lt = sb("tri_lt", [P, P])
    ones = sb("ones", [P, P])
    small = sb("small", [P, 512])
    NL = 7
    masks = sb("masks", [P, NL + 3, P])
    neg_u = masks[:, NL, :]
    pos_l = masks[:, NL + 1, :]
    gng = masks[:, NL + 2, :]
    arena = sb("arena", [P, 25600])
    ps = ctx.enter_context(nc.psum_tensor("ps", [P, 8, 512], F32))

    def ar(at, *dims):
        n = math.prod(dims)
        assert at + n <= 25600, (at, dims)
        v = arena[:, at:at + n]
        if len(dims) == 1:
            return v
        names = "abcd"[:len(dims)]
        pat = f"p ({' '.join(names)}) -> p {' '.join(names)}"
        return v.rearrange(pat, **dict(zip(names, dims)))

    def banks(b, n, *dims):
        v = ps[:, b:b + n, :].rearrange("p a b -> p (a b)")
        names = "abcd"[:len(dims)]
        return v.rearrange(f"p ({' '.join(names)}) -> p {' '.join(names)}", **dict(zip(names, dims)))

    x_res = ar(0, T, D)
    mix = ar(2048, T, 2 * D)

    c_v, c_a, c_g = Chain(V, sem("vector_order")), Chain(A, sem("scalar_order")), Chain(G, sem("gpsimd_order"))

    def vv(ins):
        return c_v(ins)

    def aa(ins):
        return c_a(ins)

    def gg(ins):
        return c_g(ins)

    def bcast(ap, n):
        return ap.unsqueeze(len(ap.shape)).to_broadcast(list(ap.shape) + [n])

    def rep(ap, n):
        return ap.unsqueeze(1).to_broadcast([ap.shape[0], n] + list(ap.shape[1:]))

    def row_everywhere(ap):
        return ap.partition_broadcast(P)

    eps_t, eps128_t = small[:, 510:511], small[:, 511:512]

    def cols(w, c0, n=512):
        return w[:, c0:c0 + n].rearrange("(k p) n -> p k n", p=P)

    def slot(s, k=KD, n=512):
        v = ring[:, s, 0:k * n]
        return v.rearrange("p (k n) -> p k n", k=k)

    class Ring:

        def __init__(self, name):
            self.full = [sem(f"{name}_slot{s}_full") for s in range(SLOTS)]
            self.chunks, self.sent, self.used = [], 0, 0

        def add(self, src, shape, released):
            self.chunks.append((src, shape, released))

        def load(self, sp, upto):
            while self.sent < min(upto, len(self.chunks)):
                n = self.sent
                src, (k, w), _ = self.chunks[n]
                if n >= SLOTS:
                    sp.wait_ge(*self.chunks[n - SLOTS][2])
                sp.dma_start(slot(n % SLOTS, k, w), src).then_inc(self.full[n % SLOTS], 16)
                self.sent += 1

        def take(self, pe):
            n = self.used
            pe.wait_ge(self.full[n % SLOTS], 16 * (n // SLOTS + 1))
            self.used += 1
            _, (k, w), _ = self.chunks[n]
            return slot(n % SLOTS, k, w)

    w_in, ada_w = a["w_in"][0], a["ada_w"][0]
    ra = Ring("pre1")
    s_ada = sem("ada_chunk_multiplied")
    s_unit = sem("ssd_projection_ready")
    s_gunit = sem("gdn_projection_ready")
    for j in range(4):
        ra.add(cols(ada_w, 512 * j), (KD, 512), (s_ada, j + 1))
    for j in range(3):
        ra.add(cols(w_in, C_XBC + 512 * j), (KD, 512), (s_unit, 4 * j + 4))
    for j in range(2):
        ra.add(cols(w_in, C_SZ + 512 * j), (KD, 512), (s_unit, 12 + 2 * j + 2))
    for j in range(6):
        ra.add(cols(w_in, 512 * j), (KD, 512), (s_gunit, 4 * j + 4))
    for j in range(2):
        ra.add(cols(w_in, C_GZ + 512 * j), (KD, 512), (s_gunit, 24 + 2 * j + 2))
    for j in range(4, 12):
        ra.add(cols(ada_w, 512 * j), (KD, 512), (s_ada, j + 1))
    s_wout = sem("w_out_chunk_multiplied")
    for n in range(2):
        for k in range(2):
            ra.add(a["w_out"][0][1024 * k:1024 * k + 1024, 512 * n:512 * n + 512]
                   .rearrange("(k p) n -> p k n", p=P), (KD, 512), (s_wout, 2 * n + k + 1))

    hT = ar(12288, KD, T * P)
    xbcT = ar(14336, 12, T * P)
    convw = sb("convw", [P, 36 * 4 + 12 + 8])
    heads = small[:, 0:64]
    wsm = ar(6144, KD, 32)
    rowsA, rowsB = ar(17408, P), ar(17536, P)
    cb = ar(18432, KD, 32)
    mod_part = ar(18688, 512)
    abias = ar(19456, 2 * D)
    n1g = ar(21504, D)
    modA, modB = ar(22528, D), ar(23552, D)
    hn = ar(2048, T, D)
    ss = small[:, 64:66]
    rstd = small[:, 66:68]

    s_const = sem("constants_ready")
    s_rows = sem("parameter_rows_loaded")
    s_small = sem("small_parameters_loaded")
    s_x = sem("x_loaded")
    s_rowsT = sem("parameter_rows_transposed")
    s_cb = sem("condition_ready")
    s_cz = sem("condition_columns_cleared")
    s_part = sem("modulation_sums_taken")
    s_comb = sem("modulation_chunk_ready")
    s_ss = sem("squares_summed")
    s_h = sem("normed_ready")
    s_hT = sem("normed_transposed")
    s_hTt = sem("normed_transposed_taken")

    def modulation_sums(pe, cond, bank):
        w = ra.take(pe)
        for r in range(2):
            for g in range(4):
                last = M.matmul(ps[32 * g:32 * g + 32, bank, :], cond[:, 2 * g + r, :], w[:, 2 * g + r, :],
                                start=(r == 0), stop=(r == 1))
        last.then_inc(s_ada, 1)

    with nc.Block() as block:
        @block.sync
        def _(sp):
            sp.dma_start(rowsA[0:96, :], a["gdn_conv_w"][0].rearrange("k (c p) -> (k c) p", p=P)).then_inc(s_rows, 16)
            sp.dma_start(rowsB[0:48, :], a["ssd_conv_w"][0].rearrange("k (c p) -> (k c) p", p=P)).then_inc(s_rows, 16)
            sp.dma_start(rowsB[48:60, :], a["ssd_conv_b"][0].rearrange("(c p) -> c p", p=P)).then_inc(s_rows, 16)
            sp.dma_start(rowsB[60:68, :], a["c"][0].rearrange("(c p) -> c p", p=P)).then_inc(s_rows, 16)
            sp.dma_start(x_res, a["x"][0].rearrange("(t p) d -> p t d", p=P)).then_inc(s_x, 16)
            ra.load(sp, 2)
            at = 0
            for name, n in (("gdn_dt_bias", 8), ("ssd_dt_bias", 16), ("gdn_a_log", 8), ("ssd_a_log", 16), ("ssd_d", 16)):
                sp.dma_start(heads[:, at:at + n], row_everywhere(a[name][0])).then_inc(s_small, 16)
                at += n
            sp.dma_start(abias, row_everywhere(a["ada_b"][0][0:2 * D])).then_inc(s_small, 16)
            sp.dma_start(n1g, row_everywhere(a["norm1_g"][0])).then_inc(s_small, 16)
            sp.dma_start(wsm[:, :, 0:16], cols(w_in, C_BA, 16)).then_inc(s_small, 16)
            sp.dma_start(wsm[:, :, 16:32], cols(w_in, C_DT, 16)).then_inc(s_small, 16)
            ra.load(sp, 4 + SLOTS)

        @block.gpsimd
        def _(pool):
            gg(G.memset(ident[:, :], 0.0))
            G.memset(cb, 0.0).then_inc(s_cz, 1)
            gg(G.memset(tri_le[:, :], 1.0))
            gg(G.memset(tri_lt[:, :], 1.0))
            gg(G.memset(ones[:, :], 1.0))
            gg(G.memset(eps_t, EPS))
            gg(G.memset(eps128_t, EPS * P))
            gg(G.affine_select(out=ident[:, :], in_=ident[:, :], compare_op=ALU.not_equal, fill=1.0,
                               base=0, pattern=[[-1, P]], channel_multiplier=1))
            gg(G.affine_select(out=tri_le[:, :], in_=tri_le[:, :], compare_op=ALU.is_ge, fill=0.0,
                               base=0, pattern=[[1, P]], channel_multiplier=-1))
            G.affine_select(out=tri_lt[:, :], in_=tri_lt[:, :], compare_op=ALU.is_gt, fill=0.0,
                            base=0, pattern=[[1, P]], channel_multiplier=-1).then_inc(s_const, 1)

        @block.tensor
        def _(pe):
            pe.wait_ge(s_const, 1)
            pe.wait_ge(s_rows, 64)
            M.transpose(ps[:, 7, 0:96], rowsA[0:96, :], ident[0:96, 0:96])
            M.transpose(ps[:, 7, 96:164], rowsB[0:68, :], ident[0:68, 0:68]).then_inc(s_rowsT, 1)
            pe.wait_ge(s_cb, 1)
            for j in range(4):
                modulation_sums(pe, cb, 4 + j % 2)
                pe.wait_ge(s_part, j + 1)
                M.matmul(ps[:, j, :], ones[:, :], mod_part).then_inc(s_comb, 1)
            for t in range(T):
                pe.wait_ge(s_h, t + 1)
                for k in range(KD):
                    last = M.transpose(ps[:, 4 + 2 * t + k // 4, (k % 4) * P:(k % 4 + 1) * P],
                                       hn[:, t, k * P:(k + 1) * P], ident[:, :])
                last.then_inc(s_hT, 1)

        @block.scalar
        def _(act):
            act.wait_ge(s_rowsT, 1)
            aa(A.activation(convw[:, :], ps[:, 7, 0:164], ACT.Copy))
            aa(A.activation(convw[:, 156:164], convw[:, 156:164], ACT.Silu))
            act.wait_ge(s_cz, 1)
            A.activation(cb[:, :, 0], convw[:, 156:164], ACT.Copy).then_inc(s_cb, 1)
            act.wait_ge(s_x, 16)
            for t in range(T):
                A.activation(hn[:, t, :], x_res[:, t, :], ACT.Square, accum_out=ss[:, t:t + 1]).then_inc(s_ss, 1)
            act.wait_ge(s_ss, 2)
            A.activation(rstd, ss, ACT.Sqrt, bias=eps_t, scale=1.0 / D).then_inc(s_ss, 1)
            for j in range(4):
                act.wait_ge(s_ada, j + 1)
                if j:
                    act.wait_ge(s_comb, j)
                A.activation(mod_part, ps[:, 4 + j % 2, :], ACT.Copy).then_inc(s_part, 1)
            for t in range(T):
                act.wait_ge(s_hT, t + 1)
                for k2 in range(2):
                    A.activation(hT[:, 4 * k2:4 * k2 + 4, t * P:(t + 1) * P],
                                 ps[:, 4 + 2 * t + k2, :].rearrange("p (k m) -> p k m", k=4), ACT.Copy).then_inc(s_hTt, 1)

        @block.vector
        def _(dve):
            dve.wait_ge(s_ss, 3)
            vv(V.reciprocal(rstd, rstd))
            dve.wait_ge(s_x, 16)
            for t in range(T):
                vv(V.tensor_scalar(hn[:, t, :], x_res[:, t, :], rstd[:, t:t + 1], None, ALU.mult))
            dve.wait_ge(s_small, 16 * 9)
            dve.wait_ge(s_comb, 4)
            vv(V.tensor_tensor(modB, banks(0, 2, 1024), abias[:, 0:D], ALU.add))
            vv(V.tensor_tensor(modA, banks(2, 2, 1024), abias[:, D:2 * D], ALU.add))
            vv(V.scalar_tensor_tensor(modA, modA, 1.0, n1g, ALU.add, ALU.mult))
            for t in range(T):
                vv(V.tensor_tensor(hn[:, t, :], hn[:, t, :], modA, ALU.mult))
                V.tensor_tensor(hn[:, t, :], hn[:, t, :], modB, ALU.add).then_inc(s_h, 1)

    sm = small[:, 96:160].rearrange("p (t c) -> p t c", t=T)
    soft = small[:, 160:208].rearrange("p (t c) -> p t c", t=T)
    dec = small[:, 208:256].rearrange("p (t c) -> p t c", t=T)
    beta = small[:, 256:272].rearrange("p (t c) -> p t c", t=T)
    negA = small[:, 272:296]
    tmp24 = small[:, 296:344].rearrange("p (t c) -> p t c", t=T)
    s_conv = sem("ssd_unit_taken")
    s_act = sem("ssd_convolved")
    s_zt = sem("ssd_gate_taken")
    s_sm = sem("narrow_taken")
    s_sp = sem("softplus_steps")

    def conv(dve, n, nbanks, dst, tap0, bias0, ready, taken, taps):
        for u in range(n):
            dve.wait_ge(ready, u + 1)
            src = ps[:, u % nbanks, 0:T * P]
            w = [convw[:, tap0 + k * taps + u:tap0 + k * taps + u + 1] for k in range(4)]
            if bias0 is None:
                vv(V.tensor_scalar(dst(u), src, w[3], None, ALU.mult))
            else:
                vv(V.tensor_scalar(dst(u), src, w[3], convw[:, bias0 + u:bias0 + u + 1], ALU.mult, ALU.add))
            for s in (1, 2, 3):
                ins = V.scalar_tensor_tensor(dst(u)[:, s:T * P], src[:, 0:T * P - s], w[3 - s], dst(u)[:, s:T * P],
                                             ALU.mult, ALU.add)
                if s < 3:
                    vv(ins)
                else:
                    ins.then_inc(taken, 1)

    with nc.Block() as block:
        @block.sync
        def _(sp):
            ra.load(sp, 9 + SLOTS)

        @block.gpsimd
        def _(pool):
            gg(G.memset(masks[:, 0:NL + 1, :], 0.0))
            gg(G.memset(pos_l, 0.0))
            for lv in range(NL):
                b = 1 << lv
                m = masks[:, lv, :].rearrange("p (n j) -> p n j", j=2 * b)
                gg(G.memset(m[:, :, 0:b], 1.0))
                gg(G.affine_select(out=m, in_=m, compare_op=ALU.is_ge, fill=0.0, base=-b,
                                   pattern=[[-2 * b, P // (2 * b)], [0, 2 * b]], channel_multiplier=1))
                gg(G.affine_select(out=m, in_=m, compare_op=ALU.is_ge, fill=0.0, base=2 * b - 1,
                                   pattern=[[2 * b, P // (2 * b)], [0, 2 * b]], channel_multiplier=-1))
            gg(G.affine_select(out=neg_u, in_=neg_u, compare_op=ALU.is_ge, fill=-BIG, base=0,
                               pattern=[[1, P]], channel_multiplier=-1))
            G.affine_select(out=pos_l, in_=pos_l, compare_op=ALU.is_gt, fill=BIG, base=0,
                            pattern=[[-1, P]], channel_multiplier=1)

        @block.tensor
        def _(pe):
            for j in range(3):
                w = ra.take(pe)
                for c in range(4):
                    u = 4 * j + c
                    if u >= 8:
                        pe.wait_ge(s_conv, u - 7)
                    for k in range(KD):
                        last = M.matmul(ps[:, u % 8, 0:T * P], w[:, k, c * P:(c + 1) * P], hT[:, k, :],
                                        start=(k == 0), stop=(k == KD - 1))
                    last.then_inc(s_unit, 1)
            for n in range(2):
                w = ra.take(pe)
                for t in range(T):
                    u = 12 + 2 * n + t
                    pe.wait_ge(s_conv, u - 7)
                    for k in range(KD):
                        last = M.matmul(ps[:, u % 8, :], hT[:, k, t * P:(t + 1) * P], w[:, k, :],
                                        start=(k == 0), stop=(k == KD - 1))
                    last.then_inc(s_unit, 1)
            for t in range(T):
                u = 16 + t
                pe.wait_ge(s_conv, u - 7)
                for k in range(KD):
                    last = M.matmul(ps[:, u % 8, 0:32], hT[:, k, t * P:(t + 1) * P], wsm[:, k, :],
                                    start=(k == 0), stop=(k == KD - 1))
                last.then_inc(s_unit, 1)

        @block.scalar
        def _(act):
            for u in range(12):
                act.wait_ge(s_conv, u + 1)
                A.activation(xbcT[:, u, :], xbcT[:, u, :], ACT.Silu).then_inc(s_act, 1)
            for u in range(12, 16):
                act.wait_ge(s_unit, u + 1)
                n, t = divmod(u - 12, 2)
                A.activation(mix[:, t, D + 512 * n:D + 512 * n + 512], ps[:, u % 8, :], ACT.Silu).then_inc(s_zt, 1)
            act.wait_ge(s_sm, 3)
            aa(A.activation(beta, sm[:, :, 0:8], ACT.Sigmoid))
            aa(A.activation(tmp24, tmp24, ACT.Exp))
            aa(A.activation(negA, heads[:, 24:48], ACT.Exp))
            A.activation(tmp24, tmp24, ACT.Ln, bias=1.0).then_inc(s_sp, 1)

        @block.vector
        def _(dve):
            conv(dve, 12, 8, lambda u: xbcT[:, u, :], 96, 144, s_unit, s_conv, 12)
            dve.wait_ge(s_unit, 18)
            for t in range(T):
                V.tensor_copy(sm[:, t, :], ps[:, t, 0:32]).then_inc(s_sm, 1)
            dve.wait_ge(s_sm, 2)
            vv(V.tensor_tensor(soft, sm[:, :, 8:32], rep(heads[:, 0:24], T), ALU.add))
            V.scalar_tensor_tensor(tmp24, soft, -1.0, soft, ALU.mult, ALU.min).then_inc(s_sm, 1)
            vv(V.tensor_scalar(soft, soft, 0.0, None, ALU.max))
            dve.wait_ge(s_sp, 1)
            vv(V.tensor_tensor(soft, soft, tmp24, ALU.add))
            vv(V.scalar_tensor_tensor(dec, soft, -1.0, rep(negA, T), ALU.mult, ALU.mult))

    x_tok = ar(6400, D)
    b_tok = ar(7424, 2, P)
    xdt = ar(7680, D)
    xde = ar(8704, D)
    state = ar(9728, 2, 512)
    yb = ar(10752, D)
    abc = ar(17408, SH, P)
    dmat = ar(19456, SH, P)
    cbT = ar(21632, 2, P)
    ysq = ar(21888, D)
    sng = ar(22912, D)
    acum = small[:, 344:360]
    eac = small[:, 360:376]
    edec = small[:, 376:392]
    atot = small[:, 392:408]
    gss = small[:, 408:410]

    s_p3 = sem("ssd_parameters_loaded")
    s_abc = sem("ssd_decays_repeated")
    s_row = sem("ssd_decay_rows")
    s_tr = sem("ssd_transposes")
    s_dx = sem("ssd_exponents_ready")
    s_de = sem("ssd_decays_ready")
    s_m3 = sem("ssd_operands_ready")
    s_y3 = sem("ssd_products_ready")
    s_st = sem("ssd_state_taken")
    s_y3t = sem("ssd_products_taken")
    s_var3, s_root3 = sem("ssd_squares_summed"), sem("ssd_roots_ready")

    with nc.Block() as block:
        @block.sync
        def _(sp):
            sp.dma_start(sng, row_everywhere(a["ssd_norm_g"][0])).then_inc(s_p3, 16)

        @block.tensor
        def _(pe):
            for t in range(T):
                tok = slice(t * P, (t + 1) * P)
                pe.wait_ge(s_abc, t + 1)
                if t:
                    pe.wait_ge(s_y3t, 1)
                    pe.wait_ge(s_st, 1)
                for h in range(SH):
                    last = M.matmul(ps[:, h // 4, (h % 4) * P:(h % 4 + 1) * P], abc[:, h, :], tri_le[:, :])
                M.matmul(ps[:, 4, 0:SH], tri_le[:, :], dec[:, t, 8:24])
                last = M.matmul(ps[:, 4, 16:16 + SH], ones[:, :], dec[:, t, 8:24])
                last.then_inc(s_row, 1)
                for g in range(2):
                    M.matmul(ps[:, 5, g * P:(g + 1) * P], xbcT[:, 8 + g, tok], xbcT[:, 10 + g, tok])
                for g in range(2):
                    last = M.transpose(ps[:, 5, (2 + g) * P:(3 + g) * P], xbcT[:, 8 + g, tok], ident[:, :])
                for k in range(KD):
                    last = M.transpose(ps[:, 6 + k // 4, (k % 4) * P:(k % 4 + 1) * P], xbcT[:, k, tok], ident[:, :])
                last.then_inc(s_tr, 1)
                pe.wait_ge(s_m3, 2 * t + 2)
                for h in range(SH):
                    last = M.matmul(ps[:, h // 8, (h % 8) * SP_:(h % 8 + 1) * SP_], abc[:, h, :],
                                    xdt[:, h * SP_:(h + 1) * SP_])
                for g in range(2):
                    if t == 0:
                        last = M.matmul(ps[:, 2 + g, :], b_tok[:, g, :], xde[:, g * 512:(g + 1) * 512])
                    else:
                        last = M.matmul(ps[:, 2 + g, :], xbcT[:, 10 + g, tok], state[:, g, :])
                last.then_inc(s_y3, 2)

        @block.scalar
        def _(act):
            def repeat_decays(t):
                A.activation(abc, bcast(dec[:, t, 8:24], P), ACT.Copy).then_inc(s_abc, 1)
            repeat_decays(0)
            for t in range(T):
                act.wait_ge(s_dx, 3 * t + 1)
                A.activation(eac, acum, ACT.Exp).then_inc(s_de, 1)
                A.activation(edec, edec, ACT.Exp).then_inc(s_de, 1)
                for q in range(2):
                    act.wait_ge(s_dx, 3 * t + 2 + q)
                    A.activation(dmat[:, 8 * q:8 * q + 8, :], dmat[:, 8 * q:8 * q + 8, :], ACT.Exp).then_inc(s_de, 1)
                if t == 0:
                    act.wait_ge(s_y3, 2)
                    repeat_decays(1)
                    A.activation(state, banks(2, 2, 2, 512), ACT.Copy).then_inc(s_st, 1)
                act.wait_ge(s_var3, t + 1)
                A.activation(gss, gss, ACT.Sqrt, bias=eps_t, scale=1.0 / 512).then_inc(s_root3, 1)

        @block.vector
        def _(dve):
            for t in range(T):
                dve.wait_ge(s_row, t + 1)
                vv(V.tensor_copy(acum, ps[:, 4, 0:SH]))
                V.tensor_tensor(edec, ps[:, 4, 16:16 + SH], acum, ALU.subtract).then_inc(s_dx, 1)
                for h in range(SH):
                    ins = V.scalar_tensor_tensor(dmat[:, h, :], ps[:, h // 4, (h % 4) * P:(h % 4 + 1) * P],
                                                 acum[:, h:h + 1], neg_u, ALU.subtract, ALU.add)
                    if h % 8 == 7:
                        ins.then_inc(s_dx, 1)
                dve.wait_ge(s_tr, t + 1)
                vv(V.tensor_copy(b_tok, ps[:, 5, 256:512].rearrange("p (g n) -> p g n", g=2)))
                vv(V.tensor_copy(cbT, ps[:, 5, 0:256].rearrange("p (g n) -> p g n", g=2)))
                vv(V.tensor_copy(x_tok, banks(6, 2, 1024)))
                xh = x_tok.rearrange("p (h q) -> p h q", h=SH)
                xd = xdt.rearrange("p (h q) -> p h q", h=SH)
                vv(V.tensor_tensor(xd, xh, bcast(soft[:, t, 8:24], SP_), ALU.mult))
                dve.wait_ge(s_de, 4 * t + 2)
                V.tensor_tensor(xde.rearrange("p (h q) -> p h q", h=SH), xd, bcast(edec, SP_), ALU.mult).then_inc(s_m3, 1)
                dve.wait_ge(s_de, 4 * t + 4)
                for g in range(2):
                    ins = V.tensor_tensor(abc[:, 8 * g:8 * g + 8, :], dmat[:, 8 * g:8 * g + 8, :],
                                          rep(cbT[:, g, :], 8), ALU.mult)
                    if g == 0:
                        vv(ins)
                ins.then_inc(s_m3, 1)
                dve.wait_ge(s_y3, 2 * t + 2)
                yh = yb.rearrange("p (h q) -> p h q", h=SH)
                vv(V.tensor_tensor(ysq.rearrange("p (h q) -> p h q", h=SH), xh, bcast(heads[:, 48:64], SP_), ALU.mult))
                ins = V.tensor_tensor(yb, ysq, banks(0, 2, 1024), ALU.add)
                if t == 0:
                    ins.then_inc(s_y3t, 1)
                    dve.wait_ge(s_y3t, 1)
                else:
                    vv(ins)
                    vv(V.tensor_tensor(ysq.rearrange("p (h q) -> p h q", h=SH), banks(2, 2, SH, SP_), bcast(eac, SP_), ALU.mult))
                    vv(V.tensor_tensor(yb, yb, ysq, ALU.add))
                vv(V.tensor_tensor(yb, yb, mix[:, t, D:2 * D], ALU.mult))
                vv(V.tensor_tensor(ysq, yb, yb, ALU.mult))
                V.tensor_reduce(gss, ysq.rearrange("p (g n) -> p g n", g=2), X_AXIS, ALU.add).then_inc(s_var3, 1)
                dve.wait_ge(s_root3, t + 1)
                vv(V.reciprocal(gss, gss))
                if t == 0:
                    dve.wait_ge(s_p3, 16)
                vv(V.tensor_tensor(yb, yb, sng, ALU.mult))
                vv(V.tensor_tensor(mix[:, t, D:2 * D].rearrange("p (g n) -> p g n", g=2),
                                   yb.rearrange("p (g n) -> p g n", g=2), bcast(gss, 512), ALU.mult))

    qkvT = ar(6144, 24, T * P)
    sqT = ar(14336, 16, T * P)
    rsT = ar(18432, 16, T * P)
    ones128 = ar(22528, P)
    s_gconv = sem("gdn_unit_taken")
    s_gact = sem("gdn_convolved")
    s_gz = sem("gdn_gate_taken")
    s_sq = sem("gdn_squares_ready")
    s_sqs = sem("gdn_lengths_ready")
    s_on = sem("scaled_ones_ready")
    s_sqt = sem("gdn_lengths_taken")
    s_ln = sem("gdn_length_logarithms_ready")
    s_len = sem("gdn_inverse_lengths_ready")

    with nc.Block() as block:
        @block.sync
        def _(sp):
            ra.load(sp, 17 + SLOTS)

        @block.gpsimd
        def _(pool):
            G.memset(ones128, float(P)).then_inc(s_on, 1)
            for u in range(16):
                pool.wait_ge(s_gact, u + 1)
                G.tensor_tensor(sqT[:, u, :], qkvT[:, u, :], qkvT[:, u, :], ALU.mult).then_inc(s_sq, 1)

        @block.tensor
        def _(pe):
            for j in range(6):
                w = ra.take(pe)
                for c in range(4):
                    u = 4 * j + c
                    if u >= 6:
                        pe.wait_ge(s_gconv, u - 5)
                    for k in range(KD):
                        last = M.matmul(ps[:, u % 6, 0:T * P], w[:, k, c * P:(c + 1) * P], hT[:, k, :],
                                        start=(k == 0), stop=(k == KD - 1))
                    last.then_inc(s_gunit, 1)
                    if u >= 16:
                        b = u - 16
                        if b == 0:
                            pe.wait_ge(s_on, 1)
                        if b >= 2:
                            pe.wait_ge(s_sqt, b - 1)
                        pe.wait_ge(s_sq, 2 * b + 2)
                        M.matmul(ps[:, 6 + b % 2, :], ones128 if b < 4 else ones[:, :],
                                 sqT[:, 2 * b:2 * b + 2, :].rearrange("p a b -> p (a b)")).then_inc(s_sqs, 1)
            for n in range(2):
                w = ra.take(pe)
                for t in range(T):
                    u = 24 + 2 * n + t
                    pe.wait_ge(s_gconv, u - 5)
                    for k in range(KD):
                        last = M.matmul(ps[:, u % 6, :], hT[:, k, t * P:(t + 1) * P], w[:, k, :],
                                        start=(k == 0), stop=(k == KD - 1))
                    last.then_inc(s_gunit, 1)

        @block.scalar
        def _(act):
            for u in range(24):
                act.wait_ge(s_gconv, u + 1)
                A.activation(qkvT[:, u, :], qkvT[:, u, :], ACT.Silu).then_inc(s_gact, 1)
                if u >= 16:
                    b = u - 16
                    act.wait_ge(s_sqs, b + 1)
                    A.activation(rsT[:, 2 * b:2 * b + 2, :], ps[:, 6 + b % 2, :].rearrange("p (a b) -> p a b", a=2),
                                 ACT.Copy).then_inc(s_sqt, 1)
            act.wait_ge(s_sqt, 8)
            for q in range(2):
                A.activation(rsT[:, 8 * q:8 * q + 8, :], rsT[:, 8 * q:8 * q + 8, :], ACT.Ln,
                             bias=(eps128_t, eps_t)[q]).then_inc(s_ln, 1)
            for q in range(2):
                act.wait_ge(s_ln, q + 1)
                A.activation(rsT[:, 8 * q:8 * q + 8, :], rsT[:, 8 * q:8 * q + 8, :], ACT.Exp, scale=-0.5).then_inc(s_len, 1)
            for u in range(24, 28):
                act.wait_ge(s_gunit, u + 1)
                n, t = divmod(u - 24, 2)
                A.activation(mix[:, t, 512 * n:512 * n + 512], ps[:, u % 6, :], ACT.Silu).then_inc(s_gz, 1)

        @block.vector
        def _(dve):
            conv(dve, 24, 6, lambda u: qkvT[:, u, :], 0, None, s_gunit, s_gconv, 24)
            for q in range(2):
                dve.wait_ge(s_len, q + 1)
                qk = qkvT[:, 8 * q:8 * q + 8, :]
                vv(V.tensor_tensor(qk, qk, rsT[:, 8 * q:8 * q + 8, :], ALU.mult))


    W = 12288
    Lm, Xi, Yi = ar(W, GH, P), ar(W + 1024, GH, P), ar(W + 2048, GH, P)
    LM, Q1 = ar(W + 3072, GH, P), ar(W + 4096, GH, P)
    qkd, kbe, kdc = ar(W + 5120, GH, P), ar(W + 6144, GH, P), ar(W + 7168, GH, P)
    Ug, wTg, qdT, stg = ar(W + 8192, GH, P), ar(W + 9216, GH, P), ar(W + 10240, GH, P), ar(W + 11264, GH, P)
    ob, osq, gbc = LM, Q1, Xi
    gam, gdk = small[:, 344:352], small[:, 352:360]
    gtot, eg, beg = small[:, 360:368], small[:, 368:376], small[:, 376:384]
    oss = small[:, 384:392]

    s_gn = sem("gdn_norm_weight_loaded")
    s_gbc = sem("gdn_decays_repeated")
    s_grow = sem("gdn_decay_rows")
    s_gx = sem("gdn_exponents_ready")
    s_ge = sem("gdn_decays_ready")
    s_gkk = sem("gdn_products_of_keys")
    s_gtr = sem("gdn_transposes")
    s_L = sem("gdn_L_ready")
    s_gops = sem("gdn_operands_ready")
    s_lm = sem("gdn_masked_L_ready")
    s_xi = sem("gdn_inverse_started")
    s_xt = sem("gdn_inverse_transposed")
    s_yt = sem("gdn_inverse_transpose_taken")
    s_q1 = sem("gdn_level_product")
    s_q1t = sem("gdn_level_product_taken")
    s_dd = sem("gdn_level_correction")
    s_upd = sem("gdn_inverse_updated")
    s_uw = sem("gdn_solutions")
    s_wt = sem("gdn_w_taken")
    s_ws = sem("gdn_state_read")
    s_u = sem("gdn_new_values")
    s_o = sem("gdn_outputs")
    s_gst = sem("gdn_state_taken")
    s_oss = sem("gdn_output_squares")
    s_or = sem("gdn_output_roots")

    with nc.Block() as block:
        @block.sync
        def _(sp):
            sp.dma_start(gng, row_everywhere(a["gdn_norm_g"][0])).then_inc(s_gn, 16)

        @block.gpsimd
        def _(pool):
            for t in range(T):
                pool.wait_ge(s_L, t + 1)
                G.tensor_tensor(LM, Lm, rep(masks[:, 0, :], GH), ALU.mult).then_inc(s_lm, 1)
                for lv in range(1, NL):
                    for g in range(2):
                        if lv == 1:
                            pool.wait_ge(s_xi, t + 1)
                        else:
                            pool.wait_ge(s_q1, 12 * t + 2 * (lv - 2) + g + 1)
                        G.tensor_tensor(LM[:, 4 * g:4 * g + 4, :], Lm[:, 4 * g:4 * g + 4, :],
                                        rep(masks[:, lv, :], 4), ALU.mult).then_inc(s_lm, 1)

        @block.tensor
        def _(pe):
            def per_head(b0, fn, start=True, stop=True):
                for h in range(GH):
                    lhsT, rhs = fn(h)
                    ins = M.matmul(ps[:, b0 + h // 4, (h % 4) * P:(h % 4 + 1) * P], lhsT, rhs, start=start, stop=stop)
                return ins

            for t in range(T):
                tok = slice(t * P, (t + 1) * P)
                pe.wait_ge(s_gbc, t + 1)
                per_head(0, lambda h: (gbc[:, h, :], tri_le[:, :]))
                M.matmul(ps[:, 7, 0:8], tri_le[:, :], dec[:, t, 0:8])
                M.matmul(ps[:, 7, 8:16], ones[:, :], dec[:, t, 0:8]).then_inc(s_grow, 1)
                per_head(2, lambda h: (qkvT[:, 8 + h, tok], qkvT[:, 8 + h, tok]))
                per_head(4, lambda h: (qkvT[:, 8 + h, tok], qkvT[:, h, tok])).then_inc(s_gkk, 1)
                pe.wait_ge(s_ge, 3 if t == 0 else 7)
                for b0, c0 in ((6, 8), (0, 16)):
                    for h in range(GH):
                        last = M.transpose(ps[:, b0 + h // 4, (h % 4) * P:(h % 4 + 1) * P], qkvT[:, c0 + h, tok], ident[:, :])
                    last.then_inc(s_gtr, 1)
                pe.wait_ge(s_xi, t + 1)
                pe.wait_ge(s_gops, t + 1)
                for h in range(GH):
                    last = M.transpose(ps[:, 2 + h // 4, (h % 4) * P:(h % 4 + 1) * P], Xi[:, h, :], ident[:, :])
                last.then_inc(s_xt, 1)
                pe.wait_ge(s_yt, t + 1)
                for lv in range(1, NL):
                    for g in range(2):
                        pe.wait_ge(s_lm, 13 * t + 2 + 2 * (lv - 1) + g)
                        if lv > 1:
                            pe.wait_ge(s_upd, 12 * t + 2 * (lv - 2) + g + 1)
                        for h in range(4 * g, 4 * g + 4):
                            last = M.matmul(ps[:, g, (h % 4) * P:(h % 4 + 1) * P], LM[:, h, :], Yi[:, h, :])
                        last.then_inc(s_q1, 1)
                    for g in range(2):
                        pe.wait_ge(s_q1t, 12 * t + 2 * (lv - 1) + g + 1)
                        for h in range(4 * g, 4 * g + 4):
                            last = M.matmul(ps[:, 2 + g, (h % 4) * P:(h % 4 + 1) * P], Xi[:, h, :], Q1[:, h, :])
                        if lv < NL - 1:
                            for h in range(4 * g, 4 * g + 4):
                                last = M.matmul(ps[:, 4 + g, (h % 4) * P:(h % 4 + 1) * P], Q1[:, h, :], Xi[:, h, :])
                        last.then_inc(s_dd, 1)
                pe.wait_ge(s_upd, 12 * t + 12)
                last = per_head(0, lambda h: (Yi[:, h, :], Ug[:, h, :]))
                if t:
                    last = per_head(2, lambda h: (kbe[:, h, :], Yi[:, h, :]))
                last.then_inc(s_uw, 1)
                if t == 0:
                    pe.wait_ge(s_u, 1)
                    per_head(4, lambda h: (qkd[:, h, :], Ug[:, h, :]))
                    per_head(6, lambda h: (kdc[:, h, :], Ug[:, h, :])).then_inc(s_o, 1)
                    pe.wait_ge(s_gst, 1)
                    pe.wait_ge(s_oss, 1)
                else:
                    pe.wait_ge(s_wt, 1)
                    per_head(6, lambda h: (wTg[:, h, :], stg[:, h, :])).then_inc(s_ws, 1)
                    pe.wait_ge(s_u, 2)
                    for h in range(GH):
                        dst = ps[:, 4 + h // 4, (h % 4) * P:(h % 4 + 1) * P]
                        M.matmul(dst, qdT[:, h, :], stg[:, h, :], start=True, stop=False)
                        last = M.matmul(dst, qkd[:, h, :], Ug[:, h, :], start=False, stop=True)
                    last.then_inc(s_o, 1)

        @block.scalar
        def _(act):
            def repeat_decays(t):
                A.activation(gbc, bcast(dec[:, t, 0:8], P), ACT.Copy).then_inc(s_gbc, 1)
            repeat_decays(0)
            for t in range(T):
                act.wait_ge(s_gx, 3 * t + 1)
                aa(A.activation(eg, gam, ACT.Exp))
                A.activation(gdk, gdk, ACT.Exp).then_inc(s_ge, 1)
                act.wait_ge(s_gx, 3 * t + 3)
                A.activation(LM, LM, ACT.Exp, scale=-1.0).then_inc(s_ge, 1)
                A.activation(Q1, Q1, ACT.Exp).then_inc(s_ge, 1)
                if t:
                    A.activation(qdT, banks(0, 2, GH, P), ACT.Exp).then_inc(s_ge, 1)
                act.wait_ge(s_xt, t + 1)
                A.activation(Yi, banks(2, 2, GH, P), ACT.Copy).then_inc(s_yt, 1)
                for lv in range(1, NL):
                    for g in range(2):
                        act.wait_ge(s_q1, 12 * t + 2 * (lv - 1) + g + 1)
                        A.activation(Q1[:, 4 * g:4 * g + 4, :], ps[:, g, :].rearrange("p (h m) -> p h m", h=4),
                                     ACT.Copy).then_inc(s_q1t, 1)
                act.wait_ge(s_uw, t + 1)
                if t:
                    A.activation(wTg, banks(2, 2, GH, P), ACT.Copy).then_inc(s_wt, 1)
                else:
                    act.wait_ge(s_o, 1)
                    repeat_decays(1)
                    A.activation(stg, banks(6, 2, GH, P), ACT.Copy).then_inc(s_gst, 1)
                act.wait_ge(s_oss, 2 * t + 2)
                A.activation(oss, oss, ACT.Sqrt, bias=eps_t, scale=1.0 / P).then_inc(s_or, 1)

        @block.vector
        def _(dve):
            dve.wait_ge(s_gn, 16)
            for t in range(T):
                bt = beta[:, t, :]
                dve.wait_ge(s_grow, t + 1)
                vv(V.tensor_copy(gam, ps[:, 7, 0:8]))
                V.tensor_tensor(gdk, ps[:, 7, 8:16], gam, ALU.subtract).then_inc(s_gx, 1)
                for dst, mask in ((LM, pos_l), (Q1, neg_u)):
                    for h in range(GH):
                        last = V.scalar_tensor_tensor(dst[:, h, :], ps[:, h // 4, (h % 4) * P:(h % 4 + 1) * P],
                                                      gam[:, h:h + 1], mask, ALU.subtract, ALU.add)
                    last.then_inc(s_gx, 1)
                dve.wait_ge(s_gkk, t + 1)
                dve.wait_ge(s_ge, 3 if t == 0 else 7)
                for h in range(GH):
                    last = V.scalar_tensor_tensor(Lm[:, h, :], ps[:, 2 + h // 4, (h % 4) * P:(h % 4 + 1) * P],
                                                  bt[:, h:h + 1], LM[:, h, :], ALU.mult, ALU.mult)
                last.then_inc(s_L, 1)
                vv(V.tensor_tensor(qkd, banks(4, 2, GH, P), Q1, ALU.mult))
                vv(V.tensor_tensor(beg, bt, eg, ALU.mult))
                dve.wait_ge(s_gtr, 2 * t + 2)
                vv(V.tensor_tensor(kbe, banks(6, 2, GH, P), bcast(beg, P), ALU.mult))
                vv(V.tensor_tensor(kdc, banks(6, 2, GH, P), bcast(gdk, P), ALU.mult))
                if t:
                    vv(V.tensor_tensor(qdT, qdT, qkvT[:, 0:8, P:2 * P], ALU.mult))
                V.tensor_tensor(Ug, banks(0, 2, GH, P), bcast(bt, P), ALU.mult).then_inc(s_gops, 1)
                dve.wait_ge(s_lm, 13 * t + 1)
                V.tensor_tensor(Xi, rep(ident[:, :], GH), LM, ALU.subtract).then_inc(s_xi, 1)
                dve.wait_ge(s_xi, t + 1)
                for lv in range(1, NL):
                    for g in range(2):
                        dve.wait_ge(s_dd, 12 * t + 2 * (lv - 1) + g + 1)
                        y, x = Yi[:, 4 * g:4 * g + 4, :], Xi[:, 4 * g:4 * g + 4, :]
                        if lv < NL - 1:
                            vv(V.tensor_tensor(x, x, ps[:, 4 + g, :].rearrange("p (h m) -> p h m", h=4), ALU.subtract))
                        V.tensor_tensor(y, y, ps[:, 2 + g, :].rearrange("p (h m) -> p h m", h=4), ALU.subtract).then_inc(s_upd, 1)
                dve.wait_ge(s_uw, t + 1)
                if t == 0:
                    V.tensor_copy(Ug, banks(0, 2, GH, P)).then_inc(s_u, 1)
                else:
                    vv(V.tensor_copy(Ug, banks(0, 2, GH, P)))
                    dve.wait_ge(s_ws, 1)
                    V.tensor_tensor(Ug, Ug, banks(6, 2, GH, P), ALU.subtract).then_inc(s_u, 1)
                dve.wait_ge(s_o, t + 1)
                V.tensor_copy(ob, banks(4, 2, GH, P)).then_inc(s_oss, 1)
                dve.wait_ge(s_oss, 2 * t + 1)
                vv(V.tensor_tensor(osq, ob, ob, ALU.mult))
                V.tensor_reduce(oss, osq, X_AXIS, ALU.add).then_inc(s_oss, 1)
                dve.wait_ge(s_or, t + 1)
                vv(V.reciprocal(oss, oss))
                z = mix[:, t, 0:D].rearrange("p (h m) -> p h m", h=GH)
                vv(V.tensor_tensor(ob, ob, bcast(oss, P), ALU.mult))
                vv(V.tensor_tensor(ob, ob, rep(gng, GH), ALU.mult))
                vv(V.tensor_tensor(z, z, ob, ALU.mult))


    mixT = ar(6144, 16, T * P)
    h2T = ar(10240, KD, T * P)
    cb2 = ar(12288, KD, 32)
    mod_parts = (ar(12544, 512), ar(16640, 512))
    n2g = ar(13312, D)
    rw = ar(14336, KD, NE)
    rb = ar(14592, NE)
    wo_t = ar(15616, 2 * 512)
    abias2 = ar(17408, 4, D)
    mods = ar(21504, 4, D)
    h2 = ar(2048, T, D)
    MAXP = T * P // CAP
    NI = MAXP * NE + 2
    slot_of = ar(13600, T, NI)
    gate_of = ar(13600 + T * NI, T, NI)
    iota_row = sb("iota_row", [P, 2, CAP])
    passes = sb("passes", [1, 1], I32)

    def select_top(dve, l, k, m8, sel, tmp, s1):
        n = l.shape[1]
        vv(V.max(m8, l))
        vv(V.tensor_scalar(sel, l, m8[:, k - 1:k], None, ALU.is_gt))
        vv(V.tensor_scalar(tmp, l, m8[:, k - 1:k], None, ALU.is_equal))
        vv(V.tensor_reduce(s1, sel, X_AXIS, ALU.add))
        vv(V.tensor_scalar(s1, s1, -1.0, float(k), ALU.mult, ALU.add))
        cum = scratch_cum[:, 0:n]
        vv(V.tensor_tensor_scan(cum, ones[:, 0:n], tmp, 0.0, ALU.mult, ALU.add))
        vv(V.scalar_tensor_tensor(tmp, cum, s1, tmp, ALU.is_le, ALU.mult))
        vv(V.tensor_tensor(sel, sel, tmp, ALU.add))

    scratch_cum = small[:, 470:502]
    lg = small[:, 0:64].rearrange("p (t e) -> p t e", t=T)
    sel = small[:, 64:128].rearrange("p (t e) -> p t e", t=T)
    selsum = small[:, 128:160]
    m8 = small[:, 160:176].rearrange("p (t e) -> p t e", t=T)
    nm = small[:, 176:178]
    s1 = small[:, 178:179]
    gs = small[:, 180:182]
    cmax = small[:, 184:186]
    tmpe = small[:, 192:224]
    ss2 = small[:, 224:226]

    s_p6 = sem("block6_parameters_loaded")
    s_cz2 = sem("condition_columns_cleared_again")
    s_cb2 = sem("condition_ready_again")
    s_modt = sem("late_modulation_taken")
    s_mT = sem("mixed_transposed")
    s_mTt = sem("mixed_transposed_taken")
    s_res = sem("residual_added")
    s_ss2 = sem("second_norm_squares")
    s_h2 = sem("second_normed_ready")
    s_h2T = sem("second_normed_transposed")
    s_h2Tt = sem("second_normed_transposed_taken")
    s_lg = sem("router_logits_ready")
    s_nm = sem("router_max_ready")
    s_el = sem("router_exponentials")
    s_sel = sem("selection_ready")
    s_rk = sem("ranks_ready")

    def dispatch_tables(dve, rank_bank):
        for t in range(T):
            vv(V.scalar_tensor_tensor(tmpe, ps[:, rank_bank, 32 * t:32 * t + 32], 1.0, sel[:, t, :], ALU.add, ALU.mult))
            for b in range(MAXP):
                vv(V.tensor_scalar(slot_of[:, t, b * NE:(b + 1) * NE], tmpe, -1.0 - b * CAP, None, ALU.add))
                if b:
                    vv(V.tensor_copy(gate_of[:, t, b * NE:(b + 1) * NE], gate_of[:, t, 0:NE]))
            vv(V.memset(slot_of[:, t, NI - 2:NI], -1.0))
            vv(V.memset(gate_of[:, t, NI - 2:NI], 0.0))
        vv(V.tensor_reduce(cmax[:, 0:1], ps[:, rank_bank, 64:96], X_AXIS, ALU.max))
        vv(V.tensor_scalar(cmax[:, 1:2], cmax[:, 0:1], float(CAP), 1.0, ALU.is_gt, ALU.add))
        for b in range(2, MAXP):
            vv(V.scalar_tensor_tensor(cmax[:, 1:2], cmax[:, 0:1], float(b * CAP), cmax[:, 1:2], ALU.is_gt, ALU.add))
        return V.tensor_copy(passes[0:1, 0:1], cmax[0:1, 1:2])

    def rank_matmuls(rank_bank):
        M.matmul(ps[:, rank_bank, 0:32], tri_lt[:, :], sel[:, 0, :])
        M.matmul(ps[:, rank_bank, 32:64], tri_lt[:, :], sel[:, 1, :], start=True, stop=False)
        M.matmul(ps[:, rank_bank, 32:64], ones[:, :], sel[:, 0, :], start=False, stop=True)
        return M.matmul(ps[:, rank_bank, 64:96], ones[:, :], selsum)

    class ExpertLoads:

        def __init__(self, name, chunks, bias=None):
            self.name, self.chunks, self.bias = name, chunks, bias
            self.full = [sem(f"{name}_slot{s}_full") for s in range(SLOTS)]
            self.s_done = sem(f"{name}_gate_up_or_down_multiplied")
            self.s_bias = sem(f"{name}_bias_loaded") if bias else None
            self.bias_t = ar(5120, 2, 512)

        def load_bias(self, sp, e):
            for which in range(2):
                for j in range(2):
                    sp.dma_start(self.bias_t[halves[j], which, :],
                                 self.bias(e, which, j).partition_broadcast(CAP)).then_inc(self.s_bias, 16)

        def load_first(self, sp, ring):
            for n in range(len(ring.chunks) - SLOTS, len(ring.chunks)):
                sp.wait_ge(*ring.chunks[n][2])
                s = n % SLOTS
                src, k, w = self.chunks(0)[s]
                sp.dma_start(slot(s, k, w), src).then_inc(self.full[s], 16)

        def load_rest(self, sp, items, biases_used=None):
            n = sp.value_load(passes[0:1, 0:1], min_val=1, max_val=MAXP)

            def load(item, base):
                for s, (src, k, w) in enumerate(self.chunks(item)):
                    sp.wait_ge(self.s_done, base * 3 + s // 2 + 1)
                    sp.dma_start(slot(s, k, w), src).then_inc(self.full[s], 16)
                    if biases_used and s == 3:
                        sp.wait_ge(biases_used, base * 2 + 2)
                        self.load_bias(sp, item)

            with sp.Fori(0, items - 1) as q:
                load(q + 1, q)
            with sp.If(n > 1):
                with sp.Fori(0, n - 1) as p:
                    load(0, p * items + items - 1)
                    with sp.Fori(0, items - 1) as q:
                        load(q + 1, p * items + items + q)

        def arrived(self, pe, s, i, k=KD, w=512):
            pe.wait_ge(self.full[s], i * 16 + 16)
            return slot(s, k, w)

    halves = [slice(CAP * j, CAP * (j + 1)) for j in range(2)]

    def one(w, e):
        return w[e] if isinstance(e, int) else w[bass.ds(e, 1)].rearrange("o r c -> (o r) c")

    w_gu, w_dn, b_gu = a["moe_w_gu"][0], a["moe_w_down"][0], a["moe_b_gu"][0]
    def gate_up_down(e):
        gu, dn = one(w_gu, e), one(w_dn, e)
        return [(cols(gu, 512 * j), KD, 512) for j in range(4)] + [(cols(dn, 512 * j), KD, 512) for j in range(2)]

    def gu_bias(e, which, j):
        at = 1024 * which + 512 * j
        if isinstance(e, int):
            return b_gu[e, at:at + 512]
        return b_gu[bass.ds(e, 1), at:at + 512].rearrange("o n -> (o n)")

    loads1 = ExpertLoads("experts1", gate_up_down, gu_bias)
    bdn = ar(17408, D)
    s_bdn = sem("down_bias_loaded")

    with nc.Block() as block:
        @block.sync
        def _(sp):
            sp.dma_start(abias2.rearrange("p a b -> p (a b)"), row_everywhere(a["ada_b"][0][2 * D:6 * D])).then_inc(s_p6, 16)
            sp.dma_start(n2g, row_everywhere(a["norm2_g"][0])).then_inc(s_p6, 16)
            sp.dma_start(rw, a["router_w"][0].rearrange("(k p) e -> p k e", p=P)).then_inc(s_p6, 16)
            sp.dma_start(rb, row_everywhere(a["router_b"][0])).then_inc(s_p6, 16)
            ra.load(sp, len(ra.chunks))
            sp.wait_ge(s_modt, 8)
            sp.dma_start(bdn[0:NE, :], a["moe_b_down"][0]).then_inc(s_bdn, 16)
            sp.wait_ge(s_mT, 4)
            loads1.load_bias(sp, 0)
            loads1.load_first(sp, ra)

        @block.gpsimd
        def _(pool):
            G.memset(cb2, 0.0).then_inc(s_cz2, 1)
            gg(G.iota(iota_row[:, :, :], pattern=[[0, 2], [1, CAP]], base=0, channel_multiplier=0,
                      allow_small_or_imprecise_dtypes=True))

        @block.tensor
        def _(pe):
            pe.wait_ge(s_cb2, 1)
            for j in range(9):
                if j < 8:
                    if j >= 2:
                        pe.wait_ge(s_part, 4 + j - 1)
                    modulation_sums(pe, cb2, j % 2)
                if j:
                    pe.wait_ge(s_part, 4 + j)
                    if j >= 3:
                        pe.wait_ge(s_modt, j - 2)
                    M.matmul(ps[:, 2 + (j - 1) % 2, :], ones[:, :], mod_parts[(j - 1) % 2]).then_inc(s_comb, 1)
                if j % 2 == 1 and j // 2 < 4:
                    i = j // 2
                    t, half = divmod(i, 2)
                    if i >= 2:
                        pe.wait_ge(s_mTt, i - 1)
                    for k in range(8):
                        last = M.transpose(ps[:, 4 + 2 * (i % 2) + k // 4, (k % 4) * P:(k % 4 + 1) * P],
                                           mix[:, t, (8 * half + k) * P:(8 * half + k + 1) * P], ident[:, :])
                    last.then_inc(s_mT, 1)
            pe.wait_ge(s_modt, 8)
            pe.wait_ge(s_mTt, 4)
            for n in range(2):
                for kh in range(2):
                    w = ra.take(pe)
                    for t in range(T):
                        for k in range(KD):
                            last = M.matmul(ps[:, 2 * t + n, :], mixT[:, 8 * kh + k, t * P:(t + 1) * P], w[:, k, :],
                                            start=(kh == 0 and k == 0), stop=(kh == 1 and k == KD - 1))
                    last.then_inc(s_wout, 1)
            for t in range(T):
                pe.wait_ge(s_h2, t + 1)
                for k in range(KD):
                    last = M.transpose(ps[:, 4 + 2 * t + k // 4, (k % 4) * P:(k % 4 + 1) * P],
                                       h2[:, t, k * P:(k + 1) * P], ident[:, :])
                last.then_inc(s_h2T, 1)
            pe.wait_ge(s_h2Tt, 4)
            for t in range(T):
                for k in range(KD):
                    last = M.matmul(ps[:, 0, 32 * t:32 * t + 32], h2T[:, k, t * P:(t + 1) * P], rw[:, k, :],
                                    start=(k == 0), stop=(k == KD - 1))
            last.then_inc(s_lg, 1)
            pe.wait_ge(s_sel, 1)
            rank_matmuls(1).then_inc(s_rk, 1)

        @block.scalar
        def _(act):
            act.wait_ge(s_cz2, 1)
            A.activation(cb2[:, :, 0], convw[:, 156:164], ACT.Copy).then_inc(s_cb2, 1)
            for j in range(8):
                act.wait_ge(s_ada, 5 + j)
                if j >= 2:
                    act.wait_ge(s_comb, 4 + j - 1)
                A.activation(mod_parts[j % 2], ps[:, j % 2, :], ACT.Copy).then_inc(s_part, 1)
                if j % 2 == 0:
                    continue
                i = j // 2
                act.wait_ge(s_mT, i + 1)
                t, half = divmod(i, 2)
                A.activation(mixT[:, 8 * half:8 * half + 8, t * P:(t + 1) * P],
                             banks(4 + 2 * (i % 2), 2, 8, P), ACT.Copy).then_inc(s_mTt, 1)
            for t in range(T):
                act.wait_ge(s_res, t + 1)
                A.activation(h2[:, t, :], x_res[:, t, :], ACT.Square, accum_out=ss2[:, t:t + 1]).then_inc(s_ss2, 1)
            act.wait_ge(s_ss2, 2)
            A.activation(ss2, ss2, ACT.Sqrt, bias=eps_t, scale=1.0 / D).then_inc(s_ss2, 1)
            for t in range(T):
                act.wait_ge(s_h2T, t + 1)
                for k2 in range(2):
                    A.activation(h2T[:, 4 * k2:4 * k2 + 4, t * P:(t + 1) * P],
                                 ps[:, 4 + 2 * t + k2, :].rearrange("p (k m) -> p k m", k=4), ACT.Copy).then_inc(s_h2Tt, 1)
            act.wait_ge(s_nm, 1)
            for t in range(T):
                A.activation(gate_of[:, t, 0:NE], lg[:, t, :], ACT.Exp, bias=nm[:, t:t + 1]).then_inc(s_el, 1)

        @block.vector
        def _(dve):
            dve.wait_ge(s_p6, 64)
            for j in range(8):
                dve.wait_ge(s_comb, 5 + j)
                i, half = divmod(j, 2)
                V.tensor_tensor(mods[:, i, 512 * half:512 * half + 512], ps[:, 2 + j % 2, :],
                                abias2[:, i, 512 * half:512 * half + 512], ALU.add).then_inc(s_modt, 1)
            dve.wait_ge(s_modt, 8)
            vv(V.scalar_tensor_tensor(mods[:, 2, :], mods[:, 2, :], 1.0, n2g, ALU.add, ALU.mult))
            dve.wait_ge(s_wout, 4)
            for t in range(T):
                vv(V.tensor_tensor(wo_t, banks(2 * t, 2, 1024), mods[:, 0, :], ALU.mult))
                V.tensor_tensor(x_res[:, t, :], x_res[:, t, :], wo_t, ALU.add).then_inc(s_res, 1)
                dve.wait_ge(s_res, t + 1)
            dve.wait_ge(s_ss2, 3)
            vv(V.reciprocal(ss2, ss2))
            for t in range(T):
                vv(V.scalar_tensor_tensor(h2[:, t, :], x_res[:, t, :], ss2[:, t:t + 1], mods[:, 2, :], ALU.mult, ALU.mult))
                V.tensor_tensor(h2[:, t, :], h2[:, t, :], mods[:, 1, :], ALU.add).then_inc(s_h2, 1)
            dve.wait_ge(s_lg, 1)
            vv(V.tensor_tensor(lg, ps[:, 0, 0:64].rearrange("p (t e) -> p t e", t=T), rep(rb, T), ALU.add))
            for t in range(T):
                select_top(dve, lg[:, t, :], 4, m8[:, t, :], sel[:, t, :], tmpe, s1)
            vv(V.tensor_tensor(selsum, sel[:, 0, :], sel[:, 1, :], ALU.add))
            V.tensor_scalar(nm, m8[:, :, 0], -1.0, None, ALU.mult).then_inc(s_nm, 1)
            dve.wait_ge(s_nm, 1)
            V.tensor_copy(gs, nm).then_inc(s_sel, 1)
            dve.wait_ge(s_el, 2)
            vv(V.tensor_tensor(gate_of[:, :, 0:NE], gate_of[:, :, 0:NE], sel, ALU.mult))
            vv(V.tensor_reduce(gs, gate_of[:, :, 0:NE], X_AXIS, ALU.add))
            vv(V.reciprocal(gs, gs))
            vv(V.tensor_tensor(gate_of[:, :, 0:NE], gate_of[:, :, 0:NE], bcast(gs, NE), ALU.mult))
            dve.wait_ge(s_rk, 1)
            vv(dispatch_tables(dve, 1))

    def experts(loads, x_tok, acc_start):
        KH = 4
        xgT, tg, tu, sg = ar(7168, KD, CAP), ar(8192, 512), ar(8704, 512), ar(9216, 512)
        y, yT, y2 = ar(9728, KH, P), ar(10752, KH, P), ar(11776, 512)
        onehot, gated, GT = ar(12800, T, CAP), ar(13056, T, P), ar(13312, T, P)
        name, s_done, bias_t = loads.name, loads.s_done, loads.bias_t
        s_one = sem(f"{name}_onehot_ready")
        s_gat = sem(f"{name}_gated_ready")
        s_xg = sem(f"{name}_gathered")
        s_xgt = sem(f"{name}_gathered_taken")
        s_bb = sem(f"{name}_biases_added")
        s_g = sem(f"{name}_gate_clamped")
        s_sig = sem(f"{name}_sigmoid_ready")
        s_y = sem(f"{name}_hidden_ready")
        s_yT = sem(f"{name}_hidden_transposed")
        s_yTt = sem(f"{name}_hidden_transposed_taken")
        s_GT = sem(f"{name}_gated_transposed")
        s_GTt = sem(f"{name}_gated_transposed_taken")
        s_y2 = sem(f"{name}_result_taken")
        s_v = sem(f"{name}_product_ready")

        with nc.Block() as block:
            @block.sync
            def _(sp):
                loads.load_rest(sp, NE, s_bb)

            @block.tensor
            def _(pe):
                def gather(i):
                    pe.wait_ge(s_one, i + 1)
                    for k in range(KD):
                        for t in range(T):
                            last = M.matmul(ps[:, 6, k * CAP:(k + 1) * CAP], x_tok[:, t, k * P:(k + 1) * P], onehot[:, t, :],
                                            start=(t == 0), stop=(t == T - 1))
                    last.then_inc(s_xg, 1)

                acc_start(pe)
                gather(0)
                n = pe.value_load(passes[0:1, 0:1], min_val=1, max_val=MAXP)
                with pe.Fori(0, n) as p:
                    with pe.Fori(0, NE) as q:
                        i = p * NE + q
                        pe.wait_ge(s_xgt, i + 1)
                        for which in range(2):
                            w = [loads.arrived(pe, 2 * which + j, i) for j in range(2)]
                            for k in range(KD):
                                for j in range(2):
                                    last = M.matmul(ps[halves[j], 4 + which, :], xgT[:, k, :], w[j][:, k, :],
                                                    start=(k == 0), stop=(k == KD - 1))
                            last.then_inc(s_done, 1)
                        gather(i + 1)
                        pe.wait_ge(s_y, i + 1)
                        for k in range(KH):
                            last = M.transpose(ps[:, 7, k * P:(k + 1) * P], y[:, k, :], ident[:, :])
                        last.then_inc(s_yT, 1)
                        pe.wait_ge(s_gat, i + 1)
                        pe.wait_ge(s_xgt, i + 2)
                        for t in range(T):
                            last = M.transpose(ps[:, 6, t * P:(t + 1) * P], gated[:, t, :], ident[:, :])
                        last.then_inc(s_GT, 1)
                        w = [loads.arrived(pe, 4 + j, i) for j in range(2)]
                        pe.wait_ge(s_yTt, i + 1)
                        for k in range(2 * KH):
                            for j in range(2):
                                last = M.matmul(ps[halves[j], 4, :], yT[:, k % KH, halves[k // KH]], w[j][:, k, :],
                                                start=(k == 0), stop=(k == 2 * KH - 1))
                        last.then_inc(s_done, 1)
                        pe.wait_ge(s_GTt, i + 1)
                        pe.wait_ge(s_y2, i + 1)
                        for t in range(T):
                            for j in range(2):
                                M.matmul(ps[:, 2 * t + j, :], GT[halves[j], t, :], y2[halves[j], :], start=False, stop=False,
                                         skip_group_check=True)
                M.matmul(ps[:, 7, 0:P], ident[:, :], ident[:, :]).then_inc(s_GT, 1)

            @block.scalar
            def _(act):
                def take_gathered(i):
                    act.wait_ge(s_xg, i + 1)
                    A.activation(xgT, ps[:, 6, :].rearrange("p (k m) -> p k m", k=KD), ACT.Copy).then_inc(s_xgt, 1)
                take_gathered(0)
                n = act.value_load(passes[0:1, 0:1], min_val=1, max_val=MAXP)
                with act.Fori(0, n) as p:
                    with act.Fori(0, NE) as q:
                        i = p * NE + q
                        act.wait_ge(s_g, i + 1)
                        A.activation(sg, tg, ACT.Sigmoid, scale=1.702).then_inc(s_sig, 1)
                        take_gathered(i + 1)
                        act.wait_ge(s_yT, i + 1)
                        A.activation(yT, ps[:, 7, :].rearrange("p (k m) -> p k m", k=KH), ACT.Copy).then_inc(s_yTt, 1)
                        act.wait_ge(s_GT, i + 1)
                        A.activation(GT, ps[:, 6, 0:2 * P].rearrange("p (t m) -> p t m", t=T), ACT.Copy).then_inc(s_GTt, 1)
                        act.wait_ge(s_done, i * 3 + 3)
                        A.activation(y2, ps[:, 4, :], ACT.Copy).then_inc(s_y2, 1)

            @block.vector
            def _(dve):
                def make_onehot(i):
                    for t in range(T):
                        ins = V.tensor_scalar(onehot[:, t, :], iota_row[:, 0, :], slot_of[:, t, bass.ds(i, 1)], None, ALU.is_equal)
                    ins.then_inc(s_one, 1)
                make_onehot(0)
                n = dve.value_load(passes[0:1, 0:1], min_val=1, max_val=MAXP)
                with dve.Fori(0, n) as p:
                    with dve.Fori(0, NE) as q:
                        i = p * NE + q
                        dve.wait_ge(s_done, i * 3 + 1)
                        dve.wait_ge(loads.s_bias, i * 64 + 64)
                        V.tensor_tensor(tg, ps[:, 4, :], bias_t[:, 0, :], ALU.add).then_inc(s_bb, 1)
                        dve.wait_ge(s_bb, i * 2 + 1)
                        V.tensor_scalar(tg, tg, 7.0, None, ALU.min).then_inc(s_g, 1)
                        make_onehot(i + 1)
                        for t in range(T):
                            ins = V.tensor_scalar(gated[:, t, :], iota_row.rearrange("p a b -> p (a b)"), slot_of[:, t, bass.ds(i, 1)],
                                                  gate_of[:, t, bass.ds(i, 1)], ALU.is_equal, ALU.mult)
                        ins.then_inc(s_gat, 1)
                        dve.wait_ge(s_done, i * 3 + 2)
                        V.tensor_tensor(tu, ps[:, 5, :], bias_t[:, 1, :], ALU.add).then_inc(s_bb, 1)
                        dve.wait_ge(s_bb, i * 2 + 2)
                        V.tensor_scalar(tu, tu, 7.0, -7.0, ALU.min, ALU.max).then_inc(s_v, 1)
                        dve.wait_ge(s_sig, i + 1)
                        V.tensor_tensor(tg, tg, sg, ALU.mult).then_inc(s_v, 1)
                        dve.wait_ge(s_v, i * 2 + 2)
                        V.scalar_tensor_tensor(y.rearrange("p a b -> p (a b)"), tu, 1.0, tg, ALU.add, ALU.mult).then_inc(s_y, 1)

    gT = ar(15360, T * P)
    s_gT, s_gTt = sem("gates_transposed"), sem("gates_transposed_taken")
    with nc.Block() as block:
        @block.tensor
        def _(pe):
            for t in range(T):
                last = M.transpose(ps[0:NE, 7, t * P:(t + 1) * P], gate_of[:, t, 0:NE], ident[:, :])
            last.then_inc(s_gT, 1)

        @block.scalar
        def _(act):
            act.wait_ge(s_gT, 1)
            A.activation(gT[0:NE, :], ps[0:NE, 7, 0:T * P], ACT.Copy).then_inc(s_gTt, 1)

    def start_acc(pe):
        pe.wait_ge(s_bdn, 16)
        pe.wait_ge(s_gTt, 1)
        for t in range(T):
            for d in range(2):
                M.matmul(ps[:, 2 * t + d, :], gT[0:NE, t * P:(t + 1) * P], bdn[0:NE, 512 * d:512 * d + 512],
                         start=True, stop=False, skip_group_check=True)

    experts(loads1, h2, start_acc)


    recycle([s for s in made if s not in (c_v.sem, c_a.sem, c_g.sem)])

    class C2:
        Q, KC, VC, KS, VS, KW, VW, GATE, GQ, GK, GV, GA, GR, MA, MB, END = (
            0, 512, 640, 768, 896, 1024, 1152, 1280, 1304, 1560, 1816, 2328, 2344, 2856, 3880, 4904)

    ZW = C2.END
    z = ar(2048, T, ZW)
    uT = ar(11856, KD, T * P)
    un = ar(13904, T, D)
    fg, mg = ar(15952, D), ar(16976, D)
    acc_sb = ar(18000, T, D)
    rope_in = ar(20100, 3, 32)
    rope_k = ar(20200, 3, 32)
    trig = ar(25088, 2, 3, 32)
    inv = ar(20300, 32)
    posi = ar(20400, 4).bitcast(I32)
    posf = ar(20408, 4)
    ss3 = small[:, 230:232]

    rb2 = Ring("pre2")
    s_z = sem("projection_unit_ready")
    s_cmp = sem("compressed_hidden_ready")
    s_pa = sem("branch_projection_ready")
    s_po = sem("output_projection_ready")
    w2 = a["w_in_2"][0]
    NZ = -(-ZW // 512)
    for j in range(NZ):
        n = min(512, ZW - 512 * j)
        rb2.add(cols(w2, 512 * j, n), (KD, n), (s_z, 2 * j + 2))
    for i, kv in enumerate("kv"):
        rb2.add(a[f"cmp_w1_{kv}_2"][0].rearrange("(j p) n -> p j n", p=P), (16, 256), (s_cmp, i + 1))
    for i, nm_ in enumerate(("w_proj_nsa_2", "w_proj_gla_2")):
        rb2.add(a[nm_][0].rearrange("(k p) n -> p k n", p=P), (4, 1024), (s_pa, i + 1))
    for i in range(2):
        rb2.add(cols(a["w_out_2"][0], 512 * i), (KD, 512), (s_po, i + 1))

    s_p8 = sem("block8_parameters_loaded")
    s_pos = sem("positions_loaded")
    s_pz = sem("positions_cleared")
    s_inv = sem("frequencies_ready")
    s_fs = sem("norm_squares_ready")
    s_fr = sem("norm_roots_ready")
    s_un = sem("normed_again_ready")
    s_uT = sem("normed_again_transposed")
    s_uTt = sem("normed_again_transposed_taken")
    s_zt2 = sem("projection_unit_taken")
    s_ang = sem("angles_reduced")

    TWO_PI = 2.0 * math.pi
    PI_C1 = 6.28125
    PI_C2 = math.floor((TWO_PI - PI_C1) * 2.0 ** 22) / 2.0 ** 22
    PI_C3 = TWO_PI - PI_C1 - PI_C2
    ROUND = 1.5 * 2.0 ** 23
    PI_F = 3.1415925

    s_xr = sem("residual2_added")
    with nc.Block() as block:
        @block.sync
        def _(sp):
            sp.dma_start(fg, row_everywhere(a["final_g"])).then_inc(s_p8, 16)
            sp.dma_start(mg, row_everywhere(a["g_mix_2"][0])).then_inc(s_p8, 16)
            rb2.load(sp, 1)
            pos = a["positions_2"][0]
            sp.wait_ge(s_pz, 1)
            sp.dma_start(posi[:, 0:2], pos.rearrange("(t p) -> p t", p=P), allow_slow_non_contiguous=True).then_inc(s_pos, 16)
            for q in range(4):
                sp.dma_start(posi[32 * q:32 * q + 15, 2:3], pos[31:256:16].rearrange("(p o) -> p o", o=1), allow_slow_non_contiguous=True).then_inc(s_pos, 16)
            rb2.load(sp, NZ + SLOTS)

        @block.gpsimd
        def _(pool):
            G.memset(posi[:, :], 0).then_inc(s_pz, 1)
            for i in range(32):
                last = G.memset(inv[:, i:i + 1], 10000.0 ** (-i / 32.0))
            last.then_inc(s_inv, 1)

        @block.tensor
        def _(pe):
            for t in range(T):
                pe.wait_ge(s_un, t + 1)
                for k in range(KD):
                    last = M.transpose(ps[:, 4 + 2 * t + k // 4, (k % 4) * P:(k % 4 + 1) * P],
                                       un[:, t, k * P:(k + 1) * P], ident[:, :])
                last.then_inc(s_uT, 1)
            pe.wait_ge(s_uTt, 4)
            for j in range(NZ):
                w = rb2.take(pe)
                n = min(512, ZW - 512 * j)
                for t in range(T):
                    u = 2 * j + t
                    if u >= 8:
                        pe.wait_ge(s_zt2, u - 7)
                    for k in range(KD):
                        last = M.matmul(ps[:, u % 8, 0:n], uT[:, k, t * P:(t + 1) * P], w[:, k, :],
                                        start=(k == 0), stop=(k == KD - 1))
                    last.then_inc(s_z, 1)

        @block.scalar
        def _(act):
            for rnd in range(2):
                for t in range(T):
                    act.wait_ge(s_xr, 2 * rnd + t + 1)
                    A.activation(un[:, t, :], x_res[:, t, :], ACT.Square, accum_out=ss3[:, t:t + 1]).then_inc(s_fs, 1)
                act.wait_ge(s_fs, 2 * rnd + 2)
                A.activation(ss3, ss3, ACT.Sqrt, bias=eps_t, scale=1.0 / D).then_inc(s_fr, 1)
            for t in range(T):
                act.wait_ge(s_uT, t + 1)
                for k2 in range(2):
                    A.activation(uT[:, 4 * k2:4 * k2 + 4, t * P:(t + 1) * P],
                                 ps[:, 4 + 2 * t + k2, :].rearrange("p (k m) -> p k m", k=4), ACT.Copy).then_inc(s_uTt, 1)
            for j in range(NZ):
                n = min(512, ZW - 512 * j)
                for t in range(T):
                    act.wait_ge(s_z, 2 * j + t + 1)
                    A.activation(z[:, t, 512 * j:512 * j + n], ps[:, (2 * j + t) % 8, 0:n], ACT.Copy).then_inc(s_zt2, 1)
            act.wait_ge(s_ang, 1)
            A.activation(trig.rearrange("p a b c -> p (a b c)"), trig.rearrange("p a b c -> p (a b c)"), ACT.Sin)

        @block.vector
        def _(dve):
            g2m = mods[:, 3, :]
            for t in range(T):
                vv(V.tensor_tensor(acc_sb[:, t, :], banks(2 * t, 2, 1024), g2m, ALU.mult))
                V.tensor_tensor(x_res[:, t, :], x_res[:, t, :], acc_sb[:, t, :], ALU.add).then_inc(s_xr, 1)
            dve.wait_ge(s_p8, 32)
            for rnd in range(2):
                dve.wait_ge(s_fr, rnd + 1)
                vv(V.reciprocal(ss3, ss3))
                for t in range(T):
                    if rnd == 0:
                        V.scalar_tensor_tensor(x_res[:, t, :], x_res[:, t, :], ss3[:, t:t + 1], fg, ALU.mult, ALU.mult).then_inc(s_xr, 1)
                    else:
                        V.scalar_tensor_tensor(un[:, t, :], x_res[:, t, :], ss3[:, t:t + 1], mg, ALU.mult, ALU.mult).then_inc(s_un, 1)
            dve.wait_ge(s_pos, 80)
            dve.wait_ge(s_inv, 1)
            vv(V.tensor_copy(posf[:, 0:3], posi[:, 0:3]))
            for c in range(3):
                vv(V.tensor_scalar(rope_in[:, c, :], inv, posf[:, c:c + 1], None, ALU.mult))
            flat = lambda v: v.rearrange("p a b -> p (a b)")
            ri, rk, cosv, sinv = flat(rope_in), flat(rope_k), flat(trig[:, 0, :, :]), flat(trig[:, 1, :, :])
            vv(V.tensor_scalar(rk, ri, 1.0 / TWO_PI, ROUND, ALU.mult, ALU.add))
            vv(V.tensor_scalar(rk, rk, ROUND, None, ALU.subtract))
            for part in (PI_C1, PI_C2, PI_C3):
                vv(V.scalar_tensor_tensor(ri, rk, -part, ri, ALU.mult, ALU.add))
            vv(V.tensor_scalar(sinv, ri, PI_F, -PI_F, ALU.min, ALU.max))
            vv(V.tensor_scalar(cosv, ri, math.pi / 2, None, ALU.add))
            vv(V.tensor_scalar(rk, cosv, PI_F, -TWO_PI, ALU.is_gt, ALU.mult))
            vv(V.tensor_tensor(cosv, cosv, rk, ALU.add))
            V.tensor_scalar(cosv, cosv, PI_F, -PI_F, ALU.min, ALU.max).then_inc(s_ang, 1)

    NH, NG, DH, NCB = 8, 2, 64, 15
    B = 11856
    qT2, kT2, cT2 = ar(B, 4, T * P), ar(B + 1024, 4, T * P), ar(B + 2048, 4, T * P)
    Fc = ar(B + 3072, 2, 16, P)
    S = ar(B + 3072, 2048)
    PT = ar(B + 5120, 2048)
    o_nsa = ar(B + 7168, T, 512)
    o_gla = ar(B + 8192, T, 512)
    rt = ar(B + 9216, 4, 256)
    hid = ar(B + 9216, 2, 256)
    hidT = ar(B + 9728, 4, P)
    b1 = ar(B + 10240, 2, 256)
    w2c = ar(B + 10752, 2, 2, DH)
    b2c = ar(B + 11008, 2, DH)
    kv_c = ar(B + 11136, 2, DH)
    kcT = ar(B + 11264, P)
    posT = ar(B + 11392, 32)
    pos_rows = ar(B + 11424, P)
    cmp_ok = ar(B + 11552, 2, T, DH)
    cmp_neg = ar(B + 11808, 2, T, DH)
    caus = ar(B + 12064, P)
    kdup = ar(B + 12192, P)
    kd = ar(B + 7168, T, 8, P)
    sg_nsa = ar(B + 12320, T, 24)
    rmax, rsum = ar(B + 12368, NH), ar(B + 12376, NH)
    assert B + 12384 <= 25088

    s_p9 = sem("nsa_parameters_loaded")
    s_m9 = sem("nsa_masks_ready")
    s_rp = sem("roped")
    s_dup = sem("doubled")
    s_t9 = sem("nsa_transposed")
    s_t9t = sem("nsa_transposed_taken")
    s_pT = sem("block_positions_transposed")
    s_F = sem("block_inputs_ready")
    s_hb = sem("compressed_hidden_biased")
    s_hg = sem("compressed_hidden_activated")
    s_hT = sem("compressed_hidden_transposed")
    s_hTt2 = sem("compressed_hidden_transposed_taken")
    s_kc = sem("compressed_ready")
    s_kct = sem("compressed_taken")
    s_kcT = sem("compressed_keys_transposed")
    s_kcTt = sem("compressed_keys_transposed_taken")
    s_sc = sem("scores_ready")
    s_sm9 = sem("scores_shifted")
    s_ex = sem("scores_exponentiated")
    s_pr = sem("probabilities_ready")
    s_ptr = sem("probabilities_transposed")
    s_ptt = sem("probabilities_transposed_taken")
    s_ov = sem("attention_part_ready")
    s_ovt = sem("attention_part_taken")
    s_sg9 = sem("branch_gates_ready")

    UNITS = [(t, br) for t in range(T) for br in range(3)]

    def head_of(s):
        return 2 * (s % 4) + s // 4

    def score_at(s, Lk):
        return s * Lk if Lk >= P else (s // 4) * 512 + (s % 4) * Lk

    def parts_of(t, br):
        return 2 if (br and t) else 1

    with nc.Block() as block:
        @block.sync
        def _(sp):
            for i, kv in enumerate("kv"):
                sp.dma_start(pos_rows[16 * i:16 * i + 16, :], a[f"cmp_pos_{kv}_2"][0].rearrange("(j i) d -> j (i d)", i=2)).then_inc(s_p9, 16)
                sp.dma_start(b1[:, i, :], row_everywhere(a[f"cmp_b1_{kv}_2"][0])).then_inc(s_p9, 16)
                sp.dma_start(w2c[:, i, :, :], a[f"cmp_w2_{kv}_2"][0].rearrange("(k p) n -> p k n", p=P)).then_inc(s_p9, 16)
                sp.dma_start(b2c[:, i, :], row_everywhere(a[f"cmp_b2_{kv}_2"][0])).then_inc(s_p9, 16)
            rb2.load(sp, 99)

        @block.gpsimd
        def _(pool):
            gg(G.memset(Fc.rearrange("p a b c -> p (a b c)"), 0.0))
            gg(G.memset(caus, 0.0))
            gg(G.affine_select(out=caus, in_=caus, compare_op=ALU.is_ge, fill=-BIG, base=0,
                               pattern=[[-1, P]], channel_multiplier=1))
            gg(G.memset(cmp_ok.rearrange("p a b c -> p (a b c)"), 0.0))
            for g in range(NG):
                for t in range(T):
                    own = cmp_ok[:, g, t, 32 * g:32 * g + NCB]
                    gg(G.memset(own, 1.0))
                    gg(G.affine_select(out=own, in_=own, compare_op=ALU.is_ge, fill=0.0, base=P * t - 31,
                                       pattern=[[-16, NCB]], channel_multiplier=1))
            f = lambda v: v.rearrange("p a b c -> p (a b c)")
            G.tensor_scalar(f(cmp_neg), f(cmp_ok), BIG, -BIG, ALU.mult, ALU.add).then_inc(s_m9, 1)

        @block.tensor
        def _(pe):
            pe.wait_ge(s_p9, 128)
            M.transpose(ps[:, 6, 0:32], pos_rows[0:32, :], ident[0:32, 0:32]).then_inc(s_pT, 1)
            pe.wait_ge(s_dup, 2)
            for g in range(NG):
                for kv in range(2):
                    for t in range(T):
                        last = M.transpose(ps[:, 4 + kv, (2 * g + t) * P:(2 * g + t + 1) * P],
                                           kd[:, t, 2 * kv + g, :], ident[:, :])
            last.then_inc(s_t9, 1)
            pe.wait_ge(s_dup, 6)
            for hp in range(4):
                for t in range(T):
                    M.transpose(ps[:, hp // 2, (hp % 2) * 256 + t * P:(hp % 2) * 256 + (t + 1) * P],
                                z[:, t, P * hp:P * hp + P], ident[:, :])
            for br in range(2):
                for g in range(NG):
                    for t in range(T):
                        last = M.transpose(ps[:, 2 + br, 256 * g + t * P:256 * g + (t + 1) * P],
                                           kd[:, t, 4 + 2 * br + g, :], ident[:, :])
            last.then_inc(s_t9, 1)
            pe.wait_ge(s_F, 1)
            for kv in range(2):
                w = rb2.take(pe)
                for j in range(16):
                    last = M.matmul(ps[:, 6 + kv, 0:256], Fc[:, kv, j, :], w[:, j, :], start=(j == 0), stop=(j == 15))
                last.then_inc(s_cmp, 1)
            pe.wait_ge(s_hg, 1)
            pe.wait_ge(s_t9t, 2)
            for kv in range(2):
                for k in range(2):
                    last = M.transpose(ps[:, 5, (2 * kv + k) * P:(2 * kv + k + 1) * P], hid[:, kv, k * P:(k + 1) * P], ident[:, :])
            last.then_inc(s_hT, 1)
            pe.wait_ge(s_hTt2, 1)
            for kv in range(2):
                for k in range(2):
                    last = M.matmul(ps[:, 6, DH * kv:DH * kv + DH], hidT[:, 2 * kv + k, :], w2c[:, kv, k, :],
                                    start=(k == 0), stop=(k == 1))
            last.then_inc(s_kc, 1)
            pe.wait_ge(s_kct, 1)
            M.transpose(ps[:, 5, 0:P], kdup, ident[:, :]).then_inc(s_kcT, 1)
            pe.wait_ge(s_kcTt, 1)
            pe.wait_ge(s_t9t, 4)
            np_ = 0
            for n, (t, br) in enumerate(UNITS):
                if n:
                    pe.wait_ge(s_sm9, 2 * n - 1)
                Lk = DH if br == 0 else P * (t + 1)
                for s in range(NH):
                    h = head_of(s)
                    b, g = DH * (h % 2), h // 4
                    q = qT2[b:b + DH, h // 2, t * P:(t + 1) * P]
                    keys = kcT[b:b + DH, 0:DH] if br == 0 else kT2[b:b + DH, 2 * (br - 1) + g, 0:Lk]
                    at = score_at(s, Lk)
                    last = M.matmul(ps[:, at // 512, at % 512:at % 512 + Lk], q, keys)
                last.then_inc(s_sc, 1)
                pe.wait_ge(s_pr, n + 1)
                for part in range(parts_of(t, br)):
                    if np_:
                        pe.wait_ge(s_ptt, np_)
                    places = range(NH) if parts_of(t, br) == 1 else range(4 * part, 4 * part + 4)
                    Sv = S[:, 0:NH * Lk]
                    if br == 0:
                        for hp in range(4):
                            last = M.transpose(ps[:, 4, hp * P:(hp + 1) * P], Sv[:, hp * P:(hp + 1) * P], ident[:, :])
                    else:
                        for i, s in enumerate(places):
                            for kt in range(t + 1):
                                at = (i * (t + 1) + kt) * P
                                last = M.transpose(ps[:, 4 + at // 512, at % 512:at % 512 + P],
                                                   Sv[:, s * Lk + kt * P:s * Lk + (kt + 1) * P], ident[:, :])
                    last.then_inc(s_ptr, 1)
                    np_ += 1
                    pe.wait_ge(s_ptt, np_)
                    if part == 0 and n:
                        pe.wait_ge(s_ovt, n)
                    for i, s in enumerate(places):
                        b, g = DH * (s % 2), head_of(s) // 4
                        dst = ps[:, 6 + s % 2, DH * (s // 2):DH * (s // 2) + DH]
                        if br == 0:
                            last = M.matmul(dst, PT[b:b + DH, (s // 2) * P:(s // 2 + 1) * P], kv_c[b:b + DH, 1, :])
                        else:
                            c0 = C2.VS + 256 * (br - 1) + DH * g
                            for kt in range(t + 1):
                                at = (i * (t + 1) + kt) * P
                                last = M.matmul(dst, PT[:, at:at + P], z[:, kt, c0:c0 + DH],
                                                start=(kt == 0), stop=(kt == t))
                last.then_inc(s_ov, 1)

        @block.scalar
        def _(act):
            aa(A.activation(posT, ones[:, 0:32], ACT.Copy))
            act.wait_ge(s_pT, 1)
            A.activation(posT, ps[:, 6, 0:32], ACT.Copy).then_inc(s_t9t, 1)
            act.wait_ge(s_t9, 1)
            A.activation(cT2, banks(4, 2, 4, 256), ACT.Copy).then_inc(s_t9t, 1)
            A.activation(sg_nsa, z[:, :, C2.GATE:C2.GATE + 24], ACT.Sigmoid).then_inc(s_sg9, 1)
            act.wait_ge(s_t9, 2)
            A.activation(qT2, banks(0, 2, 4, 256), ACT.Copy).then_inc(s_t9t, 1)
            A.activation(kT2, banks(2, 2, 4, 256), ACT.Copy).then_inc(s_t9t, 1)
            act.wait_ge(s_hb, 1)
            A.activation(hid, hid, ACT.Gelu_apprx_tanh).then_inc(s_hg, 1)
            act.wait_ge(s_hT, 1)
            A.activation(hidT, ps[:, 5, :].rearrange("p (k m) -> p k m", k=4), ACT.Copy).then_inc(s_hTt2, 1)
            act.wait_ge(s_kcT, 1)
            A.activation(kcT, ps[:, 5, 0:P], ACT.Copy).then_inc(s_kcTt, 1)
            np_ = 0
            for n, (t, br) in enumerate(UNITS):
                Lk = DH if br == 0 else P * (t + 1)
                act.wait_ge(s_sm9, 2 * n + 2)
                A.activation(S[:, 0:NH * Lk], S[:, 0:NH * Lk], ACT.Exp, scale=DH ** -0.5).then_inc(s_ex, 1)
                for part in range(parts_of(t, br)):
                    act.wait_ge(s_ptr, np_ + 1)
                    if np_ and part == 0:
                        act.wait_ge(s_ov, n)
                    w = 512 if br == 0 else 1024
                    A.activation(PT[:, 0 + 0:w], ps[:, 4:6, :].rearrange("p a b -> p (a b)")[:, 0:w], ACT.Copy).then_inc(s_ptt, 1)
                    np_ += 1

        @block.vector
        def _(dve):
            def rope_heads(v, c, s):
                nh = v.shape[1]
                x1, x2 = v[:, :, 0:32], v[:, :, 32:64]
                cc, sn = rep(c, nh), rep(s, nh)
                t_ = [rt[:, i, 0:nh * 32].rearrange("p (h d) -> p h d", d=32) for i in range(4)]
                vv(V.tensor_tensor(t_[0], x1, cc, ALU.mult))
                vv(V.tensor_tensor(t_[1], x2, sn, ALU.mult))
                vv(V.tensor_tensor(t_[2], x2, cc, ALU.mult))
                vv(V.tensor_tensor(t_[3], x1, sn, ALU.mult))
                vv(V.tensor_tensor(x1, t_[0], t_[1], ALU.subtract))
                return V.tensor_tensor(x2, t_[2], t_[3], ALU.add)

            def doubled(dst, src):
                return V.tensor_copy(dst.rearrange("p n (a d) -> p n a d", a=2),
                                     src.unsqueeze(2).to_broadcast([P, src.shape[1], 2, DH]))

            for t in range(T):
                doubled(kd[:, t, 0:4, :], z[:, t, C2.KC:C2.KC + 256].rearrange("p (n d) -> p n d", d=DH)).then_inc(s_dup, 1)
            dve.wait_ge(s_m9, 1)
            dve.wait_ge(s_t9t, 2)
            for kv in range(2):
                for g in range(NG):
                    for i in range(2):
                        rows = slice(DH * i, DH * i + DH)
                        tokens = cT2[rows, 2 * kv + g, :].rearrange("p (m j i) -> p m j i", j=8, i=2)
                        for jh in range(2):
                            dst = Fc[rows, kv, 8 * jh:8 * jh + 8, 32 * g:32 * g + NCB].rearrange("p j n -> p n j")
                            pos_ = rep(posT[rows, 16 * kv + 8 * jh:16 * kv + 8 * jh + 8], NCB)
                            vv(V.tensor_tensor(dst, tokens[:, jh:jh + NCB, :, i], pos_, ALU.add))
            V.tensor_copy(Fc[:, :, :, DH:P], Fc[:, :, :, 0:DH]).then_inc(s_F, 1)
            for t in range(T):
                for c0, nh in ((C2.Q, NH), (C2.KS, NG), (C2.KW, NG)):
                    rope_heads(z[:, t, c0:c0 + nh * DH].rearrange("p (h d) -> p h d", d=DH),
                               trig[:, 0, t, :], trig[:, 1, t, :]).then_inc(s_rp, 1)
                    dve.wait_ge(s_rp, 3 * t + {C2.Q: 1, C2.KS: 2, C2.KW: 3}[c0])
                for br in range(2):
                    c0 = C2.KS + 256 * br
                    doubled(kd[:, t, 4 + 2 * br:6 + 2 * br, :],
                            z[:, t, c0:c0 + P].rearrange("p (n d) -> p n d", d=DH)).then_inc(s_dup, 1)
            dve.wait_ge(s_cmp, 2)
            dve.wait_ge(s_p9, 128)
            V.tensor_tensor(hid, ps[:, 6:8, 0:256], b1, ALU.add).then_inc(s_hb, 1)
            dve.wait_ge(s_kc, 1)
            vv(V.tensor_tensor(kv_c, ps[:, 6, 0:P].rearrange("p (a b) -> p a b", a=2), b2c, ALU.add))
            vv(rope_heads(kv_c[:, 0:1, :], trig[:, 0, 2, :], trig[:, 1, 2, :]))
            doubled(kdup.unsqueeze(1), kv_c[:, 0:1, :]).then_inc(s_kct, 1)
            dve.wait_ge(s_sg9, 1)
            for n, (t, br) in enumerate(UNITS):
                Lk = DH if br == 0 else P * (t + 1)
                sv = S[:, 0:NH * Lk].rearrange("p (h k) -> p h k", h=NH)
                if br == 0:
                    sc = ps[:, 0:2, 0:4 * DH].rearrange("p a (g o k) -> p a g o k", g=NG, k=DH)
                    sg4 = S[:, 0:NH * DH].rearrange("p (a g o k) -> p a g o k", a=2, g=NG, k=DH)
                else:
                    sc = ps[:, 0:4, :].rearrange("p a b -> p (a b)")[:, 0:NH * Lk].rearrange("p (h k) -> p h k", h=NH)
                dve.wait_ge(s_sc, n + 1)
                if n:
                    dve.wait_ge(s_ov, n)
                if br == 0:
                    for g in range(NG):
                        for par in range(2):
                            ins = V.tensor_tensor(sg4[:, par, g, :, :], sc[:, par, g, :, :], rep(cmp_neg[:, g, t, :], 2), ALU.add)
                            if (g, par) != (1, 1):
                                vv(ins)
                else:
                    if t:
                        vv(V.tensor_copy(sv[:, :, 0:P], sc[:, :, 0:P]))
                    ins = V.tensor_tensor(sv[:, :, Lk - P:Lk], sc[:, :, Lk - P:Lk], rep(caus, NH), ALU.add)
                ins.then_inc(s_sm9, 1)
                dve.wait_ge(s_sm9, 2 * n + 1)
                vv(V.tensor_reduce(rmax, sv, X_AXIS, ALU.max))
                V.tensor_tensor(sv, sv, bcast(rmax, Lk), ALU.subtract).then_inc(s_sm9, 1)
                dve.wait_ge(s_ex, n + 1)
                vv(V.tensor_reduce(rsum, sv, X_AXIS, ALU.add))
                vv(V.reciprocal(rsum, rsum))
                gate = sg_nsa[:, t, :].rearrange("p (i a b) -> p a i b", a=2, b=3)[:, :, :, br]
                vv(V.tensor_tensor(rsum.rearrange("p (a i) -> p a i", a=2), rsum.rearrange("p (a i) -> p a i", a=2), gate, ALU.mult))
                if br == 0:
                    for g in range(NG):
                        for par in range(2):
                            v_ = sg4[:, par, g, :, :]
                            vv(V.tensor_tensor(v_, v_, rep(cmp_ok[:, g, t, :], 2), ALU.mult))
                V.tensor_tensor(sv, sv, bcast(rsum, Lk), ALU.mult).then_inc(s_pr, 1)
                dve.wait_ge(s_ov, n + 1)
                for par in range(2):
                    dst = o_nsa[:, t, :].rearrange("p (g r o d) -> p r o g d", g=2, r=2, o=2)[:, par]
                    src = ps[:, 6 + par, 0:4 * DH].rearrange("p (o g d) -> p o g d", o=2, g=2)
                    ins = V.tensor_copy(dst, src) if br == 0 else V.tensor_tensor(dst, dst, src, ALU.add)
                    if par == 0:
                        vv(ins)
                ins.then_inc(s_ovt, 1)
                dve.wait_ge(s_ovt, n + 1)


    LH, LK, LV, LR, SUB = 4, 64, 128, 16, 16
    NSUB = T * P // SUB
    lq, lk, la = ar(B, 2, T * P), ar(B + 512, 2, T * P), ar(B + 1024, T * P)
    bT = ar(B + 1280, 2, T * P)
    bex = ar(B + 1792, 2, T * P)
    absx = ar(B + 2304, 2, T * P)
    refs = ar(B + 2816, 2, NSUB)
    NBUF = 4
    kt_buf = [ar(B + 2848 + 512 * i, 2, T * P) for i in range(NBUF)]
    negcap = ar(B + 4896, 512)
    wa2 = ar(B + 5408, 256)
    ba = ar(B + 5664, 2)
    lrows = ar(B + 5666, P)
    ST = ar(B + 9216, LH, 384)
    one_row = ar(B + 11776, T * P)
    lng = ar(B + 10752, LH * LV)
    osq2 = ar(B + 11264, 512)
    lss = small[:, 236:240]
    silu_r = ar(B + 5794, 1024).rearrange("p (t n) -> p t n", t=T)

    s_p10 = sem("gla_parameters_loaded")
    s_cap = sem("exponent_caps_ready")
    s_lt = sem("gla_transposed")
    s_ltt = sem("gla_transposed_taken")
    s_la = sem("log_decay_logits")
    s_lab = sem("log_decay_steps")
    s_lae = sem("log_decay_exponentials")
    s_lb = sem("query_exponents_ready")
    s_lbe = sem("query_decays_ready")
    s_lqd = sem("decayed_queries_ready")
    s_ke = sem("key_exponents_ready")
    s_kee = sem("key_decays_ready")
    s_kd = sem("decayed_keys_ready")
    s_ls = sem("gla_scores_ready")
    s_lm2 = sem("gla_scores_masked")
    s_lo = sem("gla_outputs_ready")
    s_lr = sem("gla_gate_ready")
    s_lsq = sem("gla_squares_summed")
    s_lrt = sem("gla_roots_ready")

    def span(i):
        return P * (i // (P // SUB) + 1)

    with nc.Block() as block:
        @block.sync
        def _(sp):
            sp.dma_start(wa2[0:LR, :], a["gla_w_a2_2"][0]).then_inc(s_p10, 16)
            sp.dma_start(lrows[0:2, :], a["gla_b_a_2"][0].rearrange("(h p) -> h p", p=P)).then_inc(s_p10, 16)
            sp.dma_start(lng, row_everywhere(a["gla_norm_g_2"][0])).then_inc(s_p10, 16)

        @block.gpsimd
        def _(pool):
            G.memset(negcap[:, 0:256], -80.0).then_inc(s_cap, 1)
            G.memset(negcap[:, 256:512], 1e4).then_inc(s_cap, 1)
            for i in range(NSUB):
                L = span(i)
                pool.wait_ge(s_kee, i + 1)
                kt = kt_buf[i % NBUF]
                G.tensor_tensor(kt[:, :, 0:L], kt[:, :, 0:L], lk[:, :, 0:L], ALU.mult).then_inc(s_kd, 1)

        @block.tensor
        def _(pe):
            pe.wait_ge(s_p10, 48)
            M.transpose(ps[:, 3, 0:2], lrows[0:2, :], ident[0:2, 0:2])
            for t in range(T):
                M.transpose(ps[0:LR, 2, t * P:(t + 1) * P], z[:, t, C2.GA:C2.GA + LR], ident[:, :])
                for hp in range(2):
                    M.transpose(ps[:, 0, 256 * hp + t * P:256 * hp + (t + 1) * P], z[:, t, C2.GQ + P * hp:C2.GQ + P * hp + P], ident[:, :])
                    last = M.transpose(ps[:, 1, 256 * hp + t * P:256 * hp + (t + 1) * P], z[:, t, C2.GK + P * hp:C2.GK + P * hp + P], ident[:, :])
            last.then_inc(s_lt, 1)
            pe.wait_ge(s_ltt, 2)
            for hp in range(2):
                last = M.matmul(ps[:, 7, 256 * hp:256 * hp + 256], wa2[0:LR, P * hp:P * hp + P], la[0:LR, :])
            last.then_inc(s_la, 1)
            pe.wait_ge(s_ltt, 4)
            pe.wait_ge(s_lqd, 1)
            for i in range(NSUB):
                pe.wait_ge(s_kd, i + 1)
                kt = kt_buf[i % NBUF]
                for h in range(LH):
                    b, hp = LK * (h % 2), h // 2
                    for st in range(span(i) // P):
                        if st == 0:
                            dst = ps[:, 4 + h % 2, 256 * hp + SUB * i:256 * hp + SUB * i + SUB]
                        else:
                            dst = ps[:, 2 + h % 2, P * hp + SUB * i - P:P * hp + SUB * i - P + SUB]
                        last = M.matmul(dst, kt[b:b + LK, hp, st * P:(st + 1) * P], bex[b:b + LK, hp, SUB * i:SUB * i + SUB])
                last.then_inc(s_ls, 1)
            pe.wait_ge(s_lm2, 1)
            for t in range(T):
                for h in range(LH):
                    for st in range(t + 1):
                        lhsT = ST[:, h, t * P:(t + 1) * P] if st == 0 else ST[:, h, 256:384]
                        last = M.matmul(ps[:, t, LV * h:LV * h + LV], lhsT, z[:, st, C2.GV + LV * h:C2.GV + LV * h + LV],
                                        start=(st == 0), stop=(st == t))
                last.then_inc(s_lo, 1)

        @block.scalar
        def _(act):
            act.wait_ge(s_lt, 1)
            A.activation(la[0:LR, :], ps[0:LR, 2, 0:T * P], ACT.Copy).then_inc(s_ltt, 1)
            A.activation(ba, ps[:, 3, 0:2], ACT.Copy).then_inc(s_ltt, 1)
            A.activation(lq, ps[:, 0, :].rearrange("p (h n) -> p h n", h=2), ACT.Copy).then_inc(s_ltt, 1)
            A.activation(lk, ps[:, 1, :].rearrange("p (h n) -> p h n", h=2), ACT.Copy).then_inc(s_ltt, 1)
            act.wait_ge(s_lab, 1)
            aa(A.activation(absx, absx, ACT.Exp))
            A.activation(absx, absx, ACT.Ln, bias=1.0).then_inc(s_lae, 1)
            act.wait_ge(s_lb, 1)
            A.activation(bex, bex, ACT.Exp).then_inc(s_lbe, 1)
            for i in range(NSUB):
                L = span(i)
                act.wait_ge(s_ke, i + 1)
                kt = kt_buf[i % NBUF]
                A.activation(kt[:, :, 0:L], kt[:, :, 0:L], ACT.Exp, scale=-1.0).then_inc(s_kee, 1)
            A.activation(silu_r, z[:, :, C2.GR:C2.GR + 512], ACT.Silu).then_inc(s_lr, 1)
            A.activation(z[:, :, C2.MA:C2.END], z[:, :, C2.MA:C2.END], ACT.Sigmoid).then_inc(s_lr, 1)
            for t in range(T):
                act.wait_ge(s_lsq, t + 1)
                A.activation(lss, lss, ACT.Sqrt, bias=eps_t, scale=1.0 / LV).then_inc(s_lrt, 1)

        @block.vector
        def _(dve):
            dve.wait_ge(s_la, 1)
            dve.wait_ge(s_ltt, 2)
            for hp in range(2):
                vv(V.tensor_scalar(bT[:, hp, :], ps[:, 7, 256 * hp:256 * hp + 256], ba[:, hp:hp + 1], None, ALU.add))
            V.scalar_tensor_tensor(absx, bT, -1.0, bT, ALU.mult, ALU.min).then_inc(s_lab, 1)
            vv(V.tensor_scalar(bT, bT, 0.0, None, ALU.min))
            dve.wait_ge(s_lae, 1)
            vv(V.tensor_tensor(bT, bT, absx, ALU.subtract))
            vv(V.tensor_scalar(bT, bT, 1.0 / 16.0, None, ALU.mult))
            vv(V.memset(one_row, 1.0))
            for hp in range(2):
                vv(V.tensor_tensor_scan(absx[:, hp, :], one_row, bT[:, hp, :], 0.0, ALU.mult, ALU.add))
            b_ = absx
            vv(V.memset(refs[:, :, 0:1], 0.0))
            vv(V.tensor_copy(refs[:, :, 1:NSUB], b_[:, :, SUB - 1:T * P - 1:SUB]))
            for hp in range(2):
                ins = V.tensor_tensor(bex[:, hp, :].rearrange("p (n s) -> p n s", s=SUB),
                                      b_[:, hp, :].rearrange("p (n s) -> p n s", s=SUB), bcast(refs[:, hp, :], SUB), ALU.subtract)
                if hp == 0:
                    vv(ins)
            ins.then_inc(s_lb, 1)
            dve.wait_ge(s_lbe, 1)
            dve.wait_ge(s_ltt, 3)
            V.scalar_tensor_tensor(bex, bex, LK ** -0.5, lq, ALU.mult, ALU.mult).then_inc(s_lqd, 1)
            dve.wait_ge(s_cap, 2)
            for i in range(NSUB):
                L = span(i)
                if i >= NBUF:
                    dve.wait_ge(s_ls, i - NBUF + 1)
                kt = kt_buf[i % NBUF]
                for hp in range(2):
                    at = 256 - SUB * (i + 1)
                    ins = V.scalar_tensor_tensor(kt[:, hp, 0:L], b_[:, hp, 0:L], refs[:, hp, i:i + 1], negcap[:, at:at + L],
                                                 ALU.subtract, ALU.max)
                ins.then_inc(s_ke, 1)
            dve.wait_ge(s_ls, NSUB)
            for h in range(LH):
                b0 = 256 * (h // 2)
                vv(V.tensor_tensor(ST[:, h, 0:P], ps[:, 4 + h % 2, b0:b0 + P], tri_le[:, :], ALU.mult))
                vv(V.tensor_copy(ST[:, h, P:2 * P], ps[:, 4 + h % 2, b0 + P:b0 + 2 * P]))
                ins = V.tensor_tensor(ST[:, h, 2 * P:3 * P], ps[:, 2 + h % 2, P * (h // 2):P * (h // 2) + P], tri_le[:, :], ALU.mult)
                if h < LH - 1:
                    vv(ins)
            ins.then_inc(s_lm2, 1)
            dve.wait_ge(s_lr, 2)
            dve.wait_ge(s_p10, 48)
            for t in range(T):
                o = o_gla[:, t, :]
                dve.wait_ge(s_lo, t + 1)
                vv(V.tensor_copy(o, ps[:, t, :]))
                vv(V.tensor_tensor(osq2, o, o, ALU.mult))
                V.tensor_reduce(lss, osq2.rearrange("p (h v) -> p h v", h=LH), X_AXIS, ALU.add).then_inc(s_lsq, 1)
                dve.wait_ge(s_lrt, t + 1)
                vv(V.reciprocal(lss, lss))
                oh = o.rearrange("p (h v) -> p h v", h=LH)
                vv(V.tensor_tensor(oh, oh, bcast(lss, LV), ALU.mult))
                vv(V.tensor_tensor(o, o, lng, ALU.mult))
                vv(V.tensor_tensor(o, o, silu_r[:, t, :], ALU.mult))

    oT = ar(B, 8, T * P)
    mx = ar(B + 2048, T, D)
    mT = ar(B + 4096, KD, T * P)
    h2b = ar(2048, T, D)
    h2bT = ar(B, KD, T * P)
    rw2 = ar(B + 6144, KD, 36)
    rb2_ = ar(B + 6432, 36)
    fgn = ar(B + 9216, D)
    lg2 = small[:, 388:460].rearrange("p (t e) -> p t e", t=T)
    lg8 = small[:, 256:272].rearrange("p (t e) -> p t e", t=T)
    gsel = small[:, 272:288].rearrange("p (t e) -> p t e", t=T)
    gexp = small[:, 288:296].rearrange("p (t e) -> p t e", t=T)
    gm8 = small[:, 296:312].rearrange("p (t e) -> p t e", t=T)
    gsum = small[:, 312:314]
    gneg = small[:, 314:316]
    lgm = small[:, 316:380].rearrange("p (t e) -> p t e", t=T)
    gexpm = small[:, 380:388].rearrange("p (t e) -> p t e", t=T)

    s_p11 = sem("router2_parameters_loaded")
    s_oT = sem("branches_transposed")
    s_oTt = sem("branches_transposed_taken")
    s_mxr = sem("mixed2_ready")
    s_mxT = sem("mixed2_transposed")
    s_mxTt = sem("mixed2_transposed_taken")
    s_r11 = sem("residual3_added")
    s_q11 = sem("norm3_squares")
    s_n11 = sem("norm3_ready")
    s_nT = sem("norm3_transposed")
    s_nTt = sem("norm3_transposed_taken")
    s_l11 = sem("router2_logits_ready")
    s_g11 = sem("group_max_ready")
    s_e11 = sem("group_exponentials")
    s_m11 = sem("expert_max_ready")
    s_e12 = sem("expert_exponentials")
    s_s11 = sem("selection2_ready")
    s_k11 = sem("ranks2_ready")

    w_gt, w_up, w_d2 = a["w_gate_2"][0], a["w_up_2"][0], a["w_down_2"][0]
    def gate_up_down2(q):
        pair = (2 * q, 2 * q + 1)
        return ([(cols(one(w_gt, e), 0), KD, 512) for e in pair] + [(cols(one(w_up, e), 0), KD, 512) for e in pair]
                + [(one(w_d2, e).rearrange("(k p) n -> p k n", p=P), 4, 1024) for e in pair])

    loads2 = ExpertLoads("experts2", gate_up_down2)

    with nc.Block() as block:
        @block.sync
        def _(sp):
            sp.dma_start(rw2[:, :, 0:4], a["w_grp_2"][0].rearrange("(k p) e -> p k e", p=P)).then_inc(s_p11, 16)
            sp.dma_start(rw2[:, :, 4:36], a["w_exp_2"][0].rearrange("(k p) e -> p k e", p=P)).then_inc(s_p11, 16)
            sp.dma_start(rb2_[:, 0:4], row_everywhere(a["b_grp_2"][0])).then_inc(s_p11, 16)
            sp.dma_start(rb2_[:, 4:36], row_everywhere(a["b_exp_2"][0])).then_inc(s_p11, 16)
            sp.dma_start(fgn, row_everywhere(a["g_ffn_2"][0])).then_inc(s_p11, 16)
            loads2.load_first(sp, rb2)

        @block.tensor
        def _(pe):
            for i, o in enumerate((o_nsa, o_gla)):
                for t in range(T):
                    for k in range(4):
                        last = M.transpose(ps[:, 2 * i + k // 2, (k % 2) * 256 + t * P:(k % 2) * 256 + (t + 1) * P],
                                           o[:, t, k * P:(k + 1) * P], ident[:, :])
                last.then_inc(s_oT, 1)
            pe.wait_ge(s_oTt, 2)
            for i in range(2):
                w = rb2.take(pe)
                for t in range(T):
                    for n in range(2):
                        for k in range(4):
                            last = M.matmul(ps[:, 4 * i + 2 * t + n, :], oT[:, 4 * i + k, t * P:(t + 1) * P],
                                            w[:, k, 512 * n:512 * n + 512], start=(k == 0), stop=(k == 3))
                last.then_inc(s_pa, 1)
            for t in range(T):
                pe.wait_ge(s_mxr, t + 1)
                for k in range(KD):
                    last = M.transpose(ps[:, 2 * t + k // 4, (k % 4) * P:(k % 4 + 1) * P], mx[:, t, k * P:(k + 1) * P], ident[:, :])
                last.then_inc(s_mxT, 1)
            pe.wait_ge(s_mxTt, 2)
            for n in range(2):
                w = rb2.take(pe)
                for t in range(T):
                    for k in range(KD):
                        last = M.matmul(ps[:, 4 + 2 * t + n, :], mT[:, k, t * P:(t + 1) * P], w[:, k, :],
                                        start=(k == 0), stop=(k == KD - 1))
                last.then_inc(s_po, 1)
            for t in range(T):
                pe.wait_ge(s_n11, t + 1)
                for k in range(KD):
                    last = M.transpose(ps[:, 2 * t + k // 4, (k % 4) * P:(k % 4 + 1) * P], h2b[:, t, k * P:(k + 1) * P], ident[:, :])
                last.then_inc(s_nT, 1)
            pe.wait_ge(s_nTt, 2)
            pe.wait_ge(s_p11, 80)
            for t in range(T):
                for k in range(KD):
                    last = M.matmul(ps[:, 4, 36 * t:36 * t + 36], h2bT[:, k, t * P:(t + 1) * P], rw2[:, k, :],
                                    start=(k == 0), stop=(k == KD - 1))
            last.then_inc(s_l11, 1)
            pe.wait_ge(s_s11, 1)
            rank_matmuls(5).then_inc(s_k11, 1)

        @block.scalar
        def _(act):
            for i in range(2):
                act.wait_ge(s_oT, i + 1)
                A.activation(oT[:, 4 * i:4 * i + 4, :], banks(2 * i, 2, 4, 256), ACT.Copy).then_inc(s_oTt, 1)
            for t in range(T):
                act.wait_ge(s_mxT, t + 1)
                A.activation(mT[:, :, t * P:(t + 1) * P], banks(2 * t, 2, KD, P), ACT.Copy).then_inc(s_mxTt, 1)
            for t in range(T):
                act.wait_ge(s_r11, t + 1)
                A.activation(mx[:, t, :], x_res[:, t, :], ACT.Square, accum_out=ss3[:, t:t + 1]).then_inc(s_q11, 1)
            act.wait_ge(s_q11, 2)
            A.activation(ss3, ss3, ACT.Sqrt, bias=eps_t, scale=1.0 / D).then_inc(s_q11, 1)
            for t in range(T):
                act.wait_ge(s_nT, t + 1)
                A.activation(h2bT[:, :, t * P:(t + 1) * P], banks(2 * t, 2, KD, P), ACT.Copy).then_inc(s_nTt, 1)
            act.wait_ge(s_g11, 1)
            for t in range(T):
                A.activation(gexp[:, t, :], lg2[:, t, 0:4], ACT.Exp, bias=gneg[:, t:t + 1]).then_inc(s_e11, 1)
            act.wait_ge(s_m11, 1)
            for t in range(T):
                A.activation(gate_of[:, t, 0:NE], lgm[:, t, :], ACT.Exp, bias=nm[:, t:t + 1]).then_inc(s_e12, 1)

        @block.vector
        def _(dve):
            dve.wait_ge(s_pa, 2)
            for t in range(T):
                vv(V.tensor_tensor(mx[:, t, :], banks(2 * t, 2, D), z[:, t, C2.MA:C2.MB], ALU.mult))
                zb = z[:, t, C2.MB:C2.END]
                vv(V.tensor_tensor(zb, banks(4 + 2 * t, 2, D), zb, ALU.mult))
                V.tensor_tensor(mx[:, t, :], mx[:, t, :], zb, ALU.add).then_inc(s_mxr, 1)
            dve.wait_ge(s_po, 2)
            for t in range(T):
                V.tensor_tensor(x_res[:, t, :], x_res[:, t, :], banks(4 + 2 * t, 2, D), ALU.add).then_inc(s_r11, 1)
            dve.wait_ge(s_q11, 3)
            vv(V.reciprocal(ss3, ss3))
            dve.wait_ge(s_p11, 80)
            for t in range(T):
                V.scalar_tensor_tensor(h2b[:, t, :], x_res[:, t, :], ss3[:, t:t + 1], fgn, ALU.mult, ALU.mult).then_inc(s_n11, 1)
            dve.wait_ge(s_l11, 1)
            vv(V.tensor_tensor(lg2, ps[:, 4, 0:72].rearrange("p (t e) -> p t e", t=T), rep(rb2_, T), ALU.add))
            vv(V.memset(lg8, -BIG))
            vv(V.tensor_copy(lg8[:, :, 0:4], lg2[:, :, 0:4]))
            for t in range(T):
                select_top(dve, lg8[:, t, :], 1, gm8[:, t, :], gsel[:, t, :], tmpe[:, 0:8], s1)
            V.tensor_scalar(gneg, gm8[:, :, 0], -1.0, None, ALU.mult).then_inc(s_g11, 1)
            for t in range(T):
                vv(V.tensor_scalar(gexpm[:, t, :], gsel[:, t, 0:4], BIG, -BIG, ALU.mult, ALU.add))
                vv(V.tensor_tensor(lgm[:, t, :].rearrange("p (g e) -> p g e", g=4),
                                   lg2[:, t, 4:36].rearrange("p (g e) -> p g e", g=4), bcast(gexpm[:, t, :], 8), ALU.add))
                select_top(dve, lgm[:, t, :], 2, m8[:, t, :], sel[:, t, :], tmpe, s1)
            vv(V.tensor_tensor(selsum, sel[:, 0, :], sel[:, 1, :], ALU.add))
            V.tensor_scalar(nm, m8[:, :, 0], -1.0, None, ALU.mult).then_inc(s_m11, 1)
            dve.wait_ge(s_m11, 1)
            V.tensor_copy(gs, nm).then_inc(s_s11, 1)
            dve.wait_ge(s_e11, 2)
            vv(V.tensor_reduce(gsum, gexp, X_AXIS, ALU.add))
            dve.wait_ge(s_e12, 2)
            vv(V.tensor_tensor(gate_of[:, :, 0:NE], gate_of[:, :, 0:NE], sel, ALU.mult))
            vv(V.tensor_reduce(gs, gate_of[:, :, 0:NE], X_AXIS, ALU.add))
            vv(V.tensor_tensor(gs, gs, gsum, ALU.mult))
            vv(V.reciprocal(gs, gs))
            vv(V.tensor_tensor(gate_of[:, :, 0:NE], gate_of[:, :, 0:NE], bcast(gs, NE), ALU.mult))
            dve.wait_ge(s_k11, 1)
            vv(dispatch_tables(dve, 5))

    zero = ar(14336, P)
    s_zero = sem("zero_ready")

    def start_zero(pe):
        pe.wait_ge(s_zero, 1)
        for b in range(4):
            M.matmul(ps[:, b, :], zero, h2b[:, 0, 0:512], start=True, stop=False, skip_group_check=True)

    with nc.Block() as block:
        @block.gpsimd
        def _(pool):
            G.memset(zero, 0.0).then_inc(s_zero, 1)

    def expert_pairs(loads, x_tok, acc_start):
        KH = 4
        NP = NE // 2
        xgT, sg, y, yT = ar(7168, KD, P), ar(8192, 512), ar(8704, KH, P), ar(9216, KH, P)
        y2 = ar(9728, 2, 512)
        onehot, gated, GT = ar(12800, T, P), ar(13056, T, P), ar(13312, T, P)
        name, s_done = loads.name, loads.s_done
        s_one = sem(f"{name}_onehot_ready")
        s_gat = sem(f"{name}_gated_ready")
        s_xg = sem(f"{name}_gathered")
        s_xgt = sem(f"{name}_gathered_taken")
        s_sig = sem(f"{name}_silu_ready")
        s_y = sem(f"{name}_hidden_ready")
        s_yT = sem(f"{name}_hidden_transposed")
        s_yTt = sem(f"{name}_hidden_transposed_taken")
        s_GT = sem(f"{name}_gated_transposed")
        s_GTt = sem(f"{name}_gated_transposed_taken")
        s_y2 = sem(f"{name}_result_taken")

        with nc.Block() as block:
            @block.sync
            def _(sp):
                loads.load_rest(sp, NP)

            @block.tensor
            def _(pe):
                def gather(i):
                    pe.wait_ge(s_one, i + 1)
                    for k in range(KD):
                        for t in range(T):
                            last = M.matmul(ps[:, 6 + k // 4, (k % 4) * P:(k % 4 + 1) * P], x_tok[:, t, k * P:(k + 1) * P],
                                            onehot[:, t, :], start=(t == 0), stop=(t == T - 1))
                    last.then_inc(s_xg, 1)

                acc_start(pe)
                gather(0)
                n = pe.value_load(passes[0:1, 0:1], min_val=1, max_val=MAXP)
                with pe.Fori(0, n) as p:
                    with pe.Fori(0, NP) as q:
                        i = p * NP + q
                        pe.wait_ge(s_xgt, i + 1)
                        for which in range(2):
                            w = [loads.arrived(pe, 2 * which + j, i) for j in range(2)]
                            for k in range(KD):
                                for j in range(2):
                                    last = M.matmul(ps[halves[j], 4 + which, :], xgT[:, k, halves[j]], w[j][:, k, :],
                                                    start=(k == 0), stop=(k == KD - 1))
                            last.then_inc(s_done, 1)
                        gather(i + 1)
                        pe.wait_ge(s_y, i + 1)
                        for k in range(KH):
                            last = M.transpose(ps[:, 5, k * P:(k + 1) * P], y[:, k, :], ident[:, :])
                        last.then_inc(s_yT, 1)
                        pe.wait_ge(s_gat, i + 1)
                        pe.wait_ge(s_xgt, i + 2)
                        for t in range(T):
                            last = M.transpose(ps[:, 6, t * P:(t + 1) * P], gated[:, t, :], ident[:, :])
                        last.then_inc(s_GT, 1)
                        w = [loads.arrived(pe, 4 + j, i, 4, 1024) for j in range(2)]
                        pe.wait_ge(s_yTt, i + 1)
                        for d in range(2):
                            for k in range(KH):
                                for j in range(2):
                                    last = M.matmul(ps[halves[j], (4, 7)[d], :], yT[:, k, halves[j]],
                                                    w[j][:, k, 512 * d:512 * (d + 1)], start=(k == 0), stop=(k == KH - 1))
                        last.then_inc(s_done, 1)
                        pe.wait_ge(s_GTt, i + 1)
                        pe.wait_ge(s_y2, i * 2 + 2)
                        for t in range(T):
                            for d in range(2):
                                M.matmul(ps[:, 2 * t + d, :], GT[:, t, :], y2[:, d, :], start=False, stop=False,
                                         skip_group_check=True)
                M.matmul(ps[:, 7, 0:P], ident[:, :], ident[:, :]).then_inc(s_GT, 1)

            @block.scalar
            def _(act):
                def take_gathered(i):
                    act.wait_ge(s_xg, i + 1)
                    A.activation(xgT, banks(6, 2, KD, P), ACT.Copy).then_inc(s_xgt, 1)
                take_gathered(0)
                n = act.value_load(passes[0:1, 0:1], min_val=1, max_val=MAXP)
                with act.Fori(0, n) as p:
                    with act.Fori(0, NP) as q:
                        i = p * NP + q
                        act.wait_ge(s_done, i * 3 + 1)
                        A.activation(sg, ps[:, 4, :], ACT.Silu).then_inc(s_sig, 1)
                        act.wait_ge(s_done, i * 3 + 2)
                        take_gathered(i + 1)
                        act.wait_ge(s_yT, i + 1)
                        A.activation(yT, ps[:, 5, :].rearrange("p (k m) -> p k m", k=KH), ACT.Copy).then_inc(s_yTt, 1)
                        act.wait_ge(s_GT, i + 1)
                        A.activation(GT, ps[:, 6, 0:2 * P].rearrange("p (t m) -> p t m", t=T), ACT.Copy).then_inc(s_GTt, 1)
                        act.wait_ge(s_done, i * 3 + 3)
                        for d in range(2):
                            A.activation(y2[:, d, :], ps[:, (4, 7)[d], :], ACT.Copy).then_inc(s_y2, 1)

            @block.vector
            def _(dve):
                def make_onehot(i):
                    for t in range(T):
                        for j in range(2):
                            ins = V.tensor_scalar(onehot[:, t, halves[j]], iota_row[:, 0, :], slot_of[:, t, bass.ds(i * 2 + j, 1)],
                                                  None, ALU.is_equal)
                    ins.then_inc(s_one, 1)
                make_onehot(0)
                n = dve.value_load(passes[0:1, 0:1], min_val=1, max_val=MAXP)
                with dve.Fori(0, n) as p:
                    with dve.Fori(0, NP) as q:
                        i = p * NP + q
                        dve.wait_ge(s_done, i * 3 + 1)
                        make_onehot(i + 1)
                        for t in range(T):
                            for j in range(2):
                                ins = V.tensor_scalar(gated[:, t, halves[j]], iota_row[:, 0, :], slot_of[:, t, bass.ds(i * 2 + j, 1)],
                                                      gate_of[:, t, bass.ds(i * 2 + j, 1)], ALU.is_equal, ALU.mult)
                        ins.then_inc(s_gat, 1)
                        dve.wait_ge(s_done, i * 3 + 2)
                        dve.wait_ge(s_sig, i + 1)
                        V.tensor_tensor(y.rearrange("p a b -> p (a b)"), ps[:, 5, :], sg, ALU.mult).then_inc(s_y, 1)

    expert_pairs(loads2, h2b, start_zero)

    gfin = ar(5120, D)
    fin = ar(6144, T, D)
    s_p13 = sem("final_weight_loaded")
    s_r13 = sem("last_residual_added")
    s_q13 = sem("last_squares")
    s_f13 = sem("result_ready")
    s_out = sem("result_stored")
    with nc.Block() as block:
        @block.sync
        def _(sp):
            sp.dma_start(gfin, row_everywhere(a["g_final_2"])).then_inc(s_p13, 16)
            sp.wait_ge(s_f13, 2)
            sp.dma_start(out[0].rearrange("(t p) d -> p t d", p=P), fin).then_inc(s_out, 16)
            sp.wait_ge(s_out, 16)

        @block.scalar
        def _(act):
            for t in range(T):
                act.wait_ge(s_r13, t + 1)
                A.activation(fin[:, t, :], x_res[:, t, :], ACT.Square, accum_out=ss3[:, t:t + 1]).then_inc(s_q13, 1)
            act.wait_ge(s_q13, 2)
            A.activation(ss3, ss3, ACT.Sqrt, bias=eps_t, scale=1.0 / D).then_inc(s_q13, 1)

        @block.vector
        def _(dve):
            for t in range(T):
                V.tensor_tensor(x_res[:, t, :], x_res[:, t, :], banks(2 * t, 2, D), ALU.add).then_inc(s_r13, 1)
            dve.wait_ge(s_q13, 3)
            vv(V.reciprocal(ss3, ss3))
            dve.wait_ge(s_p13, 16)
            for t in range(T):
                V.scalar_tensor_tensor(fin[:, t, :], x_res[:, t, :], ss3[:, t:t + 1], gfin, ALU.mult, ALU.mult).then_inc(s_f13, 1)



def kernel(**inputs):
    import numpy as np
    import concourse.bacc as bacc
    from concourse.bass_utils import run_bass_kernel_spmd

    nc = bacc.Bacc("TRN2", target_bir_lowering=False, num_devices=1)
    arrays, args = {}, {}
    for name in inputs:
        value = np.ascontiguousarray(inputs[name])
        arrays[f"in_{name}"] = value
        args[name] = nc.dram_tensor(f"in_{name}", value.shape, mybir.dt.from_np(value.dtype), kind="ExternalInput").ap()
    out = nc.dram_tensor("out", (1, T * P, D), F32, kind="ExternalOutput").ap()
    program(nc, args, out)
    got = run_bass_kernel_spmd(nc, [arrays], core_ids=[0])
    return got.results[0]["out"]
```
